# Optimizing a Trainium2 kernel written in Bass

```python
import jax, jax.numpy as jnp
from jax import lax
import numpy as np

D_MODEL = 1024
BATCH = 1
SEQ = 512
DEPTH = 1
DEC_BATCH = 8
DEC_SEQ = 1
PAST_LEN = 2048
PAGE_SIZE = 128

HEAD_DIM = 64
MIX_WIDTH = D_MODEL
ATTN_WIDTH = MIX_WIDTH // 2
RWKV_WIDTH = MIX_WIDTH - ATTN_WIDTH
N_ATTN_HEADS = ATTN_WIDTH // HEAD_DIM
N_RWKV_HEADS = RWKV_WIDTH // HEAD_DIM

DILATED_PATTERNS = ((128, 1), (512, 4), (2048, 16))
MAX_WINDOW = max(w for w, _ in DILATED_PATTERNS)
ATTN_QBLOCK = 128
ROPE_THETA = 10000.0

DECAY_LORA = 64
AAA_LORA = 64
GATE_LORA = 128
RWKV_COLS = 3 * RWKV_WIDTH + DECAY_LORA + AAA_LORA + GATE_LORA
RWKV_SPLITS = (RWKV_WIDTH, 2 * RWKV_WIDTH, 3 * RWKV_WIDTH,
               3 * RWKV_WIDTH + DECAY_LORA, 3 * RWKV_WIDTH + DECAY_LORA + AAA_LORA)
IN_COLS = 3 * ATTN_WIDTH + RWKV_COLS

N_EXPERTS = 32
TOP_K = 4
D_EXPERT = D_MODEL
SWIGLU_ALPHA = 1.702
SWIGLU_LIMIT = 7.0
MOE_BLOCK = 128

NORM_EPS = 1e-6
GN_EPS = 64e-5

kernel_name = 'hymba_rwkv7_dilated_moe_step'

def rms_norm(x, g):
    xf = x.astype(jnp.float32)
    y = xf * lax.rsqrt(jnp.mean(xf * xf, axis=-1, keepdims=True) + NORM_EPS)
    return y * g.astype(jnp.float32)

def rope(x, pos):
    half = HEAD_DIM // 2
    inv_freq = 1.0 / (ROPE_THETA ** (jnp.arange(0, HEAD_DIM, 2, dtype=jnp.float32) / HEAD_DIM))
    ang = pos.astype(jnp.float32)[:, None] * inv_freq[None, :]
    cos = jnp.cos(ang)[None, :, None, :]
    sin = jnp.sin(ang)[None, :, None, :]
    xf = x.astype(jnp.float32)
    x1, x2 = xf[..., :half], xf[..., half:]
    return jnp.concatenate([x1 * cos - x2 * sin, x2 * cos + x1 * sin], axis=-1)

def dilated_attention(q, k_all, v_all, q_off):
    B, Tq, H, Dh = q.shape
    qb = ATTN_QBLOCK if Tq % ATTN_QBLOCK == 0 else Tq
    n_blk = Tq // qb
    scale = 1.0 / np.sqrt(HEAD_DIM).astype(np.float32)
    q_blocks = jnp.moveaxis(q.astype(jnp.float32).reshape(B, n_blk, qb, H, Dh), 1, 0)

    def one_block(args):
        blk, q_blk = args
        q_idx = q_off + blk * qb + jnp.arange(qb)
        outs, lses = [], []
        for (w, d) in DILATED_PATTERNS:
            dist = jnp.arange(w // d + 1) * d
            idx = q_idx[:, None] - dist[None, :]
            valid = idx >= 0
            idx = jnp.maximum(idx, 0)
            kg = k_all[:, idx].astype(jnp.float32)
            vg = v_all[:, idx].astype(jnp.float32)
            s = jnp.einsum('bqhd,bqkhd->bhqk', q_blk, kg) * scale
            s = jnp.where(valid[None, None], s, -jnp.inf)
            lse = jax.nn.logsumexp(s, axis=-1)
            p = jnp.exp(s - lse[..., None])
            outs.append(jnp.einsum('bhqk,bqkhd->bqhd', p, vg))
            lses.append(jnp.transpose(lse, (0, 2, 1)))
        wts = jax.nn.softmax(jnp.stack(lses, axis=0), axis=0)
        return jnp.sum(jnp.stack(outs, axis=0) * wts[..., None], axis=0)

    out = lax.map(one_block, (jnp.arange(n_blk), q_blocks))
    return jnp.moveaxis(out, 0, 1).reshape(B, Tq, H, Dh)

def rwkv7_group(p, shift0, wkv0, mu, w0, w2, a0, a2, g2, k_k, k_a, r_k, ln_w, ln_b):
    B, T, _ = p.shape
    p = p.astype(jnp.float32)
    prev = jnp.concatenate([shift0.astype(jnp.float32)[:, None, :], p[:, :-1]], axis=1)
    xs = p + mu * (prev - p)
    r, k, v, xw, xa, xg = jnp.split(xs, RWKV_SPLITS, axis=-1)
    w = -jax.nn.softplus(-(w0 + jnp.tanh(xw) @ w2)) - 0.5
    decay = jnp.exp(-jnp.exp(w))
    a = jax.nn.sigmoid(a0 + xa @ a2)
    g = jax.nn.sigmoid(xg) @ g2

    def heads(t):
        return t.reshape(B, T, N_RWKV_HEADS, HEAD_DIM)

    kk = heads(k * k_k)
    kk = kk / jnp.maximum(jnp.linalg.norm(kk, axis=-1, keepdims=True), 1e-12)
    k = k * (1.0 + (a - 1.0) * k_a)
    rh, dh, kh, vh, ah = heads(r), heads(decay), heads(k), heads(v), heads(a)

    def step(S, inp):
        r_t, d_t, k_t, v_t, a_t, b_t = inp
        sa = jnp.einsum('bhvk,bhk->bhv', S, a_t)
        S = S * d_t[:, :, None, :] + sa[..., None] * b_t[:, :, None, :] + v_t[..., None] * k_t[:, :, None, :]
        return S, jnp.einsum('bhvk,bhk->bhv', S, r_t)

    seq = tuple(jnp.moveaxis(t, 1, 0) for t in (rh, dh, kh, vh, -kk, kk * ah))
    S_final, ys = lax.scan(step, wkv0.astype(jnp.float32), seq)
    y = jnp.moveaxis(ys, 0, 1)
    mean = jnp.mean(y, axis=-1, keepdims=True)
    var = jnp.mean(jnp.square(y - mean), axis=-1, keepdims=True)
    y = ((y - mean) * lax.rsqrt(var + GN_EPS)).reshape(B, T, RWKV_WIDTH) * ln_w + ln_b
    bonus = jnp.sum(rh * kh * r_k, axis=-1, keepdims=True) * vh
    out = (y + bonus.reshape(B, T, RWKV_WIDTH)) * g
    return out, p[:, -1], S_final

def moe_ffn(h, router_w, router_b, w_gu, b_gu, w_down, b_down):
    B, T, D = h.shape
    xt = h.reshape(-1, D).astype(jnp.float32)
    n_tok = xt.shape[0]
    logits = xt @ router_w + router_b
    top_val, top_idx = lax.top_k(logits, TOP_K)
    top_w = jax.nn.softmax(top_val, axis=-1)
    n_assign = n_tok * TOP_K
    blk = max(1, min(MOE_BLOCK, n_assign // N_EXPERTS))
    n_blocks = -(-n_assign // blk) + N_EXPERTS
    flat_e = top_idx.reshape(-1)
    flat_tok = jnp.repeat(jnp.arange(n_tok, dtype=jnp.int32), TOP_K)
    flat_w = top_w.reshape(-1)
    order = jnp.argsort(flat_e)
    se = flat_e[order]
    counts = jnp.bincount(flat_e, length=N_EXPERTS)
    padded = (counts + blk - 1) // blk * blk
    pad_end = jnp.cumsum(padded)
    pad_start = pad_end - padded
    start = jnp.cumsum(counts) - counts
    dest = pad_start[se] + (jnp.arange(n_assign) - start[se])
    slot_tok = jnp.full((n_blocks * blk,), n_tok, jnp.int32).at[dest].set(flat_tok[order])
    slot_w = jnp.zeros((n_blocks * blk,), jnp.float32).at[dest].set(flat_w[order])
    blk_e = jnp.minimum(jnp.searchsorted(pad_end, jnp.arange(n_blocks) * blk, side='right'), N_EXPERTS - 1)
    x_pad = jnp.concatenate([xt, jnp.zeros((1, D), jnp.float32)], axis=0)

    def expert_block(args):
        e, toks = args
        gu = x_pad[toks] @ w_gu[e] + b_gu[e]
        gate = jnp.minimum(gu[:, :D_EXPERT], SWIGLU_LIMIT)
        up = jnp.clip(gu[:, D_EXPERT:], -SWIGLU_LIMIT, SWIGLU_LIMIT)
        act = (up + 1.0) * gate * jax.nn.sigmoid(gate * SWIGLU_ALPHA)
        return act @ w_down[e] + b_down[e]

    outs = lax.map(expert_block, (blk_e, slot_tok.reshape(n_blocks, blk)))
    y = jnp.zeros((n_tok + 1, D), jnp.float32).at[slot_tok].add(outs.reshape(-1, D) * slot_w[:, None])
    return y[:n_tok].reshape(B, T, D)

def layer_forward(x, c, pos0, k_past, v_past, wkv0, shift0,
                  w_ada, b_ada, norm1_g, norm2_g, w_in, q_norm_g, k_norm_g,
                  rwkv_mu, rwkv_w0, rwkv_w2, rwkv_a0, rwkv_a2, rwkv_g2,
                  rwkv_k_k, rwkv_k_a, rwkv_r_k, rwkv_ln_w, rwkv_ln_b, w_out,
                  router_w, router_b, moe_w_gu, moe_b_gu, moe_w_down, moe_b_down):
    B, T, _ = x.shape
    mod = jax.nn.silu(c.astype(jnp.float32)) @ w_ada + b_ada
    sh1, sc1, gt1, sh2, sc2, gt2 = jnp.split(mod[:, None, :], 6, axis=-1)
    h = rms_norm(x, norm1_g) * (1.0 + sc1) + sh1
    proj = h @ w_in
    q, k, v = jnp.split(proj[..., :3 * ATTN_WIDTH], 3, axis=-1)
    q = q.reshape(B, T, N_ATTN_HEADS, HEAD_DIM)
    k = k.reshape(B, T, N_ATTN_HEADS, HEAD_DIM)
    v = v.reshape(B, T, N_ATTN_HEADS, HEAD_DIM)
    pos = pos0 + jnp.arange(T)
    q = rope(rms_norm(q, q_norm_g), pos)
    k = rope(rms_norm(k, k_norm_g), pos)
    k_all = jnp.concatenate([k_past.astype(k.dtype), k], axis=1)
    v_all = jnp.concatenate([v_past.astype(v.dtype), v], axis=1)
    attn = dilated_attention(q, k_all, v_all, k_past.shape[1]).reshape(B, T, ATTN_WIDTH)
    rw, shift_new, wkv_new = rwkv7_group(proj[..., 3 * ATTN_WIDTH:], shift0, wkv0,
                                         rwkv_mu, rwkv_w0, rwkv_w2, rwkv_a0, rwkv_a2, rwkv_g2,
                                         rwkv_k_k, rwkv_k_a, rwkv_r_k, rwkv_ln_w, rwkv_ln_b)
    x = x + gt1 * (jnp.concatenate([attn, rw], axis=-1) @ w_out)
    h2 = rms_norm(x, norm2_g) * (1.0 + sc2) + sh2
    x = x + gt2 * moe_ffn(h2, router_w, router_b, moe_w_gu, moe_b_gu, moe_w_down, moe_b_down)
    return x, k, v, wkv_new, shift_new

def setup_inputs(seed: int = 0) -> dict:
    key = jax.random.key(seed)
    ks = jax.random.split(key, 40)

    def nrm(i, shape, s):
        return jax.random.normal(ks[i], shape, jnp.float32) * s

    buf = min(MAX_WINDOW, PAST_LEN)
    L, D, E, F = DEPTH, D_MODEL, N_EXPERTS, D_EXPERT
    return {
        'x_prompt': nrm(0, (BATCH, SEQ, D), 1.0),
        'x_sample': nrm(1, (DEC_BATCH, DEC_SEQ, D), 1.0),
        'cache_k': nrm(2, (L, DEC_BATCH, buf, N_ATTN_HEADS, HEAD_DIM), 1.0),
        'cache_v': nrm(3, (L, DEC_BATCH, buf, N_ATTN_HEADS, HEAD_DIM), 1.0),
        'state_wkv': nrm(4, (L, DEC_BATCH, N_RWKV_HEADS, HEAD_DIM, HEAD_DIM), 0.3),
        'state_shift': nrm(5, (L, DEC_BATCH, RWKV_COLS), 1.0),
        'c_prompt': nrm(6, (BATCH, D), 1.0),
        'c_sample': nrm(7, (DEC_BATCH, D), 1.0),
        'w_ada': nrm(8, (L, D, 6 * D), 0.5 * D ** -0.5),
        'b_ada': nrm(9, (L, 6 * D), 0.02),
        'norm1_g': 1.0 + nrm(10, (L, D), 0.02),
        'norm2_g': 1.0 + nrm(11, (L, D), 0.02),
        'w_in': nrm(12, (L, D, IN_COLS), D ** -0.5),
        'q_norm_g': 1.0 + nrm(13, (L, HEAD_DIM), 0.02),
        'k_norm_g': 1.0 + nrm(14, (L, HEAD_DIM), 0.02),
        'rwkv_mu': jax.random.uniform(ks[15], (L, RWKV_COLS), jnp.float32),
        'rwkv_w0': nrm(16, (L, RWKV_WIDTH), 0.5),
        'rwkv_w2': nrm(17, (L, DECAY_LORA, RWKV_WIDTH), DECAY_LORA ** -0.5),
        'rwkv_a0': nrm(18, (L, RWKV_WIDTH), 0.1),
        'rwkv_a2': nrm(19, (L, AAA_LORA, RWKV_WIDTH), AAA_LORA ** -0.5),
        'rwkv_g2': nrm(20, (L, GATE_LORA, RWKV_WIDTH), GATE_LORA ** -0.5),
        'rwkv_k_k': 0.85 + nrm(21, (L, RWKV_WIDTH), 0.05),
        'rwkv_k_a': 1.0 + nrm(22, (L, RWKV_WIDTH), 0.05),
        'rwkv_r_k': nrm(23, (L, N_RWKV_HEADS, HEAD_DIM), 0.1),
        'rwkv_ln_w': 1.0 + nrm(24, (L, RWKV_WIDTH), 0.02),
        'rwkv_ln_b': nrm(25, (L, RWKV_WIDTH), 0.02),
        'w_out': nrm(26, (L, MIX_WIDTH, D), MIX_WIDTH ** -0.5),
        'router_w': nrm(27, (L, D, E), D ** -0.5),
        'router_b': nrm(28, (L, E), 0.01),
        'moe_w_gu': nrm(29, (L, E, D, 2 * F), D ** -0.5),
        'moe_b_gu': nrm(30, (L, E, 2 * F), 0.02),
        'moe_w_down': nrm(31, (L, E, F, D), F ** -0.5),
        'moe_b_down': nrm(32, (L, E, D), 0.02),
    }

def reference(x_prompt, x_sample, cache_k, cache_v, state_wkv, state_shift, c_prompt, c_sample,
              w_ada, b_ada, norm1_g, norm2_g, w_in, q_norm_g, k_norm_g,
              rwkv_mu, rwkv_w0, rwkv_w2, rwkv_a0, rwkv_a2, rwkv_g2,
              rwkv_k_k, rwkv_k_a, rwkv_r_k, rwkv_ln_w, rwkv_ln_b, w_out,
              router_w, router_b, moe_w_gu, moe_b_gu, moe_w_down, moe_b_down):
    B, T, _ = x_prompt.shape
    keep = min(MAX_WINDOW, T)
    empty_kv = jnp.zeros((B, 0, N_ATTN_HEADS, HEAD_DIM), jnp.float32)
    zero_wkv = jnp.zeros((B, N_RWKV_HEADS, HEAD_DIM, HEAD_DIM), jnp.float32)
    zero_shift = jnp.zeros((B, RWKV_COLS), jnp.float32)
    yp, ys = x_prompt, x_sample
    kp_l, vp_l, sp_l, hp_l, ks_l, vs_l, ss_l, hs_l = [], [], [], [], [], [], [], []
    for l in range(DEPTH):
        lw = (w_ada[l], b_ada[l], norm1_g[l], norm2_g[l], w_in[l], q_norm_g[l], k_norm_g[l],
              rwkv_mu[l], rwkv_w0[l], rwkv_w2[l], rwkv_a0[l], rwkv_a2[l], rwkv_g2[l],
              rwkv_k_k[l], rwkv_k_a[l], rwkv_r_k[l], rwkv_ln_w[l], rwkv_ln_b[l], w_out[l],
              router_w[l], router_b[l], moe_w_gu[l], moe_b_gu[l], moe_w_down[l], moe_b_down[l])
        yp, kp, vp, sp, hp = layer_forward(yp, c_prompt, 0, empty_kv, empty_kv, zero_wkv, zero_shift, *lw)
        ys, kn, vn, sn, hn = layer_forward(ys, c_sample, PAST_LEN, cache_k[l], cache_v[l],
                                           state_wkv[l], state_shift[l], *lw)
        kp_l.append(kp[:, T - keep:])
        vp_l.append(vp[:, T - keep:])
        sp_l.append(sp)
        hp_l.append(hp)
        ks_l.append(kn)
        vs_l.append(vn)
        ss_l.append(sn)
        hs_l.append(hn)
    return (yp, ys, jnp.stack(kp_l), jnp.stack(vp_l), jnp.stack(sp_l), jnp.stack(hp_l),
            jnp.stack(ks_l), jnp.stack(vs_l), jnp.stack(ss_l), jnp.stack(hs_l))


_drawn_inputs = setup_inputs


def setup_inputs(seed=0):
    import zlib

    import numpy as np

    out = dict(_drawn_inputs(seed))
    spreads = {}
    factors = {'cache_k': 3.571,
     'cache_v': 2.747,
     'q_norm_g': 8.0,
     'k_norm_g': 23.845,
     'rwkv_k_k': 15.173,
     'rwkv_ln_w': 27.774,
     'rwkv_ln_b': 26.001,
     'router_b': 17.939,
     'moe_b_gu': 8.0,
     'moe_b_down': 24.49,
     'norm2_g': 4.729,
     'rwkv_r_k': 2.891}
    for name, (base, spread) in spreads.items():
        noise = np.random.default_rng([zlib.crc32(name.encode()), seed]).standard_normal(out[name].shape)
        drawn = base * np.exp(spread * noise) if base else spread * noise
        out[name] = __import__('jax').numpy.asarray(drawn.astype(out[name].dtype))
    for name, factor in factors.items():
        out[name] = (out[name] * factor).astype(out[name].dtype)
    return out
```

```python
from contextlib import ExitStack

import numpy as np

import concourse.bass as bass
from concourse import mybir

F32 = mybir.dt.float32
BF16 = mybir.dt.bfloat16
I32 = mybir.dt.int32
ALU = mybir.AluOpType
ACT = mybir.ActivationFunctionType
AXX = mybir.AxisListType.X

P = 128
D = 1024
KT = D // P
SEQ = 512
NB = 8
NT = SEQ // P
TOK = SEQ + NB
HD = 64
NH = 8
AW = NH * HD
RC = 3 * AW + 256
RF = RC // P
PAST = 2048
EXPERTS = 32
TOPK = 4
PATTERNS = ((128, 1), (512, 4), (2048, 16))
NORM_EPS = 1e-6
GN_EPS = 64e-5
ARENA = 26850
SLOT = 4096
NSLOT = 6


class Memory:
    pass


class Arena:

    def __init__(self, whole):
        self.whole, self.at = whole, 0

    def take(self, *dims, rows=P):
        n = int(np.prod(dims))
        v = self.whole[0:rows, self.at:self.at + n]
        self.at += n
        assert self.at <= self.whole.shape[1], self.at
        if len(dims) == 2:
            v = v.rearrange("p (a b) -> p a b", b=dims[1])
        if len(dims) == 3:
            v = v.rearrange("p (a b c) -> p a b c", b=dims[1], c=dims[2])
        return v


def rows_of(token_tile):
    return P if token_tile < NT else NB


def cols_of(token_tile):
    return slice(token_tile * P, token_tile * P + rows_of(token_tile))


def slot_view(wring, piece, n=512):
    s = piece % NSLOT
    return wring[:, s * SLOT:s * SLOT + KT * n].rearrange("p (k n) -> p k n", k=KT)


def wide(dram, c0, n=512):
    return dram.rearrange("(k p) n -> p k n", p=P)[:, :, c0:c0 + n]


def modulation(nc, io, m):
    NC = NB + 1
    NCH = 6 * D // 512
    with ExitStack() as ctx:
        sem = m.sem
        a = Arena(m.arena)
        c_rows = a.take(D, rows=NC)
        c_sig = a.take(D, rows=NC)
        mod = a.take(6 * D, rows=NC)
        bias = a.take(6 * D, rows=NC)
        gains = a.take(2, D, rows=NC)
        ct = a.take(KT, NC)
        levels = a.take(2 * LEVELS * P)
        c_in = sem("c_in")
        levels_in = sem("levels_in")
        bias_in = sem("bias_in")
        consts_in = sem("consts_in")
        ada_in = [sem(f"ada_in{i}") for i in range(NSLOT)]
        sig_done = sem("sig_done")
        silu_done = sem("silu_done")
        ct_psum = sem("ct_psum")
        ct_done = sem("ct_done")
        chunk_mm = sem("chunk_mm")
        chunk_added = sem("chunk_added")
        mod_scaled = sem("mod_scaled")
        mod_out = sem("mod_out")
        block = ctx.enter_context(nc.Block())

        @block.sync
        def _(sp):
            sp.dma_start(c_rows[0:NB, :], io["c_sample"]).then_inc(c_in, 16)
            sp.dma_start(c_rows[NB:NC, :], io["c_prompt"]).then_inc(c_in, 16)
            for n in range(NCH):
                if n >= NSLOT:
                    sp.wait_ge(chunk_mm, n - NSLOT + 1)
                sp.dma_start(slot_view(m.wring, n), wide(io["w_ada"][0], n * 512)).then_inc(ada_in[n % NSLOT], 16)
            sp.wait_ge(mod_scaled, 1)
            sp.dma_start(m.mod_dram, mod).then_inc(mod_out, 16)
            sp.wait_ge(mod_out, 16)

        @block.scalar
        def _(act):
            act.dma_start(m.ident[:, :], io["ident"]).then_inc(consts_in, 16)
            act.dma_start(bias, io["b_ada"].broadcast_to([NC, 6 * D])).then_inc(bias_in, 16)
            act.dma_start(gains[:, 0, :], io["norm1_g"].broadcast_to([NC, D])).then_inc(bias_in, 16)
            act.dma_start(gains[:, 1, :], io["norm2_g"].broadcast_to([NC, D])).then_inc(bias_in, 16)
            act.dma_start(levels, io["levels"]).then_inc(levels_in, 16)
            act.wait_ge(c_in, 32)
            nc.scalar.activation(c_sig, c_rows, ACT.Sigmoid).then_inc(sig_done, 1)

        @block.gpsimd
        def _(pool):
            pool.wait_ge(levels_in, 16)
            nc.gpsimd.tensor_copy(m.levels[:, :], levels)

        @block.vector
        def _(dve):
            dve.wait_ge(sig_done, 1)
            nc.vector.tensor_mul(c_rows, c_rows, c_sig).then_inc(silu_done, 1)
            dve.wait_ge(ct_psum, 1)
            nc.vector.tensor_copy(ct.rearrange("p k c -> p (k c)"), m.bank[7][:, 0:KT * NC]).then_inc(ct_done, 1)
            dve.wait_ge(bias_in, 48)
            for n in range(NCH):
                dve.wait_ge(chunk_mm, n + 1)
                nc.vector.tensor_add(mod[:, n * 512:(n + 1) * 512], m.bank[n % 2][0:NC, :],
                                     bias[:, n * 512:(n + 1) * 512]).then_inc(chunk_added, 1)
            dve.wait_ge(chunk_added, NCH)
            for i, scale_at in enumerate((1, 4)):
                v = mod[:, scale_at * D:(scale_at + 1) * D]
                last = nc.vector.scalar_tensor_tensor(v, v, 1.0, gains[:, i, :], ALU.add, ALU.mult)
            last.then_inc(mod_scaled, 1)

        @block.tensor
        def _(pe):
            pe.wait_ge(consts_in, 16)
            pe.wait_ge(silu_done, 1)
            for k in range(KT):
                last = nc.tensor.transpose(m.bank[7][:, k * NC:(k + 1) * NC], c_rows[:, k * P:(k + 1) * P],
                                           m.ident[0:NC, 0:NC])
            last.then_inc(ct_psum, 1)
            pe.wait_ge(ct_done, 1)
            for n in range(NCH):
                pe.wait_ge(ada_in[n % NSLOT], 16 * (n // NSLOT + 1))
                if n >= 2:
                    pe.wait_ge(chunk_added, n - 1)
                w = slot_view(m.wring, n)
                for k in range(KT):
                    last = nc.tensor.matmul(m.bank[n % 2][0:NC, :], ct[:, k, :], w[:, k, :],
                                            start=(k == 0), stop=(k == KT - 1))
                last.then_inc(chunk_mm, 1)


def projection(nc, io, m):
    with ExitStack() as ctx:
        sem = m.sem
        a = Arena(m.arena)
        a.at = m.scratch_at
        h = a.take(NT + 1, D)
        a.at = m.scratch_at
        qk = a.take(2, NT + 1, AW)
        tmp = a.take(2, AW)
        shift_rows = a.take(RC, rows=NB + 1)
        m.qk = qk
        a.at = m.rwkv_at
        row_p = a.take(2, D)
        row_s = a.take(2, D, rows=NB)
        gain = m.small.take(2, HD)
        cos = m.small.take(NT + 1, HD // 2)
        sin = m.small.take(NT + 1, HD // 2)
        ss = m.small.take(NT + 1)
        rstd = m.small.take(NT + 1)
        hs = m.small.take(2, NH)
        rn = m.small.take(2, NH)
        x_in = [sem(f"x_in{t}") for t in range(NT + 1)]
        rows_in = sem("rows_in")
        tables_in = sem("tables_in")
        win_in = [sem(f"win_in{i}") for i in range(7)]
        ss_set = sem("ss_set")
        squared = sem("squared")
        ms_done = sem("ms_done")
        rstd_done = sem("rstd_done")
        h_scaled = sem("h_scaled")
        h_done = sem("h_done")
        ht_psum = sem("ht_psum")
        ht_copied = sem("ht_copied")
        proj_mm = sem("proj_mm")
        proj_copied = sem("proj_copied")
        rwkv_mm = sem("rwkv_mm")
        rwkv_copied = sem("rwkv_copied")
        head_ms = sem("head_ms")
        head_rn = sem("head_rn")
        own = sem("vector_own")
        roped = sem("roped")
        qkt_psum = sem("qkt_psum")
        qkt_copied = sem("qkt_copied")
        shift_psum = sem("shift_psum")
        shift_done = sem("shift_done")
        edge_set = sem("edge_set")
        out_kv = sem("out_kv")
        units = [(n, t) for n in range(3) for t in range(NT + 1)]
        block = ctx.enter_context(nc.Block())

        def qk_of(n, t):
            if n == 2:
                return m.v_tok[:, t, :] if t < NT else m.v_new
            return qk[:, n, t, :]

        @block.sync
        def _(sp):
            for t in range(NT):
                sp.dma_start(h[:, t, :], io["x_prompt"][0, t * P:(t + 1) * P, :]).then_inc(x_in[t], 16)
            sp.dma_start(h[0:NB, NT, :], io["x_sample"][:, 0, :]).then_inc(x_in[NT], 16)
            for i in range(2):
                row = m.mod_dram[NB:NB + 1, i * D:(i + 1) * D]
                sp.dma_start(row_p[:, i, :], row.broadcast_to([P, D])).then_inc(rows_in, 16)
                sp.dma_start(row_s[:, i, :], m.mod_dram[0:NB, i * D:(i + 1) * D]).then_inc(rows_in, 16)
            for j in range(7):
                if j == NSLOT:
                    sp.wait_ge(proj_mm, NT + 1)
                n = 512 if j < 6 else 256
                sp.dma_start(slot_view(m.wring, j, n), wide(io["w_in"][0], j * 512, n)).then_inc(win_in[j], 16)
            for t in range(NT + 1):
                r = rows_of(t)
                sp.wait_ge(proj_copied, 2 * (NT + 1) + t + 1)
                dst = io["v_prompt"][0, 0, t * P:(t + 1) * P] if t < NT else io["v_new"][0, :, 0]
                sp.dma_start(dst.rearrange("t h d -> t (h d)"), qk_of(2, t)[0:r, :]).then_inc(out_kv, 16)
            for t in range(NT + 1):
                r = rows_of(t)
                sp.wait_ge(roped, NT + 1 + t + 1)
                dst = io["k_prompt"][0, 0, t * P:(t + 1) * P] if t < NT else io["k_new"][0, :, 0]
                sp.dma_start(dst.rearrange("t h d -> t (h d)"), qk[0:r, 1, t, :]).then_inc(out_kv, 16)
            sp.wait_ge(shift_done, 4)
            sp.dma_start(io["shift_sample"][0], shift_rows[1:NB + 1, :]).then_inc(out_kv, 16)
            sp.dma_start(io["shift_prompt"][0], shift_rows[0:1, :]).then_inc(out_kv, 16)
            sp.wait_ge(out_kv, 16 * (2 * (NT + 1) + 2))

        @block.scalar
        def _(act):
            act.dma_start(gain[:, 0, :], io["q_norm_g"].broadcast_to([P, HD])).then_inc(tables_in, 16)
            act.dma_start(gain[:, 1, :], io["k_norm_g"].broadcast_to([P, HD])).then_inc(tables_in, 16)
            act.dma_start(cos, io["cos"]).then_inc(tables_in, 16)
            act.dma_start(sin, io["sin"]).then_inc(tables_in, 16)
            act.wait_ge(ss_set, 1)
            for t in range(NT + 1):
                r = rows_of(t)
                act.wait_ge(x_in[t], 16)
                if t:
                    act.wait_ge(squared, t)
                nc.scalar.activation(tmp[0:r].rearrange("p a b -> p (a b)"), h[0:r, t, :], ACT.Square,
                                     accum_out=ss[0:r, t:t + 1]).then_inc(squared, 1)
            act.wait_ge(ms_done, 1)
            nc.scalar.activation(rstd, rstd, ACT.Sqrt).then_inc(rstd_done, 1)
            for t in range(NT + 1):
                r = rows_of(t)
                act.wait_ge(ht_psum, t + 1)
                for half in range(2):
                    src = m.bank[(2 * t + half) % 4][:, 0:4 * r].rearrange("p (k c) -> p k c", k=4)
                    nc.scalar.copy(m.ht[:, 4 * half:4 * half + 4, cols_of(t)], src).then_inc(ht_copied, 1)
            for u, (n, t) in enumerate(units):
                r = rows_of(t)
                act.wait_ge(proj_mm, u + 1)
                nc.scalar.copy(qk_of(n, t)[0:r, :], m.bank[4 + u % 4][0:r, :]).then_inc(proj_copied, 1)
                if n < 2:
                    act.wait_ge(head_ms, u + 1)
                    nc.scalar.activation(rn[0:r, u % 2, :], rn[0:r, u % 2, :], ACT.Sqrt).then_inc(head_rn, 1)
            for f in range(RF):
                act.wait_ge(rwkv_mm, f + 1)
                nc.scalar.copy(m.pp[:, f, 1:SEQ + 1], m.bank[f % 2][:, :])
                nc.scalar.copy(m.pp[:, f, SEQ + 1:], m.bank[2 + f % 2][:, 0:NB]).then_inc(rwkv_copied, 1)
            for u in range(2 * NT):
                n, t = u // NT, u % NT
                act.wait_ge(qkt_psum, u + 1)
                nc.scalar.copy((m.kt if n else m.qt)[:, :, cols_of(t)],
                               m.bank[4 + u % 4][:, :].rearrange("p (k c) -> p k c", k=4)).then_inc(qkt_copied, 1)

        @block.vector
        def _(dve):
            nc.vector.memset(ss, 1.0).then_inc(ss_set, 1)
            nc.vector.memset(m.pp[:, :, 0:1], 0.0).then_inc(edge_set, 1)
            dve.wait_ge(squared, NT + 1)
            nc.vector.tensor_scalar(rstd, ss, 1.0 / D, NORM_EPS, ALU.mult, ALU.add).then_inc(own, 1)
            dve.wait_ge(own, 1)
            nc.vector.reciprocal(rstd, rstd).then_inc(ms_done, 1)
            dve.wait_ge(rstd_done, 1)
            dve.wait_ge(rows_in, 64)
            for t in range(NT + 1):
                r = rows_of(t)
                rows = row_p if t < NT else row_s
                nc.vector.scalar_tensor_tensor(h[0:r, t, :], h[0:r, t, :], rstd[0:r, t:t + 1], rows[0:r, 1, :],
                                               ALU.mult, ALU.mult).then_inc(h_scaled, 1)
                dve.wait_ge(h_scaled, t + 1)
                nc.vector.tensor_add(h[0:r, t, :], h[0:r, t, :], rows[0:r, 0, :]).then_inc(h_done, 1)
            dve.wait_ge(tables_in, 64)
            done = 1

            def head_sums(u):
                nonlocal done
                n, t = units[u]
                r = rows_of(t)
                x = qk[0:r, n, t, :]
                dve.wait_ge(proj_copied, u + 1)
                if u:
                    dve.wait_ge(own, done)
                    dve.wait_ge(roped, u)
                nc.vector.tensor_mul(tmp[0:r, 0, :], x, x).then_inc(own, 1)
                dve.wait_ge(own, done + 1)
                nc.vector.tensor_reduce(hs[0:r, u % 2, :], tmp[0:r, 0, :].rearrange("p (h d) -> p h d", d=HD),
                                        AXX, ALU.add).then_inc(own, 1)
                dve.wait_ge(own, done + 2)
                nc.vector.tensor_scalar(hs[0:r, u % 2, :], hs[0:r, u % 2, :], 1.0 / HD, NORM_EPS, ALU.mult,
                                        ALU.add).then_inc(own, 1)
                dve.wait_ge(own, done + 3)
                nc.vector.reciprocal(rn[0:r, u % 2, :], hs[0:r, u % 2, :]).then_inc(head_ms, 1)
                done += 3

            def rotate(u):
                nonlocal done
                n, t = units[u]
                r = rows_of(t)
                x = qk[0:r, n, t, :]
                heads = x.rearrange("p (h d) -> p h d", d=HD)
                halves = x.rearrange("p (h s d) -> p h s d", h=NH, s=2)
                c, s = (tmp[0:r, i, :].rearrange("p (h s d) -> p h s d", h=NH, s=2) for i in range(2))
                wide_of = lambda table: table[0:r, t, :].unsqueeze(1).unsqueeze(1).broadcast_to([r, NH, 2, HD // 2])
                dve.wait_ge(head_rn, u + 1)
                nc.vector.tensor_mul(heads, heads, rn[0:r, u % 2, :].unsqueeze(2).broadcast_to([r, NH, HD])).then_inc(own, 1)
                dve.wait_ge(own, done + 1)
                nc.vector.tensor_mul(heads, heads, gain[0:r, n, :].unsqueeze(1).broadcast_to([r, NH, HD])).then_inc(own, 1)
                dve.wait_ge(own, done + 2)
                nc.vector.tensor_mul(c, halves, wide_of(cos)).then_inc(own, 1)
                nc.vector.tensor_mul(s, halves, wide_of(sin)).then_inc(own, 1)
                dve.wait_ge(own, done + 4)
                nc.vector.tensor_sub(halves[:, :, 0, :], c[:, :, 0, :], s[:, :, 1, :]).then_inc(own, 1)
                nc.vector.tensor_add(halves[:, :, 1, :], c[:, :, 1, :], s[:, :, 0, :]).then_inc(roped, 1)
                done += 5

            for u in range(2 * (NT + 1)):
                head_sums(u)
                rotate(u)
            for b in range(4):
                n = min(512, RC - b * 512)
                dve.wait_ge(shift_psum, 1)
                nc.vector.tensor_copy(shift_rows[:, b * 512:b * 512 + n], m.bank[b][0:NB + 1, 0:n]).then_inc(shift_done, 1)

        @block.tensor
        def _(pe):
            for t in range(NT + 1):
                r = rows_of(t)
                pe.wait_ge(h_done, t + 1)
                if t >= 2:
                    pe.wait_ge(ht_copied, 2 * (t - 1))
                for k in range(KT):
                    bank = m.bank[(2 * t + k // 4) % 4]
                    last = nc.tensor.transpose(bank[:, (k % 4) * r:(k % 4 + 1) * r], h[0:r, t, k * P:(k + 1) * P],
                                               m.ident[0:r, 0:r])
                last.then_inc(ht_psum, 1)
            for u, (n, t) in enumerate(units):
                r = rows_of(t)
                pe.wait_ge(ht_copied, 2 * (t + 1))
                pe.wait_ge(win_in[n], 16)
                if u >= 4:
                    pe.wait_ge(proj_copied, u - 3)
                w = slot_view(m.wring, n)
                for k in range(KT):
                    last = nc.tensor.matmul(m.bank[4 + u % 4][0:r, :], m.ht[:, k, cols_of(t)], w[:, k, :],
                                            start=(k == 0), stop=(k == KT - 1))
                last.then_inc(proj_mm, 1)
            for f in range(RF):
                j = 3 + f // 4
                pe.wait_ge(win_in[j], 16)
                if f >= 2:
                    pe.wait_ge(rwkv_copied, f - 1)
                w = slot_view(m.wring, j, 512 if j < 6 else 256)
                for out, cols in ((m.bank[f % 2][:, :], slice(0, SEQ)), (m.bank[2 + f % 2][:, 0:NB], slice(SEQ, TOK))):
                    for k in range(KT):
                        last = nc.tensor.matmul(out, w[:, k, (f % 4) * P:(f % 4 + 1) * P], m.ht[:, k, cols],
                                                start=(k == 0), stop=(k == KT - 1))
                last.then_inc(rwkv_mm, 1)
            for u in range(2 * NT):
                n, t = u // NT, u % NT
                pe.wait_ge(roped, n * (NT + 1) + t + 1)
                if u >= 4:
                    pe.wait_ge(qkt_copied, u - 3)
                else:
                    pe.wait_ge(proj_copied, 3 * (NT + 1))
                for j in range(4):
                    last = nc.tensor.transpose(m.bank[4 + u % 4][:, j * P:(j + 1) * P],
                                               qk[:, n, t, j * P:(j + 1) * P], m.ident[:, :])
                last.then_inc(qkt_psum, 1)
            pe.wait_ge(rwkv_copied, RF)
            for f in range(RF):
                last = nc.tensor.transpose(m.bank[f // 4][0:NB + 1, (f % 4) * P:(f % 4 + 1) * P],
                                           m.pp[:, f, SEQ:SEQ + NB + 1], m.ident[:, :])
            last.then_inc(shift_psum, 1)


def attention(nc, io, m):
    SCALE = 1.0 / 8.0
    G = 4
    assert HD == 64
    with ExitStack() as ctx:
        sem = m.sem
        a = Arena(m.wring)
        bias = a.take(SEQ)
        prob = a.take(3, SEQ)
        prob_t = a.take(2, SEQ)
        kg = a.take(2, G, AW)
        vg = a.take(2, G, AW)
        prod = a.take(G, AW)
        pick = a.take(NB, P, rows=NB)
        head_mask = a.take(AW, rows=NH)
        own_v = a.take(2, AW, rows=NH)
        sbias = a.take(G * NH)
        sc = a.take(NB, G * NH)
        smax = a.take(NB * NH)
        gmax = a.take(NB * NH)
        rs = a.take(NB, rows=NH)
        ones = a.take(1)
        top = a.take(32)
        ntop = a.take(32)
        psum_of_p = a.take(32)
        rinv = a.take(32)
        tables_in = sem("tables_in")
        scores_mm = sem("scores_mm")
        top_done = sem("top_done")
        max_ready = sem("max_ready")
        exp_done = sem("exp_done")
        inverse = sem("inverse")
        p_normed = sem("p_normed")
        pt_psum = sem("pt_psum")
        pt_copied = sem("pt_copied")
        pv_mm = sem("pv_mm")
        ct_copied = sem("ct_copied")
        pad_set = sem("pad_set")
        pick_set = sem("pick_set")
        kg_in = [sem(f"kg_in{i}") for i in range(2)]
        vg_in = [sem(f"vg_in{i}") for i in range(2)]
        q_spread = sem("q_spread")
        multiplied = sem("multiplied")
        scored = sem("scored")
        biased = sem("biased")
        sample_max = sem("sample_max")
        global_max = sem("global_max")
        centred = sem("centred")
        sample_exp = sem("sample_exp")
        sample_pv = sem("sample_pv")
        sample_inv = sem("sample_inv")
        own_kept = sem("own_kept")
        sample_ct = sem("sample_ct")
        units = [(h, i) for h in range(NH) for i in range(NT)]
        U = len(units)
        block = ctx.enter_context(nc.Block())

        def base(h):
            return HD * (h % 2)

        @block.sync
        def _(sp):
            sp.dma_start(bias, io["attn_bias"]).then_inc(tables_in, 16)
            sp.dma_start(sbias, io["sample_bias"]).then_inc(tables_in, 16)
            sp.dma_start(head_mask, io["head_mask"]).then_inc(tables_in, 16)
            sp.wait_ge(pad_set, 2)
            for cache, new, grp, landed, freed in ((io["cache_k"], m.qk[:, 1, NT, :], kg, kg_in, multiplied),
                                                   (io["cache_v"], m.v_new, vg, vg_in, sample_pv)):
                for b in range(NB):
                    if b >= 2:
                        sp.wait_ge(freed, b - 1)
                    past = cache[0, b].rearrange("t h d -> t (h d)")
                    for g, (w, d) in enumerate(PATTERNS):
                        sp.dma_start(grp[:, b % 2, g, :], past[PAST - w:PAST:d, :]).then_inc(landed[b % 2], 16)
                    sp.dma_start(grp[0:1, b % 2, 3, :], new[b:b + 1, :]).then_inc(landed[b % 2], 16)

        @block.gpsimd
        def _(pool):
            nc.gpsimd.memset(kg[:, :, 3, :], 0.0).then_inc(pad_set, 1)
            nc.gpsimd.memset(vg[:, :, 3, :], 0.0).then_inc(pad_set, 1)
            pool.wait_ge(sample_max, 1)
            nc.gpsimd.partition_all_reduce(gmax, smax, P, bass.bass_isa.ReduceOp.max).then_inc(global_max, 1)

        @block.scalar
        def _(act):
            for s in range(U + 2):
                if s < U:
                    h, i = units[s]
                    w = (i + 1) * P
                    act.wait_ge(max_ready, s + 1)
                    nc.scalar.activation(prob[:, s % 3, 0:w], prob[:, s % 3, 0:w], ACT.Exp, bias=ntop[:, s:s + 1],
                                         scale=SCALE, accum_out=psum_of_p[:, s:s + 1]).then_inc(exp_done, 1)
                if s >= 2:
                    u = s - 2
                    w = (units[u][1] + 1) * P
                    act.wait_ge(pt_psum, u + 1)
                    if u >= 2:
                        act.wait_ge(pv_mm, u - 1)
                    nc.scalar.copy(prob_t[:, u % 2, 0:w], m.bank[3 + u % 2][:, 0:w]).then_inc(pt_copied, 1)
            act.wait_ge(centred, 1)
            nc.scalar.activation(sc, sc, ACT.Exp, scale=SCALE).then_inc(sample_exp, 1)

        @block.vector
        def _(dve):
            nc.vector.memset(ones, 1.0).then_inc(pick_set, 1)
            nc.vector.tensor_copy(pick, m.ident[0:NB, 0:NB].unsqueeze(2).broadcast_to([NB, NB, P])).then_inc(pick_set, 1)
            dve.wait_ge(tables_in, 48)
            for s in range(U + 3):
                if s < U:
                    w = (units[s][1] + 1) * P
                    dve.wait_ge(scores_mm, s + 1)
                    if s >= 3:
                        dve.wait_ge(pt_psum, s - 2)
                    nc.vector.tensor_tensor_reduce(prob[:, s % 3, 0:w], m.bank[s % 3][:, 0:w], bias[:, SEQ - w:SEQ],
                                                   1.0, -3.0e38, ALU.add, ALU.max, top[:, s:s + 1]).then_inc(top_done, 1)
                    dve.wait_ge(top_done, s + 1)
                    nc.vector.tensor_scalar(ntop[:, s:s + 1], top[:, s:s + 1], -SCALE, None, ALU.mult).then_inc(max_ready, 1)
                if 1 <= s <= U:
                    u = s - 1
                    w = (units[u][1] + 1) * P
                    dve.wait_ge(exp_done, u + 1)
                    nc.vector.reciprocal(rinv[:, u:u + 1], psum_of_p[:, u:u + 1]).then_inc(inverse, 1)
                    dve.wait_ge(inverse, u + 1)
                    nc.vector.tensor_scalar(prob[:, u % 3, 0:w], prob[:, u % 3, 0:w], rinv[:, u:u + 1], None,
                                            ALU.mult).then_inc(p_normed, 1)
                if s >= 3:
                    u = s - 3
                    h, i = units[u]
                    dve.wait_ge(pv_mm, u + 1)
                    nc.vector.tensor_copy(m.ct[base(h):base(h) + HD, h // 2, i * P:(i + 1) * P],
                                          m.bank[5 + u % 2][base(h):base(h) + HD, 0:P]).then_inc(ct_copied, 1)
            for b in range(NB):
                dve.wait_ge(kg_in[b % 2], 64 * (b // 2 + 1))
                dve.wait_ge(q_spread, b + 1)
                if b:
                    dve.wait_ge(scored, b)
                nc.vector.tensor_mul(prod, kg[:, b % 2], m.bank[b % 2][:, :].unsqueeze(1).broadcast_to([P, G, AW]))\
                    .then_inc(multiplied, 1)
                dve.wait_ge(multiplied, b + 1)
                nc.vector.tensor_reduce(sc[:, b, :], prod.rearrange("p g (h d) -> p (g h) d", d=HD), AXX, ALU.add)\
                    .then_inc(scored, 1)
            dve.wait_ge(scored, NB)
            nc.vector.tensor_add(sc, sc, sbias.unsqueeze(1).broadcast_to([P, NB, G * NH])).then_inc(biased, 1)
            dve.wait_ge(biased, 1)
            nc.vector.tensor_reduce(smax.rearrange("p (b h) -> p b h", b=NB), sc.rearrange("p b (g h) -> p b h g", g=G),
                                    AXX, ALU.max).then_inc(sample_max, 1)
            dve.wait_ge(global_max, 1)
            by_head = sc.rearrange("p b (g h) -> p b g h", g=G)
            nc.vector.tensor_sub(by_head, by_head, gmax.rearrange("p (b h) -> p b h", b=NB).unsqueeze(2)
                                 .broadcast_to([P, NB, G, NH])).then_inc(centred, 1)
            for b in range(NB):
                dve.wait_ge(sample_pv, b + 1)
                nc.vector.reciprocal(rs[:, b:b + 1], m.bank[2 + b % 2][0:NH, 0:1]).then_inc(sample_inv, 1)
                dve.wait_ge(sample_inv, b + 1)
                nc.vector.scalar_tensor_tensor(own_v[:, b % 2, :], m.bank[b % 2][0:NH, :], rs[:, b:b + 1], head_mask,
                                               ALU.mult, ALU.mult).then_inc(own_kept, 1)
            dve.wait_ge(sample_ct, NB)
            nc.vector.tensor_copy(m.ct[:, 0:4, SEQ:TOK], m.bank[4][:, 0:4 * NB].rearrange("p (k b) -> p k b", k=4))

        @block.tensor
        def _(pe):
            for s in range(U + 3):
                if s < U:
                    h, i = units[s]
                    if s >= 3:
                        pe.wait_ge(top_done, s - 2)
                    rows = slice(base(h), base(h) + HD)
                    nc.tensor.matmul(m.bank[s % 3][:, 0:(i + 1) * P], m.qt[rows, h // 2, i * P:(i + 1) * P],
                                     m.kt[rows, h // 2, 0:(i + 1) * P], start=True, stop=True).then_inc(scores_mm, 1)
                if 2 <= s < U + 2:
                    u = s - 2
                    pe.wait_ge(p_normed, u + 1)
                    if u >= 2:
                        pe.wait_ge(pt_copied, u - 1)
                    for j in range(units[u][1] + 1):
                        last = nc.tensor.transpose(m.bank[3 + u % 2][:, j * P:(j + 1) * P],
                                                   prob[:, u % 3, j * P:(j + 1) * P], m.ident[:, :])
                    last.then_inc(pt_psum, 1)
                if s >= 3:
                    u = s - 3
                    h, i = units[u]
                    pe.wait_ge(pt_copied, u + 1)
                    if u >= 2:
                        pe.wait_ge(ct_copied, u - 1)
                    for j in range(i + 1):
                        last = nc.tensor.matmul(m.bank[5 + u % 2][base(h):base(h) + HD, 0:P],
                                                m.v_tok[:, j, h * HD:(h + 1) * HD], prob_t[:, u % 2, j * P:(j + 1) * P],
                                                start=(j == 0), stop=(j == i))
                    last.then_inc(pv_mm, 1)
            pe.wait_ge(pick_set, 2)
            pe.wait_ge(top_done, U)
            for b in range(NB):
                if b >= 2:
                    pe.wait_ge(multiplied, b - 1)
                nc.tensor.matmul(m.bank[b % 2][:, :], pick[:, b, :], m.qk[0:NB, 0, NT, :], start=True,
                                 stop=True).then_inc(q_spread, 1)
            pe.wait_ge(multiplied, NB)
            pe.wait_ge(sample_exp, 1)
            pe.wait_ge(pt_copied, U)
            for b in range(NB + 1):
                if b < NB:
                    pe.wait_ge(vg_in[b % 2], 64 * (b // 2 + 1))
                    if b >= 2:
                        pe.wait_ge(own_kept, b - 1)
                    for g in range(G):
                        p_bg = sc[:, b, g * NH:(g + 1) * NH]
                        nc.tensor.matmul(m.bank[b % 2][0:NH, :], p_bg, vg[:, b % 2, g, :], start=(g == 0), stop=(g == G - 1))
                        last = nc.tensor.matmul(m.bank[2 + b % 2][0:NH, 0:1], p_bg, ones, start=(g == 0), stop=(g == G - 1))
                    last.then_inc(sample_pv, 1)
                if b:
                    pe.wait_ge(own_kept, b)
                    for k in range(4):
                        last = nc.tensor.matmul(m.bank[4][:, k * NB + b - 1:k * NB + b],
                                                own_v[:, (b - 1) % 2, k * P:(k + 1) * P], ones[0:NH, :], start=True, stop=True)
                    last.then_inc(sample_ct, 1)


CHUNK = 64
PAIRS = 4
LEVELS = 6
DECAY = float(np.exp(-0.5))
MU, W0, A0, KK_, KA, RK, LNW, LNB = 0, 14, 18, 22, 26, 30, 34, 38
N_PAR = 42


def rwkv(nc, io, m):
    with ExitStack() as ctx:
        sem = m.sem
        w = Arena(m.wring)
        tmp_a, tmp_b, cum = (w.take(PAIRS, TOK) for _ in range(3))
        ar = w.take(PAIRS, NT * 2 * P).rearrange("p h (t x c) -> p h t x c", t=NT, x=2)
        bt, kt = w.take(PAIRS, SEQ), w.take(PAIRS, SEQ)
        b_tok, k_tok, v_tok, a_tok = (w.take(NT, AW) for _ in range(4))
        lora_wa, lora_g = w.take(AW), w.take(AW)
        ones_blk = w.take(P)
        restart = w.take(SEQ)
        tri = w.take(2, P)
        w.at = 0
        lm = [w.take(NT, 2 * P).rearrange("p t (x c) -> p t x c", x=2) for _ in range(2)]
        x_inv, x_inv_t, z = ([w.take(NT, P) for _ in range(2)] for _ in range(3))
        mv = [w.take(NT, HD) for _ in range(2)]
        w.at = 3 * PAIRS * TOK + 2 * PAIRS * SEQ + PAIRS * SEQ
        state = w.take(2, PAIRS * P).rearrange("p b (h d) -> p b h d", h=PAIRS)
        sa = w.take(2, PAIRS * 2 * HD).rearrange("p b (h s d) -> p b h s d", h=PAIRS, s=2)
        w.at = 3 * PAIRS * TOK
        ys = w.take(PAIRS, TOK)
        y_sq = w.take(PAIRS, TOK)
        a = Arena(m.arena)
        a.at = m.rwkv_at
        g = a.take(PAIRS, TOK)
        r = a.take(PAIRS, TOK)
        nn_at = a.at
        k = a.take(PAIRS, TOK)
        v = a.take(PAIRS, TOK)
        ga = a.take(PAIRS, TOK)
        sw = a.take(PAIRS, TOK)
        kk_at = a.at
        kk = a.take(PAIRS, TOK)
        par_rows = a.take(P, rows=N_PAR)
        a.at = kk_at
        xl = a.take(2, TOK)
        a.at = nn_at
        nn = a.take(PAIRS * 2 * NT, 2 * P).rearrange("p u (x c) -> p u x c", x=2)
        u_tok = a.take(NT, PAIRS * 2 * HD).rearrange("p t (h s d) -> p t h s d", h=PAIRS, s=2)
        a.at = m.pp_at
        sx = a.take(6, AW, rows=NB)
        a.at = m.pp_at
        wt = a.take(PAIRS, SEQ)
        s_st = a.take(32, HD)
        s_tmp = a.take(32, HD)
        y_rows = m.small.take(AW, rows=NB)
        par = m.small.take(N_PAR)
        ka1 = m.small.take(PAIRS)
        sh = m.small.take(RF, NB)
        sh_rows = tmp_a.rearrange("p h t -> p (h t)")[0:NB, 0:RC]
        pend = m.small.take(PAIRS, SEQ // CHUNK)
        sp_in = m.small.take(5, HD)
        sv_in = m.small.take(32)
        s_sa = m.small.take(32)
        s_y = m.small.take(32)
        names = ("tables_in state_in params_psum params_done mixed_lora lora_act lora_in lora_mm gates_done ones_in "
                 "mixed_rkv kk_sq kk_sum kk_norm kk_done keys_done scanned exp_p exp_pm exp_m pm_ready ar_r ar_a b_ready "
                 "em_used bar_ready tok_psum tok_done bonus_in bonus_psum bonus_done sx_psum sx_done sx_out sx_in "
                 "s_ta s_sa_done s_new s_tr s_y_done s_y_out s_y_in s_y_psum "
                 "score_mm score_masked x_init z_mm z_copied xz_mm xt_mm x_new xt_new mv_mm mv_copied wt_mm wt_copied "
                 "u_mm u_copied sa_mm sa_done st_mm st_done y_mm y_copied state_psum state_rows_done wkv_out "
                 "mean_mm centred squared var_mm var_ready root_done own normed scaled").split()
        q = {n: sem("rw_" + n) for n in names}
        cols = (slice(0, SEQ), slice(SEQ, TOK))
        block = ctx.enter_context(nc.Block())

        def half(s):
            return slice(HD * s, HD * s + HD)

        @block.sync
        def _(sp):
            sp.dma_start(sh_rows, io["state_shift"][0]).then_inc(q["state_in"], 16)
            at = 0
            for src, n in ((io["rwkv_mu"], RF), (io["rwkv_w0"], 4), (io["rwkv_a0"], 4), (io["rwkv_k_k"], 4), (io["rwkv_k_a"], 4),
                           (io["rwkv_r_k"], 4), (io["rwkv_ln_w"], 4), (io["rwkv_ln_b"], 4)):
                flat = src[0].rearrange("h d -> (h d)") if len(src.shape) == 3 else src[0]
                sp.dma_start(par_rows[at:at + n, :], flat.rearrange("(n p) -> n p", p=P)).then_inc(q["tables_in"], 16)
                at += n
            sp.dma_start(lora_wa[0:HD, :], io["rwkv_w2"][0]).then_inc(q["lora_in"], 16)
            sp.dma_start(lora_wa[HD:P, :], io["rwkv_a2"][0]).then_inc(q["lora_in"], 16)
            sp.dma_start(lora_g, io["rwkv_g2"][0]).then_inc(q["lora_in"], 16)
            sp.dma_start(ones_blk, io["ones_blk"]).then_inc(q["ones_in"], 16)
            sp.dma_start(restart, io["restart"]).then_inc(q["ones_in"], 16)
            sp.dma_start(tri, io["tri"]).then_inc(q["ones_in"], 16)
            sp.wait_ge(q["sx_done"], 6)
            sp.dma_start(m.sx_dram.rearrange("i b c -> b i c"), sx).then_inc(q["sx_out"], 16)
            sp.wait_ge(q["sx_out"], 16)
            for i in range(5):
                for u in range(2):
                    sp.dma_start(sp_in[u:P:2, i, :], m.sx_dram[i].rearrange("b (h d) -> (b h) d", d=HD)).then_inc(q["sx_in"], 16)
            sp.dma_start(sv_in, m.sx_dram[5].rearrange("b (p d) -> (b p) d", d=32)).then_inc(q["sx_in"], 16)
            sp.dma_start(s_st.rearrange("p v k -> p (v k)"),
                         io["state_wkv"][0].rearrange("b h (u v) k -> (b h u) (v k)", u=2)).then_inc(q["sx_in"], 16)
            sp.wait_ge(q["s_new"], 5)
            sp.dma_start(io["wkv_sample"][0].rearrange("b h (u v) k -> (b h u) (v k)", u=2),
                         s_st.rearrange("p v k -> p (v k)")).then_inc(q["wkv_out"], 16)
            sp.wait_ge(q["s_y_done"], 1)
            sp.dma_start(m.sy_dram.rearrange("b (p d) -> (b p) d", d=32), s_y).then_inc(q["s_y_out"], 16)
            sp.wait_ge(q["s_y_out"], 16)
            sp.dma_start(y_rows, m.sy_dram).then_inc(q["s_y_in"], 16)
            sp.wait_ge(q["state_rows_done"], 1)
            for h in range(NH):
                sp.dma_start(io["wkv_prompt"][0, 0, h], tmp_a[half(h % 2), 0, h * HD:(h + 1) * HD])\
                    .then_inc(q["wkv_out"], 16)
            sp.wait_ge(q["wkv_out"], 16 * (1 + NH))

        @block.gpsimd
        def _(pool):
            bc = lambda i: sp_in[:, i, :].unsqueeze(1).broadcast_to([P, 32, HD])
            bv = lambda x: x.unsqueeze(2).broadcast_to([P, 32, HD])
            pool.wait_ge(q["sx_in"], 16 * 12)
            nc.gpsimd.tensor_tensor(s_tmp, s_st, bc(2), ALU.mult).then_inc(q["s_ta"], 1)
            pool.wait_ge(q["s_ta"], 1)
            nc.gpsimd.tensor_tensor(s_st, s_st, bc(4), ALU.mult).then_inc(q["s_new"], 1)
            pool.wait_ge(q["s_sa_done"], 1)
            nc.gpsimd.tensor_tensor(s_tmp, bv(s_sa), bc(3), ALU.mult).then_inc(q["s_new"], 1)
            pool.wait_ge(q["s_new"], 2)
            nc.gpsimd.tensor_tensor(s_st, s_st, s_tmp, ALU.add).then_inc(q["s_new"], 1)
            pool.wait_ge(q["s_new"], 3)
            nc.gpsimd.tensor_tensor(s_tmp, bv(sv_in), bc(1), ALU.mult).then_inc(q["s_new"], 1)
            pool.wait_ge(q["s_new"], 4)
            nc.gpsimd.tensor_tensor(s_st, s_st, s_tmp, ALU.add).then_inc(q["s_new"], 1)
            pool.wait_ge(q["s_new"], 5)
            nc.gpsimd.tensor_tensor(s_tmp, s_st, bc(0), ALU.mult).then_inc(q["s_tr"], 1)

        @block.scalar
        def _(act):
            act.wait_ge(q["mixed_lora"], 1)
            nc.scalar.activation(xl[0:HD, 0, :], xl[0:HD, 0, :], ACT.Tanh).then_inc(q["lora_act"], 1)
            nc.scalar.activation(xl[:, 1, :], xl[:, 1, :], ACT.Sigmoid).then_inc(q["lora_act"], 1)
            act.wait_ge(q["params_done"], 1)
            for y, (dst, func, bias0) in enumerate(((sw, ACT.Sigmoid, W0), (ga, ACT.Sigmoid, A0), (g, ACT.Identity, None))):
                for h in range(PAIRS):
                    i = y * PAIRS + h
                    act.wait_ge(q["lora_mm"], i + 1)
                    for c, src in ((cols[0], m.bank[i % 6][:, :]), (cols[1], m.bank[6 + i % 2][:, 0:NB])):
                        if bias0 is None:
                            last = nc.scalar.copy(dst[:, h, c], src)
                        else:
                            last = nc.scalar.activation(dst[:, h, c], src, func, bias=par[:, bias0 + h:bias0 + h + 1])
                    last.then_inc(q["gates_done"], 1)
            for h in range(PAIRS):
                act.wait_ge(q["kk_sum"], h + 1)
                nc.scalar.activation(tmp_b[:, h, cols[0]], m.bank[h][:, :], ACT.Sqrt)
                nc.scalar.activation(tmp_b[:, h, cols[1]], m.bank[4 + h][:, 0:NB], ACT.Sqrt).then_inc(q["kk_norm"], 1)
            for i in range(6):
                act.wait_ge(q["sx_psum"], i + 1)
                src = m.bank[i][0:NB, :]
                if i == 4:
                    last = nc.scalar.activation(sx[:, i, :], src, ACT.Exp, scale=-DECAY)
                elif i == 2:
                    last = nc.scalar.mul(sx[:, i, :], src, -1.0)
                else:
                    last = nc.scalar.copy(sx[:, i, :], src)
                last.then_inc(q["sx_done"], 1)
            act.wait_ge(q["scanned"], PAIRS)
            act.wait_ge(q["kk_done"], 1)
            nc.scalar.activation(tmp_b[:, :, 0:SEQ], cum[:, :, 0:SEQ], ACT.Exp, scale=-DECAY).then_inc(q["exp_p"], 1)
            act.wait_ge(q["pm_ready"], 1)
            nc.scalar.activation(tmp_a[:, :, 0:SEQ], tmp_a[:, :, 0:SEQ], ACT.Exp, scale=-DECAY).then_inc(q["exp_pm"], 1)
            act.wait_ge(q["ar_a"], 1)
            nc.scalar.activation(tmp_a[:, :, 0:SEQ], cum[:, :, 0:SEQ], ACT.Exp, scale=DECAY).then_inc(q["exp_m"], 1)
            for i, dst in enumerate((v_tok, a_tok, k_tok, b_tok)):
                for t in range(NT):
                    act.wait_ge(q["tok_psum"], i * NT + t + 1)
                    nc.scalar.copy(dst[:, t, :], m.bank[(i * NT + t) % 6][:, :]).then_inc(q["tok_done"], 1)
            nz = 0
            for h in range(PAIRS):
                for lev in range(LEVELS):
                    for s in range(2):
                        if lev == 0:
                            continue
                        nz += 1
                        act.wait_ge(q["z_mm"], nz)
                        nc.scalar.copy(z[s].rearrange("p t c -> p (t c)"), m.bank[3 * s][:, :]).then_inc(q["z_copied"], 1)
                for s in range(2):
                    i = 2 * h + s
                    act.wait_ge(q["mv_mm"], i + 1)
                    nc.scalar.copy(mv[s].rearrange("p t d -> p (t d)"), m.bank[3 * s][:, 0:NT * HD]).then_inc(q["mv_copied"], 1)
                    act.wait_ge(q["wt_mm"], i + 1)
                    if i == 0:
                        act.wait_ge(q["sx_out"], 16)
                    nc.scalar.copy(wt[half(s), h, :], m.bank[3 * s + 1][half(s), :]).then_inc(q["wt_copied"], 1)
                    act.wait_ge(q["u_mm"], i + 1)
                    nc.scalar.copy(u_tok[:, :, h, s, :], m.bank[3 * s + 2][:, 0:NT * HD].rearrange("p (t d) -> p t d", t=NT))\
                        .then_inc(q["u_copied"], 1)
            for h in range(PAIRS):
                act.wait_ge(q["y_mm"], 8 * PAIRS)
                last = nc.scalar.copy(ys[:, h, 0:SEQ], m.bank[h][:, :])
            act.wait_ge(q["s_y_psum"], 1)
            nc.scalar.copy(ys[:, :, SEQ:TOK], m.bank[6][:, 0:PAIRS * NB].rearrange("p (h b) -> p h b", h=PAIRS)).then_inc(q["y_copied"], 1)
            act.wait_ge(q["var_ready"], 1)
            nc.scalar.activation(y_sq, y_sq, ACT.Sqrt).then_inc(q["root_done"], 1)

        @block.vector
        def _(dve):
            n_own = [0]

            def link(ins):
                n_own[0] += 1
                ins.then_inc(q["own"], 1)
                dve.wait_ge(q["own"], n_own[0])

            V = nc.vector
            dve.wait_ge(q["params_psum"], 1)
            link(V.tensor_copy(par, m.bank[0][:, 0:N_PAR]))
            V.tensor_copy(sh.rearrange("p f b -> p (f b)"), m.bank[1][:, 0:RF * NB]).then_inc(q["own"], 1)
            n_own[0] += 1
            V.tensor_scalar(ka1, par[:, KA:KA + PAIRS], -1.0, 1.0, ALU.mult, ALU.add).then_inc(q["params_done"], 1)
            dve.wait_ge(q["own"], n_own[0])
            cur_s = m.pp[:, :, SEQ + 1:]
            link(V.tensor_sub(sh, sh, cur_s))
            link(V.tensor_mul(sh, sh, par[:, MU:MU + RF].unsqueeze(2).broadcast_to([P, RF, NB])))
            for dst, f0, nf, done in ((xl, 12, 2, q["mixed_lora"]), (k, 4, 4, None), (r, 0, 4, None), (v, 8, 4, q["mixed_rkv"])):
                V.tensor_sub(dst[:, :, 0:SEQ], m.pp[:, f0:f0 + nf, 0:SEQ], m.pp[:, f0:f0 + nf, 1:SEQ + 1]).then_inc(q["own"], 1)
                n_own[0] += 1
                V.tensor_add(dst[:, :, SEQ:TOK], sh[:, f0:f0 + nf, :], cur_s[:, f0:f0 + nf, :]).then_inc(q["own"], 1)
                n_own[0] += 1
                dve.wait_ge(q["own"], n_own[0])
                for f in range(nf):
                    last = V.scalar_tensor_tensor(dst[:, f, 0:SEQ], dst[:, f, 0:SEQ], par[:, MU + f0 + f:MU + f0 + f + 1],
                                                  m.pp[:, f0 + f, 1:SEQ + 1], ALU.mult, ALU.add)
                if done is None:
                    link(last)
                else:
                    last.then_inc(done, 1)
            dve.wait_ge(q["mixed_rkv"], 1)
            dve.wait_ge(q["lora_mm"], 3 * PAIRS)
            for h in range(PAIRS):
                last = V.tensor_scalar(kk[:, h, :], k[:, h, :], par[:, KK_ + h:KK_ + h + 1], None, ALU.mult)
            link(last)
            V.tensor_mul(tmp_a, kk, kk).then_inc(q["kk_sq"], 1)
            dve.wait_ge(q["gates_done"], 2 * PAIRS)
            dve.wait_ge(q["ones_in"], 48)
            for h in range(PAIRS):
                V.tensor_tensor_scan(cum[:, h, 0:SEQ], restart, sw[:, h, 0:SEQ], 0.0, ALU.mult, ALU.add).then_inc(q["scanned"], 1)
            dve.wait_ge(q["kk_norm"], PAIRS)
            link(V.tensor_scalar(tmp_b, tmp_b, 1e-12, None, ALU.max))
            link(V.reciprocal(tmp_b, tmp_b))
            V.tensor_mul(kk, kk, tmp_b).then_inc(q["kk_done"], 1)
            dve.wait_ge(q["params_done"], 1)
            for h in range(PAIRS):
                last = V.tensor_scalar(tmp_a[:, h, :], ga[:, h, :], par[:, KA + h:KA + h + 1], ka1[:, h:h + 1], ALU.mult, ALU.add)
            link(last)
            link(V.tensor_mul(k, k, tmp_a))
            dve.wait_ge(q["kk_done"], 1)
            V.tensor_mul(ga, kk, ga).then_inc(q["keys_done"], 1)
            for h in range(PAIRS):
                last = V.scalar_tensor_tensor(tmp_a[:, h, :], r[:, h, :], par[:, RK + h:RK + h + 1], k[:, h, :], ALU.mult, ALU.mult)
            last.then_inc(q["bonus_in"], 1)
            dve.wait_ge(q["exp_p"], 1)
            by_tile = lambda x: x[:, :, 0:SEQ].rearrange("p h (t c) -> p h t c", t=NT)
            for h in range(PAIRS):
                last = V.tensor_mul(ar[:, h, :, 1, :], by_tile(r)[:, h], by_tile(tmp_b)[:, h])
            last.then_inc(q["ar_r"], 1)
            V.tensor_copy(pend, tmp_b[:, :, CHUNK - 1:SEQ:CHUNK])
            dve.wait_ge(q["bonus_psum"], PAIRS)
            dve.wait_ge(q["sx_psum"], 6)
            dve.wait_ge(q["ar_r"], 1)
            for h in range(PAIRS):
                V.tensor_mul(r[:, h, cols[0]], m.bank[h][:, :], v[:, h, cols[0]])
                last = V.tensor_mul(r[:, h, cols[1]], m.bank[4 + h // 2][:, NB * (h % 2):NB * (h % 2) + NB], v[:, h, cols[1]])
            last.then_inc(q["bonus_done"], 1)
            dve.wait_ge(q["bonus_done"], 1)
            V.tensor_sub(tmp_a[:, :, 0:SEQ], cum[:, :, 0:SEQ], sw[:, :, 0:SEQ]).then_inc(q["pm_ready"], 1)
            dve.wait_ge(q["exp_pm"], 1)
            for h in range(PAIRS):
                last = V.scalar_tensor_tensor(ar[:, h, :, 0, :], by_tile(kk)[:, h], -1.0, by_tile(tmp_a)[:, h], ALU.mult, ALU.mult)
            last.then_inc(q["ar_a"], 1)
            dve.wait_ge(q["exp_m"], 1)
            dve.wait_ge(q["keys_done"], 1)
            V.tensor_mul(bt, ga[:, :, 0:SEQ], tmp_a[:, :, 0:SEQ])
            V.tensor_mul(kt, k[:, :, 0:SEQ], tmp_a[:, :, 0:SEQ]).then_inc(q["b_ready"], 1)
            dve.wait_ge(q["b_ready"], 1)
            ends = pend.unsqueeze(3).broadcast_to([P, PAIRS, SEQ // CHUNK, CHUNK])
            by_chunk = lambda x: x[:, :, 0:SEQ].rearrange("p h (c t) -> p h c t", t=CHUNK)
            for h in range(PAIRS):
                V.tensor_mul(by_chunk(tmp_b)[:, h], by_chunk(kt)[:, h], ends[:, h])
                last = V.tensor_mul(by_chunk(cum)[:, h], by_chunk(bt)[:, h], ends[:, h])
            last.then_inc(q["bar_ready"], 1)
            dve.wait_ge(q["s_ta"], 1)
            V.tensor_reduce(s_sa, s_tmp, AXX, ALU.add).then_inc(q["s_sa_done"], 1)
            dve.wait_ge(q["tok_done"], 4 * NT)
            nsc = nz = nx = 0
            low = m.levels[:, 0:LEVELS * P].rearrange("p (l c) -> p l c", l=LEVELS)
            up = m.levels[:, LEVELS * P:2 * LEVELS * P].rearrange("p (l c) -> p l c", l=LEVELS)
            four = lambda x: x.unsqueeze(1).broadcast_to([P, NT, P])
            for h in range(PAIRS):
                for s in range(2):
                    if h:
                        dve.wait_ge(q["u_mm"], 2 * h)
                    V.tensor_copy(x_inv[s], four(m.ident[:, :]))
                    V.tensor_copy(x_inv_t[s], four(m.ident[:, :])).then_inc(q["x_init"], 1)
                    for t in range(NT):
                        nsc += 1
                        u = (2 * h + s) * NT + t
                        dve.wait_ge(q["score_mm"], nsc)
                        src = m.bank[6 + nsc % 2][:, :].rearrange("p (x y c) -> p x y c", x=2, y=2)
                        V.tensor_mul(lm[s][:, t], src[:, :, 0, :], tri[:, 0, :].unsqueeze(1).broadcast_to([P, 2, P]))
                        V.tensor_mul(nn[:, u], src[:, :, 1, :], tri[:, 1, :].unsqueeze(1).broadcast_to([P, 2, P]))\
                            .then_inc(q["score_masked"], 1)
                for lev in range(LEVELS):
                    for s in range(2):
                        nx += 1
                        bank_of = lambda i: m.bank[3 * s + i][:, :].rearrange("p (t c) -> p t c", t=NT)
                        if lev == 0:
                            dve.wait_ge(q["x_init"], 2 * h + s + 1)
                            dve.wait_ge(q["score_masked"], 8 * h + 4 * s + 4)
                            dve.wait_ge(q["xz_mm"], nx)
                            V.copy_predicated(x_inv[s], four(low[:, 0, :]), bank_of(0)).then_inc(q["x_new"], 1)
                            V.copy_predicated(x_inv_t[s], four(up[:, 0, :]), lm[s][:, :, 0, :]).then_inc(q["xt_new"], 1)
                        else:
                            dve.wait_ge(q["xz_mm"], nx)
                            V.copy_predicated(x_inv[s], four(low[:, lev, :]), bank_of(1)).then_inc(q["x_new"], 1)
                            V.copy_predicated(x_inv_t[s], four(up[:, lev, :]), bank_of(2)).then_inc(q["xt_new"], 1)
            dve.wait_ge(q["u_copied"], 2 * PAIRS)
            dve.wait_ge(q["s_tr"], 1)
            V.tensor_reduce(s_y, s_tmp, AXX, ALU.add).then_inc(q["s_y_done"], 1)
            dve.wait_ge(q["score_mm"], 8 * PAIRS)
            V.memset(state, 0.0).then_inc(q["st_done"], 1)
            for c in range(SEQ // CHUNK):
                t, rows = c // 2, half(c % 2)
                for h in range(PAIRS):
                    i = c * PAIRS + h
                    dve.wait_ge(q["sa_mm"], i + 1)
                    if c >= 2:
                        dve.wait_ge(q["y_mm"], i + 1 - 2 * PAIRS)
                    V.tensor_add(sa[rows, c % 2, h], m.bank[4 + i % 2][rows, 0:2 * HD].rearrange("p (s d) -> p s d", s=2),
                                 u_tok[rows, t, h]).then_inc(q["sa_done"], 1)
                for h in range(PAIRS):
                    i = c * PAIRS + h
                    dve.wait_ge(q["st_mm"], i + 1)
                    if c >= 1:
                        dve.wait_ge(q["y_mm"], i + 1 - PAIRS)
                    dve.wait_ge(q["st_done"], 1 + i - (PAIRS - 1) if c else 1)
                    for s in range(2):
                        last = V.scalar_tensor_tensor(state[half(s), (c + 1) % 2, h, half(s)], state[half(s), c % 2, h, half(s)],
                                                      pend[half(s), h, c:c + 1], m.bank[6 + i % 2][half(s), half(s)],
                                                      ALU.mult, ALU.add)
                    last.then_inc(q["st_done"], 1)
            dve.wait_ge(q["state_psum"], 1)
            V.tensor_copy(tmp_a[:, 0, 0:AW], m.bank[7][:, :]).then_inc(q["state_rows_done"], 1)
            dve.wait_ge(q["y_copied"], 1)
            for h in range(PAIRS):
                dve.wait_ge(q["mean_mm"], PAIRS)
                for c, total in ((cols[0], m.bank[h][:, :]), (cols[1], m.bank[4][:, NB * h:NB * h + NB])):
                    last = V.scalar_tensor_tensor(ys[:, h, c], total, -1.0 / HD, ys[:, h, c], ALU.mult, ALU.add)
                last.then_inc(q["centred"], 1)
            dve.wait_ge(q["centred"], PAIRS)
            V.tensor_mul(y_sq, ys, ys).then_inc(q["squared"], 1)
            for h in range(PAIRS):
                dve.wait_ge(q["var_mm"], PAIRS)
                V.tensor_scalar(y_sq[:, h, cols[0]], m.bank[h][:, :], 1.0 / HD, GN_EPS, ALU.mult, ALU.add)
                last = V.tensor_scalar(y_sq[:, h, cols[1]], m.bank[5][:, NB * h:NB * h + NB], 1.0 / HD, GN_EPS,
                                       ALU.mult, ALU.add)
            link(last)
            V.reciprocal(y_sq, y_sq).then_inc(q["var_ready"], 1)
            dve.wait_ge(q["root_done"], 1)
            link(V.tensor_mul(ys, ys, y_sq))
            for h in range(PAIRS):
                last = V.tensor_scalar(ys[:, h, :], ys[:, h, :], par[:, LNW + h:LNW + h + 1], par[:, LNB + h:LNB + h + 1],
                                       ALU.mult, ALU.add)
            link(last)
            link(V.tensor_add(ys, ys, r))
            V.tensor_mul(m.ct[:, 4:8, :], ys, g)

        @block.tensor
        def _(pe):
            T = nc.tensor
            pe.wait_ge(q["tables_in"], 16 * 8)
            pe.wait_ge(q["state_in"], 16)
            T.transpose(m.bank[0][:, 0:N_PAR], par_rows, m.ident[0:N_PAR, 0:N_PAR])
            for f in range(RF):
                last = T.transpose(m.bank[1][:, f * NB:(f + 1) * NB], sh_rows[:, f * P:(f + 1) * P], m.ident[0:NB, 0:NB])
            last.then_inc(q["params_psum"], 1)
            pe.wait_ge(q["lora_in"], 48)
            pe.wait_ge(q["lora_act"], 2)
            pe.wait_ge(q["params_done"], 1)
            for y in range(3):
                for h in range(PAIRS):
                    i = y * PAIRS + h
                    if i >= 2:
                        pe.wait_ge(q["gates_done"], max(i - 5, i - 1))
                    rows = (slice(0, HD), slice(HD, P), slice(0, P))[y]
                    wts = (lora_wa if y < 2 else lora_g)[rows, h * P:(h + 1) * P]
                    T.matmul(m.bank[i % 6][:, :], wts, xl[rows, y // 2, cols[0]], start=True, stop=True)
                    T.matmul(m.bank[6 + i % 2][:, 0:NB], wts, xl[rows, y // 2, cols[1]], start=True, stop=True).then_inc(q["lora_mm"], 1)
            pe.wait_ge(q["ones_in"], 48)
            pe.wait_ge(q["kk_sq"], 1)
            pe.wait_ge(q["gates_done"], 3 * PAIRS)
            for h in range(PAIRS):
                T.matmul(m.bank[h][:, :], ones_blk, tmp_a[:, h, cols[0]], start=True, stop=True)
                T.matmul(m.bank[4 + h][:, 0:NB], ones_blk, tmp_a[:, h, cols[1]], start=True, stop=True).then_inc(q["kk_sum"], 1)
            pe.wait_ge(q["keys_done"], 1)
            pe.wait_ge(q["kk_norm"], PAIRS)
            for i, src in enumerate((r, k, kk, ga, sw, v)):
                for h in range(PAIRS):
                    last = T.transpose(m.bank[i][0:NB, h * P:(h + 1) * P], src[:, h, cols[1]], m.ident[:, :])
                last.then_inc(q["sx_psum"], 1)
            pe.wait_ge(q["bonus_in"], 1)
            pe.wait_ge(q["sx_done"], 6)
            for h in range(PAIRS):
                T.matmul(m.bank[h][:, :], ones_blk, tmp_a[:, h, cols[0]], start=True, stop=True)
                T.matmul(m.bank[4 + h // 2][:, NB * (h % 2):NB * (h % 2) + NB], ones_blk, tmp_a[:, h, cols[1]],
                         start=True, stop=True).then_inc(q["bonus_psum"], 1)
            pe.wait_ge(q["bonus_done"], 1)
            for i in range(4):
                if i == 1:
                    pe.wait_ge(q["ar_a"], 1)
                if i == 2:
                    pe.wait_ge(q["bar_ready"], 1)
                for t in range(NT):
                    n = i * NT + t
                    if n >= 6:
                        pe.wait_ge(q["tok_done"], n - 5)
                    for h in range(PAIRS):
                        src = (v[:, h, t * P:(t + 1) * P], ar[:, h, t, 0, :], tmp_b[:, h, t * P:(t + 1) * P],
                               cum[:, h, t * P:(t + 1) * P])[i]
                        last = T.transpose(m.bank[n % 6][:, h * P:(h + 1) * P], src, m.ident[:, :])
                    last.then_inc(q["tok_psum"], 1)
            pe.wait_ge(q["tok_done"], 4 * NT)
            nsc = nz = nx = 0
            for h in range(PAIRS):
                if h:
                    pe.wait_ge(q["u_copied"], 2 * h)
                for s in range(2):
                    for t in range(NT):
                        nsc += 1
                        if nsc >= 3:
                            pe.wait_ge(q["score_masked"], nsc - 2)
                        bank = m.bank[6 + nsc % 2]
                        rhs = ar[half(s), h, t].rearrange("p x c -> p (x c)")
                        T.matmul(bank[:, 0:2 * P], bt[half(s), h, t * P:(t + 1) * P], rhs, start=True, stop=True)
                        T.matmul(bank[:, 2 * P:4 * P], kt[half(s), h, t * P:(t + 1) * P], rhs, start=True, stop=True)\
                            .then_inc(q["score_mm"], 1)
                for lev in range(LEVELS):
                    if lev == 0:
                        for s in range(2):
                            nx += 1
                            pe.wait_ge(q["score_masked"], 8 * h + 4 * s + 4)
                            for t in range(NT):
                                last = T.matmul(m.bank[3 * s][:, t * P:(t + 1) * P], lm[s][:, t, 0, :], m.ident[:, :],
                                                start=True, stop=True)
                            last.then_inc(q["xz_mm"], 1)
                        continue
                    for s in range(2):
                        pe.wait_ge(q["x_new"], nx - 1 + s)
                        pe.wait_ge(q["xt_new"], nx - 1 + s)
                        for t in range(NT):
                            last = T.matmul(m.bank[3 * s][:, t * P:(t + 1) * P], lm[s][:, t, 0, :], x_inv[s][:, t, :],
                                            start=True, stop=True)
                        last.then_inc(q["z_mm"], 1)
                    for s in range(2):
                        nz += 1
                        nx += 1
                        pe.wait_ge(q["z_copied"], nz)
                        for t in range(NT):
                            T.matmul(m.bank[3 * s + 1][:, t * P:(t + 1) * P], x_inv_t[s][:, t, :], z[s][:, t, :],
                                     start=True, stop=True)
                            last = T.matmul(m.bank[3 * s + 2][:, t * P:(t + 1) * P], z[s][:, t, :], x_inv_t[s][:, t, :],
                                            start=True, stop=True)
                        last.then_inc(q["xz_mm"], 1)
                for s in range(2):
                    i = 2 * h + s
                    pe.wait_ge(q["xt_new"], LEVELS * 2 * h + 2 * (LEVELS - 1) + s + 1)
                    for t in range(NT):
                        last = T.matmul(m.bank[3 * s][:, t * HD:(t + 1) * HD], lm[s][:, t, 1, :],
                                        v_tok[:, t, h * P + s * HD:h * P + (s + 1) * HD], start=True, stop=True)
                    last.then_inc(q["mv_mm"], 1)
                    for t in range(NT):
                        last = T.matmul(m.bank[3 * s + 1][half(s), t * P:(t + 1) * P],
                                        a_tok[:, t, h * P + s * HD:h * P + (s + 1) * HD], x_inv_t[s][:, t, :],
                                        start=True, stop=True)
                    last.then_inc(q["wt_mm"], 1)
                for s in range(2):
                    i = 2 * h + s
                    pe.wait_ge(q["mv_copied"], i + 1)
                    for t in range(NT):
                        last = T.matmul(m.bank[3 * s + 2][:, t * HD:(t + 1) * HD], x_inv_t[s][:, t, :], mv[s][:, t, :],
                                        start=True, stop=True)
                    last.then_inc(q["u_mm"], 1)
            pe.wait_ge(q["u_copied"], 2 * PAIRS)
            pe.wait_ge(q["score_masked"], 8 * PAIRS)
            for c in range(SEQ // CHUNK):
                t, rows = c // 2, half(c % 2)
                tc = slice(c * CHUNK, (c + 1) * CHUNK)
                for h in range(PAIRS):
                    i = c * PAIRS + h
                    pe.wait_ge(q["st_done"], 1 + max(0, i - PAIRS + 1) if c else 1)
                    if i >= 2:
                        pe.wait_ge(q["sa_done"], i - 1)
                    T.matmul(m.bank[4 + i % 2][rows, 0:P], wt[:, h, tc], state[:, c % 2, h, :], start=True,
                             stop=True).then_inc(q["sa_mm"], 1)
                for h in range(PAIRS):
                    i = c * PAIRS + h
                    pe.wait_ge(q["sa_done"], i + 1)
                    if i >= 2:
                        pe.wait_ge(q["st_done"], i)
                    both = slice(h * P, (h + 1) * P)
                    T.matmul(m.bank[6 + i % 2][:, 0:P], b_tok[rows, t, both], sa[rows, c % 2, h].rearrange("p s d -> p (s d)"),
                             start=True, stop=False)
                    T.matmul(m.bank[6 + i % 2][:, 0:P], k_tok[rows, t, both], v_tok[rows, t, both],
                             start=False, stop=True).then_inc(q["st_mm"], 1)
                    qc = half(c % 2)
                    T.matmul(m.bank[h][:, tc], state[:, c % 2, h, :], ar[:, h, t, 1, qc], start=True, stop=False)
                    for s in range(2):
                        fs = slice(h * P + s * HD, h * P + (s + 1) * HD)
                        u = (2 * h + s) * NT + t
                        out = m.bank[h][half(s), tc]
                        T.matmul(out, sa[rows, c % 2, h, s, :], nn[rows, u, 0, qc], start=False, stop=False)
                        last = T.matmul(out, v_tok[rows, t, fs], nn[rows, u, 1, qc], start=False, stop=True)
                    last.then_inc(q["y_mm"], 1)
            pe.wait_ge(q["st_done"], 1 + 8 * PAIRS)
            for h in range(PAIRS):
                last = T.transpose(m.bank[7][:, h * P:(h + 1) * P], state[:, 0, h, :], m.ident[:, :])
            last.then_inc(q["state_psum"], 1)
            pe.wait_ge(q["s_y_in"], 16)
            for h in range(PAIRS):
                last = T.transpose(m.bank[6][:, h * NB:(h + 1) * NB], y_rows[:, h * P:(h + 1) * P], m.ident[0:NB, 0:NB])
            last.then_inc(q["s_y_psum"], 1)
            pe.wait_ge(q["y_copied"], 1)
            for src, done, ready, b5 in ((ys, q["mean_mm"], None, 4), (y_sq, q["var_mm"], q["squared"], 5)):
                if ready is not None:
                    pe.wait_ge(ready, 1)
                for h in range(PAIRS):
                    T.matmul(m.bank[h][:, :], ones_blk, src[:, h, cols[0]], start=True, stop=True)
                    T.matmul(m.bank[b5][:, NB * h:NB * h + NB], ones_blk, src[:, h, cols[1]], start=True,
                             stop=True).then_inc(done, 1)


BLK = P
MORE = (TOK * TOPK - 1) // BLK
BLOCKS = EXPERTS + MORE
GUP = 3


def mix_and_route(nc, io, m):
    with ExitStack() as ctx:
        sem = lambda n: m.sem("mr_" + n)
        w = Arena(m.wring)
        w.at = 2 * SLOT
        b_raw = w.take(3 * D, rows=EXPERTS)
        b_rest = w.take(3 * D, rows=EXPERTS)
        b_part = [w.take(3 * D // 2, rows=EXPERTS).bitcast(BF16) for _ in range(GUP)]
        zero_rows = w.take(D)
        a = Arena(m.arena)
        a.at = m.x2_at + (NT + 1) * D
        row_p = a.take(3, D)
        row_s = a.take(3, D, rows=NB)
        xin = a.take(2, D)
        h2 = a.take(2, D)
        h2t = a.take(KT, P)
        rw = a.take(KT, EXPERTS)
        rb = a.take(EXPERTS)
        lg = a.take(EXPERTS)
        route = a.take(EXPERTS + MORE + NT + 1)
        tri = a.take(P)
        ones = a.take(P)
        hot = a.take((NT + 1) * TOPK, EXPERTS)
        chosen = a.take(NT + 1, EXPERTS)
        rank = a.take(NT + 1, EXPERTS)
        slot_of = a.take(NT + 1, EXPERTS)
        prod = a.take((NT + 1) * TOPK, EXPERTS)
        over = a.take(6, EXPERTS)
        ocmp = a.take(MORE, EXPERTS)
        top8 = a.take(8)
        idx8 = a.take(8).bitcast(mybir.dt.uint32)
        idxf = a.take(TOPK)
        slotf = a.take((NT + 1) * TOPK)
        oexpf = a.take(MORE)
        ss = a.take(NT + 1)
        rstd = a.take(NT + 1)
        ntop = a.take(1)
        zeros = a.take(P, rows=BLOCKS + 1)
        tab = a.take(P, rows=BLOCKS + 1)
        names = ("rows_in consts_in wout_in0 wout_in1 bias_in out_mm x2_done squared ms_done root_done h2_done h2_out "
                 "h2t_psum h2t_copied logit_mm logit_read top_done exp_done chosen_done rank_mm rank_read count_mm slots_done "
                 "own zero_set zero_out rows_zero scattered tab_in tab_psum idx_done b_hi b_mid b_r1 b_r2 b_lo b_out ones_set").split()
        q = dict({n: sem(n) for n in names if n not in ("scattered", "h2_out")}, scattered=m.scattered,
                 h2_out=[sem(f"h2_out{i}") for i in range(2)])
        x_in = [sem(f"x_in{i}") for i in range(2)]
        e_of, ob_of, tok_of = route[:, 0:EXPERTS], route[:, EXPERTS:EXPERTS + MORE], route[:, EXPERTS + MORE:]
        block = ctx.enter_context(nc.Block())

        @block.sync
        def _(sp):
            def h2_rows_out(t):
                r = rows_of(t)
                sp.wait_ge(q["h2_done"], t + 1)
                sp.dma_start(m.h2_dram[t * P:t * P + r, :], h2[0:r, t % 2, :]).then_inc(q["h2_out"][t % 2], 16)

            for j, landed in enumerate((q["wout_in0"], q["wout_in1"])):
                sp.dma_start(slot_view(m.wring, j), wide(io["w_out"][0], j * 512)).then_inc(landed, 16)
            for i, part in enumerate((2, 3, 4)):
                row = m.mod_dram[NB:NB + 1, part * D:(part + 1) * D]
                sp.dma_start(row_p[:, i, :], row.broadcast_to([P, D])).then_inc(q["rows_in"], 16)
                sp.dma_start(row_s[:, i, :], m.mod_dram[0:NB, part * D:(part + 1) * D]).then_inc(q["rows_in"], 16)
            sp.dma_start(b_raw[:, 0:2 * D], io["moe_b_gu"][0]).then_inc(q["bias_in"], 16)
            sp.dma_start(b_raw[:, 2 * D:], io["moe_b_down"][0]).then_inc(q["bias_in"], 16)
            sp.wait_ge(q["zero_set"], 2)
            sp.dma_start(m.tab_dram.rearrange("(b p) o -> b (p o)", p=P), zeros).then_inc(q["zero_out"], 16)
            sp.dma_start(m.y_dram[EXPERTS * BLK:, :].rearrange("(b p) n -> p b n", p=P),
                         zero_rows.unsqueeze(1).broadcast_to([P, MORE, D])).then_inc(q["rows_zero"], 16)
            for t in range(NT + 1):
                r = rows_of(t)
                if t >= 2:
                    sp.wait_ge(q["x2_done"], 2 * (t - 1))
                src = io["x_prompt"][0, t * P:(t + 1) * P, :] if t < NT else io["x_sample"][:, 0, :]
                sp.dma_start(xin[0:r, t % 2, :], src).then_inc(x_in[t % 2], 16)
                if t >= 2:
                    h2_rows_out(t - 2)
            h2_rows_out(NT - 1)
            h2_rows_out(NT)
            sp.wait_ge(q["b_lo"], 1)
            for i in range(GUP):
                sp.dma_start(m.bias_dram[:, i, :], b_part[i]).then_inc(q["b_out"], 16)
            sp.wait_ge(q["scattered"], 16 * (NT + 1) * TOPK)
            sp.dma_start(tab, m.tab_dram.rearrange("(b p) o -> b (p o)", p=P)).then_inc(q["tab_in"], 16)
            sp.wait_ge(q["rows_zero"], 16)
            sp.wait_ge(q["b_out"], 16 * GUP)
            for i in range(2):
                sp.wait_ge(q["h2_out"][i], 16 * ((NT + 2 - i) // 2))

        @block.gpsimd
        def _(pool):
            nc.gpsimd.memset(zero_rows, 0.0).then_inc(q["zero_set"], 1)
            nc.gpsimd.memset(zeros, 0.0).then_inc(q["zero_set"], 1)
            nc.gpsimd.memset(ones, 1.0).then_inc(q["ones_set"], 1)
            pool.wait_ge(q["b_hi"], 1)
            nc.gpsimd.tensor_tensor(b_rest, b_raw, b_part[0], ALU.subtract).then_inc(q["b_r1"], 1)
            pool.wait_ge(q["b_mid"], 1)
            nc.gpsimd.tensor_tensor(b_raw, b_rest, b_part[1], ALU.subtract).then_inc(q["b_r2"], 1)
            pool.wait_ge(q["zero_out"], 16)
            pool.wait_ge(q["slots_done"], 1)
            for t in range(NT + 1):
                r = rows_of(t)
                for c in range(TOPK):
                    i = t * TOPK + c
                    nc.gpsimd.indirect_dma_start(out=m.tab_dram, out_offset=bass.IndirectOffsetOnAxis(ap=m.slots[0:r, i:i + 1], axis=0),
                                                 in_=tok_of[0:r, t:t + 1], in_offset=None).then_inc(q["scattered"], 16)

        @block.scalar
        def _(act):
            act.dma_start(rw, io["router_w"][0].rearrange("(k p) e -> p k e", p=P)).then_inc(q["consts_in"], 16)
            act.dma_start(rb, io["router_b"].broadcast_to([P, EXPERTS])).then_inc(q["consts_in"], 16)
            act.dma_start(route, io["route"]).then_inc(q["consts_in"], 16)
            act.dma_start(tri, io["rank_tri"]).then_inc(q["consts_in"], 16)
            act.wait_ge(q["bias_in"], 32)
            nc.scalar.copy(b_part[0], b_raw).then_inc(q["b_hi"], 1)
            act.wait_ge(q["b_r1"], 1)
            nc.scalar.copy(b_part[1], b_rest).then_inc(q["b_mid"], 1)
            act.wait_ge(q["b_r2"], 1)
            nc.scalar.copy(b_part[2], b_raw).then_inc(q["b_lo"], 1)
            for t in range(NT + 1):
                r = rows_of(t)
                act.wait_ge(q["x2_done"], 2 * (t + 1))
                if t >= 2:
                    act.wait_ge(q["h2_out"][t % 2], 16 * (t // 2))
                    act.wait_ge(q["h2t_psum"], t - 1)
                nc.scalar.activation(h2[0:r, t % 2, :], m.x2[0:r, t, :], ACT.Square, accum_out=ss[0:r, t:t + 1]).then_inc(q["squared"], 1)
                act.wait_ge(q["ms_done"], t + 1)
                nc.scalar.activation(rstd[0:r, t:t + 1], rstd[0:r, t:t + 1], ACT.Sqrt).then_inc(q["root_done"], 1)
                act.wait_ge(q["h2t_psum"], t + 1)
                for half in range(2):
                    last = nc.scalar.copy(h2t[:, 4 * half:4 * half + 4, 0:r],
                                          m.bank[4 + half][:, 0:4 * r].rearrange("p (k c) -> p k c", k=4))
                last.then_inc(q["h2t_copied"], 1)
                act.wait_ge(q["top_done"], t + 1)
                nc.scalar.activation(m.weights[0:r, t * TOPK:(t + 1) * TOPK], top8[0:r, 0:TOPK], ACT.Exp,
                                     bias=ntop[0:r, :], accum_out=ss[0:r, t:t + 1]).then_inc(q["exp_done"], 1)
            act.wait_ge(q["tab_psum"], 1)
            nc.scalar.copy(m.gather_idx[:, :], m.bank[0][:, 0:BLOCKS + 1]).then_inc(q["idx_done"], 1)

        @block.vector
        def _(dve):
            n_own = [0]

            def link(ins):
                n_own[0] += 1
                ins.then_inc(q["own"], 1)
                dve.wait_ge(q["own"], n_own[0])

            V = nc.vector
            link(V.memset(hot, 0.0))
            link(V.memset(rank, 0.0))
            link(V.memset(m.weights[:, :], 0.0))
            dve.wait_ge(q["rows_in"], 96)
            dve.wait_ge(q["consts_in"], 64)

            def rows_for(t):
                return row_p if t < NT else row_s

            def x2_tile(t):
                r = rows_of(t)
                for n in range(2):
                    c = slice(n * 512, (n + 1) * 512)
                    dve.wait_ge(q["out_mm"], 2 * t + n + 1)
                    link(V.tensor_mul(m.x2[0:r, t, c], m.bank[(2 * t + n) % 4][0:r, :], rows_for(t)[0:r, 0, c]))
                    dve.wait_ge(x_in[t % 2], 16 * (t // 2 + 1))
                    V.tensor_add(m.x2[0:r, t, c], m.x2[0:r, t, c], xin[0:r, t % 2, c]).then_inc(q["x2_done"], 1)

            def norm_tile(t):
                r = rows_of(t)
                rows = rows_for(t)
                dve.wait_ge(q["squared"], t + 1)
                link(V.tensor_scalar(rstd[0:r, t:t + 1], ss[0:r, t:t + 1], 1.0 / D, NORM_EPS, ALU.mult, ALU.add))
                V.reciprocal(rstd[0:r, t:t + 1], rstd[0:r, t:t + 1]).then_inc(q["ms_done"], 1)
                dve.wait_ge(q["root_done"], t + 1)
                link(V.scalar_tensor_tensor(h2[0:r, t % 2, :], m.x2[0:r, t, :], rstd[0:r, t:t + 1], rows[0:r, 2, :],
                                            ALU.mult, ALU.mult))
                V.tensor_add(h2[0:r, t % 2, :], h2[0:r, t % 2, :], rows[0:r, 1, :]).then_inc(q["h2_done"], 1)

            def rank_tile(t):
                r = rows_of(t)
                dve.wait_ge(q["rank_mm"], t + 1)
                V.tensor_copy(rank[0:r, t, :], m.bank[7][0:r, 0:EXPERTS]).then_inc(q["rank_read"], 1)

            x2_tile(0)
            for t in range(NT + 1):
                r = rows_of(t)
                norm_tile(t)
                if t < NT:
                    x2_tile(t + 1)
                dve.wait_ge(q["logit_mm"], t + 1)
                link(V.tensor_add(lg[0:r, :], m.bank[6][0:r, 0:EXPERTS], rb[0:r, :]))
                if t:
                    dve.wait_ge(q["exp_done"], t)
                link(V.max(top8[0:r, :], lg[0:r, :]))
                link(V.max_index(idx8[0:r, :], top8[0:r, :], lg[0:r, :]))
                V.tensor_scalar(ntop[0:r, :], top8[0:r, 0:1], -1.0, None, ALU.mult).then_inc(q["top_done"], 1)
                link(V.tensor_copy(idxf[0:r, :], idx8[0:r, 0:TOPK]))
                mine = hot[0:r, t * TOPK:(t + 1) * TOPK, :]
                link(V.tensor_tensor(mine, e_of[0:r, :].unsqueeze(1).broadcast_to([r, TOPK, EXPERTS]),
                                     idxf[0:r, :].unsqueeze(2).broadcast_to([r, TOPK, EXPERTS]), ALU.is_equal))
                V.tensor_reduce(chosen[0:r, t, :], mine.rearrange("p c e -> p e c"), AXX, ALU.add).then_inc(q["chosen_done"], 1)
                dve.wait_ge(q["exp_done"], t + 1)
                link(V.reciprocal(ss[0:r, t:t + 1], ss[0:r, t:t + 1]))
                wt = m.weights[0:r, t * TOPK:(t + 1) * TOPK]
                link(V.tensor_scalar(wt, wt, ss[0:r, t:t + 1], None, ALU.mult))
                if t:
                    rank_tile(t - 1)
            rank_tile(NT)
            dve.wait_ge(q["rank_read"], NT + 1)
            dve.wait_ge(q["count_mm"], 1)
            link(V.tensor_copy(over[:, 0, :], m.bank[6][:, 0:EXPERTS]))
            link(V.tensor_scalar(over[:, 1, :], over[:, 0, :], float(BLK), None, ALU.is_gt))
            for j in range(2, TOK // BLK + 1):
                link(V.scalar_tensor_tensor(over[:, 1, :], over[:, 0, :], float(BLK * j), over[:, 1, :], ALU.is_gt, ALU.add))
            link(V.tensor_tensor_scan(over[:, 2, :], ones[:, 0:EXPERTS], over[:, 1, :], 0.0, ALU.mult, ALU.add))
            link(V.tensor_sub(over[:, 3, :], over[:, 2, :], over[:, 1, :]))
            link(V.tensor_sub(over[:, 3, :], over[:, 3, :], e_of))
            link(V.tensor_scalar(over[:, 3, :], over[:, 3, :], float(EXPERTS - 1), float(BLK), ALU.add, ALU.mult))
            link(V.tensor_scalar(over[:, 4, :], e_of, float(BLK), None, ALU.mult))
            per_tile = lambda x: x.unsqueeze(1).broadcast_to([P, NT + 1, EXPERTS])
            link(V.scalar_tensor_tensor(slot_of, rank, float(BLK), per_tile(over[:, 3, :]), ALU.is_ge, ALU.mult))
            link(V.tensor_add(slot_of, slot_of, rank))
            link(V.tensor_add(slot_of, slot_of, per_tile(over[:, 4, :])))
            link(V.tensor_mul(prod.rearrange("p (t c) e -> p t c e", c=TOPK), hot.rearrange("p (t c) e -> p t c e", c=TOPK),
                              slot_of.unsqueeze(2).broadcast_to([P, NT + 1, TOPK, EXPERTS])))
            link(V.tensor_reduce(slotf, prod, AXX, ALU.add))
            V.tensor_copy(m.slots[:, :], slotf).then_inc(q["slots_done"], 1)
            link(V.tensor_tensor(ocmp, over[:, 2, :].unsqueeze(1).broadcast_to([P, MORE, EXPERTS]),
                                 ob_of.unsqueeze(2).broadcast_to([P, MORE, EXPERTS]), ALU.is_le))
            link(V.tensor_reduce(oexpf, ocmp, AXX, ALU.add))
            link(V.tensor_scalar(oexpf, oexpf, float(EXPERTS - 1), None, ALU.min))
            link(V.tensor_copy(m.more_expert[:, 0:MORE], oexpf))
            link(V.tensor_copy(m.more_expert[:, MORE:MORE + 1], over[:, 2, EXPERTS - 1:EXPERTS]))

        @block.tensor
        def _(pe):
            T = nc.tensor

            def out_tile(t):
                r = rows_of(t)
                for n in range(2):
                    i = 2 * t + n
                    pe.wait_ge((q["wout_in0"], q["wout_in1"])[n], 16)
                    if i >= 4:
                        pe.wait_ge(q["x2_done"], i - 3)
                    for k in range(KT):
                        last = T.matmul(m.bank[i % 4][0:r, :], m.ct[:, k, cols_of(t)], slot_view(m.wring, n)[:, k, :],
                                        start=(k == 0), stop=(k == KT - 1))
                    last.then_inc(q["out_mm"], 1)

            def logits_tile(t):
                r = rows_of(t)
                pe.wait_ge(q["h2_done"], t + 1)
                if t:
                    pe.wait_ge(q["h2t_copied"], t)
                for k in range(KT):
                    last = T.transpose(m.bank[4 + k // 4][:, (k % 4) * r:(k % 4 + 1) * r], h2[0:r, t % 2, k * P:(k + 1) * P],
                                       m.ident[0:r, 0:r])
                last.then_inc(q["h2t_psum"], 1)
                pe.wait_ge(q["h2t_copied"], t + 1)
                for k in range(KT):
                    last = T.matmul(m.bank[6][0:r, 0:EXPERTS], h2t[:, k, 0:r], rw[:, k, :], start=(k == 0), stop=(k == KT - 1))
                last.then_inc(q["logit_mm"], 1)

            def rank_tile(t):
                r = rows_of(t)
                pe.wait_ge(q["chosen_done"], t + 1)
                if t:
                    pe.wait_ge(q["rank_read"], t)
                for j in range(t):
                    T.matmul(m.bank[7][0:r, 0:EXPERTS], ones[:, 0:r], chosen[:, j, :], start=(j == 0), stop=False)
                T.matmul(m.bank[7][0:r, 0:EXPERTS], tri[0:r, 0:r], chosen[0:r, t, :], start=(t == 0), stop=True)\
                    .then_inc(q["rank_mm"], 1)

            out_tile(0)
            pe.wait_ge(q["consts_in"], 64)
            pe.wait_ge(q["ones_set"], 1)
            for t in range(NT + 1):
                if t < NT:
                    out_tile(t + 1)
                logits_tile(t)
                if t:
                    rank_tile(t - 1)
            rank_tile(NT)
            for j in range(NT + 1):
                r = rows_of(j)
                last = T.matmul(m.bank[6][:, 0:EXPERTS], ones[0:r, :], chosen[0:r, j, :], start=(j == 0), stop=(j == NT))
            last.then_inc(q["count_mm"], 1)
            pe.wait_ge(q["tab_in"], 16)
            pe.wait_ge(q["x2_done"], 2 * (NT + 1))
            T.transpose(m.bank[0][:, 0:BLOCKS + 1], tab, m.ident[0:BLOCKS + 1, 0:BLOCKS + 1]).then_inc(q["tab_psum"], 1)


def experts(nc, io, m):
    LIMIT, ALPHA = 7.0, 1.702
    with ExitStack() as ctx:
        sem = lambda n: m.sem("ex_" + n)
        a = Arena(m.arena)
        a.at = m.x2_at + (NT + 1) * D
        xg = a.take(D)
        xt = a.take(KT, P)
        gate = a.take(2, 512)
        up = a.take(2, 512)
        sig = a.take(2, 512)
        acts = a.take(2, 512)
        acts_t = a.take(KT, P)
        y = a.take(D)
        idx = a.take(1).bitcast(I32)
        turn = a.take(1)
        bias = a.take(3 * D // 2, rows=GUP).bitcast(BF16)
        ones3 = a.take(P // 2, rows=GUP).bitcast(BF16)
        names = ("bias_in bias_free ones_set idx_copied xg_in xg_free xt_psum_a xt_psum_b xt_copied_a xt_copied_b gu_free0 "
                 "gu_free1 gu_mm gate_done sig_done prod_done up_done act_done actt_psum actt_copied y_free y_mm y_copied y_out").split()
        q = dict({n: sem(n) for n in names if n != "xg_in"}, xg_in=m.xg_in)
        gu_free = (q["gu_free0"], q["gu_free1"])
        piece_in = [sem(f"piece_in{j}") for j in range(NSLOT)]
        piece_free = [sem(f"piece_free{j}") for j in range(NSLOT)]
        gu_dram = io["moe_w_gu"][0].rearrange("e (k p) (g n) -> e p k g n", p=P, g=2)
        down_dram = io["moe_w_down"][0].rearrange("e (k p) n -> e p k n", p=P)
        gu_slot = lambda j: m.wring[:, j * SLOT:(j + 1) * SLOT].rearrange("p (k g n) -> p k g n", k=4, g=2)
        down_slot = lambda j: m.wring[:, j * SLOT:(j + 1) * SLOT].rearrange("p (k n) -> p k n", k=4)
        block = ctx.enter_context(nc.Block())

        def all_blocks(engine, body):
            with engine.Fori(0, EXPERTS) as b:
                body(b, False)
            more = engine.value_load(m.more_expert[0:1, MORE:MORE + 1], min_val=0, max_val=MORE)
            with engine.If(more > 0):
                with engine.Fori(EXPERTS, BLOCKS) as b:
                    body(b, True)

        @block.sync
        def _(sp):
            def body(b, further):
                e = b
                if further:
                    e = sp.value_load(m.more_expert[0:1, bass.ds(b - EXPERTS, 1)], min_val=0, max_val=EXPERTS - 1)
                sp.wait_ge(q["bias_free"], b + 1)
                sp.dma_start(bias, m.bias_dram[bass.ds(e, 1), :, :].rearrange("e i n -> (e i) n")).then_inc(q["bias_in"], 16)
                for j in range(NSLOT):
                    sp.wait_ge(piece_free[j], b + 1)
                    if j < 4:
                        c, kh = j // 2, j % 2
                        src = gu_dram[bass.ds(e, 1), :, 4 * kh:4 * kh + 4, :, c * 512:(c + 1) * 512]
                        for g in range(2):
                            sp.dma_start(gu_slot(j)[:, :, g, :], src[:, :, :, g, :].rearrange("e p k n -> (e p) k n"))\
                                .then_inc(piece_in[j], 16)
                    else:
                        kh = j - 4
                        src = down_dram[bass.ds(e, 1), :, 4 * kh:4 * kh + 4, :]
                        sp.dma_start(down_slot(j), src.rearrange("e p k n -> (e p) k n")).then_inc(piece_in[j], 16)

            all_blocks(sp, body)

        @block.gpsimd
        def _(pool):
            nc.gpsimd.memset(ones3, 1.0).then_inc(q["ones_set"], 1)

            nc.gpsimd.memset(turn, 0.0).then_inc(q["ones_set"], 1)
            pool.wait_ge(q["ones_set"], 2)

            def gather(b):
                nc.gpsimd.tensor_copy(idx, m.gather_idx[:, bass.ds(b, 1)]).then_inc(q["idx_copied"], 1)
                pool.wait_ge(q["idx_copied"], b + 1)
                pool.wait_ge(q["xg_free"], b + 1)
                nc.gpsimd.tensor_tensor(turn, turn, turn, ALU.mult)
                nc.gpsimd.indirect_dma_start(out=xg, out_offset=None, in_=m.h2_dram,
                                             in_offset=bass.IndirectOffsetOnAxis(ap=idx, axis=0)).then_inc(q["xg_in"], 16)
                pool.wait_ge(q["xg_in"], 16 * (b + 1))

            gather(0)
            all_blocks(pool, lambda b, further: gather(b + 1))

        @block.scalar
        def _(act):
            def xt_half(i):
                nc.scalar.copy(xt[:, 4 * i:4 * i + 4, :].rearrange("p k c -> p (k c)"), m.bank[6 + i][:, :])\
                    .then_inc((q["xt_copied_a"], q["xt_copied_b"])[i], 1)

            def body(b, further):
                for c in range(2):
                    act.wait_ge(q["gate_done"], 2 * b + c + 1)
                    nc.scalar.activation(sig[:, c, :], gate[:, c, :], ACT.Sigmoid, scale=ALPHA).then_inc(q["sig_done"], 1)
                act.wait_ge(q["xt_psum_a"], b + 2)
                xt_half(0)
                act.wait_ge(q["y_mm"], b + 1)
                nc.scalar.copy(y[:, 0:512], m.bank[4][:, :])
                nc.scalar.copy(y[:, 512:], m.bank[5][:, :]).then_inc(q["y_copied"], 1)
                act.wait_ge(q["y_copied"], b + 1)
                act.sem_inc(q["y_free"], 1)
                act.dma_start(m.y_dram[bass.ds(b * BLK, BLK), :], y).then_inc(q["y_out"], 16)
                act.wait_ge(q["xt_psum_b"], b + 2)
                xt_half(1)
                act.wait_ge(q["y_out"], 16 * (b + 1))

            act.sem_inc(q["y_free"], 1)
            act.wait_ge(q["xt_psum_a"], 1)
            xt_half(0)
            act.wait_ge(q["xt_psum_b"], 1)
            xt_half(1)
            all_blocks(act, body)

        @block.vector
        def _(dve):
            def body(b, further):
                for c in range(2):
                    n = 2 * b + c + 1
                    dve.wait_ge(q["gu_mm"], n)
                    nc.vector.tensor_scalar(gate[:, c, :], m.bank[2 * c][:, :], LIMIT, None, ALU.min).then_inc(q["gate_done"], 1)
                    nc.vector.tensor_scalar(up[:, c, :], m.bank[2 * c + 1][:, :], LIMIT, -LIMIT, ALU.min, ALU.max)\
                        .then_inc(gu_free[c], 1)
                    dve.wait_ge(gu_free[c], b + 2)
                    dve.wait_ge(q["gate_done"], n)
                    nc.vector.scalar_tensor_tensor(up[:, c, :], up[:, c, :], 1.0, gate[:, c, :], ALU.add, ALU.mult)\
                        .then_inc(q["prod_done"], 1)
                    dve.wait_ge(q["prod_done"], n)
                    dve.wait_ge(q["sig_done"], n)
                    nc.vector.tensor_mul(acts[:, c, :], up[:, c, :], sig[:, c, :]).then_inc(q["act_done"], 1)
                    dve.wait_ge(q["actt_psum"], n)
                    nc.vector.tensor_copy(acts_t[:, 4 * c:4 * c + 4, :].rearrange("p k c -> p (k c)"), m.bank[6 + c][:, :])\
                        .then_inc(q["actt_copied"], 1)

            for f in gu_free:
                dve.sem_inc(f, 1)
            all_blocks(dve, body)

        @block.tensor
        def _(pe):
            T = nc.tensor

            def xt_half(i):
                for k in range(4 * i, 4 * i + 4):
                    last = T.transpose(m.bank[6 + i][:, (k % 4) * P:(k % 4 + 1) * P], xg[:, k * P:(k + 1) * P], m.ident[:, :])
                last.then_inc((q["xt_psum_a"], q["xt_psum_b"])[i], 1)

            def act_half(c):
                for k in range(4):
                    last = T.transpose(m.bank[6 + c][:, k * P:(k + 1) * P], acts[:, c, k * P:(k + 1) * P], m.ident[:, :])
                last.then_inc(q["actt_psum"], 1)

            def body(b, further):
                pe.wait_ge(q["bias_in"], 16 * (b + 1))
                for c in range(2):
                    pe.wait_ge(gu_free[c], b + 1)
                    for g in range(2):
                        T.matmul(m.bank[2 * c + g][:, :], ones3, bias[:, g * D + c * 512:g * D + (c + 1) * 512],
                                 start=True, stop=False)
                    for kh in range(2):
                        if c == 0:
                            pe.wait_ge((q["xt_copied_a"], q["xt_copied_b"])[kh], b + 1)
                        pe.wait_ge(piece_in[2 * c + kh], 32 * (b + 1))
                        w = gu_slot(2 * c + kh)
                        for k in range(4):
                            for g in range(2):
                                last = T.matmul(m.bank[2 * c + g][:, :], xt[:, 4 * kh + k, :], w[:, k, g, :],
                                                start=False, stop=(kh == 1 and k == 3))
                        last.then_inc(piece_free[2 * c + kh], 1)
                    pe.wait_ge(piece_free[2 * c + 1], b + 2)
                    pe.sem_inc(q["gu_mm"], 1)
                pe.wait_ge(q["act_done"], 2 * b + 1)
                act_half(0)
                pe.wait_ge(q["y_free"], b + 1)
                for n in range(2):
                    last = T.matmul(m.bank[4 + n][:, :], ones3, bias[:, 2 * D + n * 512:2 * D + (n + 1) * 512], start=True, stop=False)
                last.then_inc(q["bias_free"], 1)
                for kh in range(2):
                    pe.wait_ge(q["actt_copied"], 2 * b + kh + 1)
                    pe.wait_ge(piece_in[4 + kh], 16 * (b + 1))
                    w = down_slot(4 + kh)
                    for k in range(4):
                        for n in range(2):
                            last = T.matmul(m.bank[4 + n][:, :], acts_t[:, 4 * kh + k, :], w[:, k, n * 512:(n + 1) * 512],
                                            start=False, stop=(kh == 1 and k == 3))
                    last.then_inc(piece_free[4 + kh], 1)
                    if kh == 0:
                        pe.wait_ge(q["act_done"], 2 * b + 2)
                        act_half(1)
                        pe.wait_ge(q["xg_in"], 16 * (b + 2))
                        xt_half(0)
                pe.wait_ge(piece_free[5], b + 2)
                pe.sem_inc(q["y_mm"], 1)
                xt_half(1)
                pe.wait_ge(q["xt_psum_b"], b + 2)
                pe.sem_inc(q["xg_free"], 1)

            pe.wait_ge(q["ones_set"], 2)
            for s in (*piece_free, q["bias_free"], q["xg_free"]):
                pe.sem_inc(s, 1)
            pe.wait_ge(q["xg_in"], 16)
            xt_half(0)
            xt_half(1)
            pe.wait_ge(q["xt_psum_b"], 1)
            pe.sem_inc(q["xg_free"], 1)
            all_blocks(pe, body)


def combine(nc, io, m):
    with ExitStack() as ctx:
        sem = lambda n: m.sem("co_" + n)
        a = Arena(m.arena)
        a.at = m.x2_at + (NT + 1) * D
        row_p = a.take(D)
        row_s = a.take(D, rows=NB)
        acc = a.take(2, D)
        w = Arena(m.wring)
        ring = w.take(8, D)
        row_in, taken, added, summed, gated, total, out = (sem(n) for n in ("row_in", "taken", "added", "summed", "gated", "total", "out"))
        got = m.got
        block = ctx.enter_context(nc.Block())

        @block.sync
        def _(sp):
            row = m.mod_dram[NB:NB + 1, 5 * D:6 * D]
            sp.dma_start(row_p, row.broadcast_to([P, D])).then_inc(row_in, 16)
            sp.dma_start(row_s, m.mod_dram[0:NB, 5 * D:6 * D]).then_inc(row_in, 16)
            for t in range(NT + 1):
                r = rows_of(t)
                sp.wait_ge(total, t + 1)
                dst = io["y_prompt"][0, t * P:(t + 1) * P, :] if t < NT else io["y_sample"][:, 0, :]
                sp.dma_start(dst, m.x2[0:r, t, :]).then_inc(out, 16)
            sp.wait_ge(out, 16 * (NT + 1))

        @block.gpsimd
        def _(pool):
            for i in range((NT + 1) * TOPK):
                r = rows_of(i // TOPK)
                if i >= 8:
                    pool.wait_ge(added, i - 7)
                nc.gpsimd.indirect_dma_start(out=ring[0:r, i % 8, :], out_offset=None, in_=m.y_dram,
                                             in_offset=bass.IndirectOffsetOnAxis(ap=m.slots[0:r, i:i + 1], axis=0))\
                    .then_inc(got[i % 8], 16)

        @block.vector
        def _(dve):
            dve.wait_ge(row_in, 32)
            for t in range(NT + 1):
                r = rows_of(t)
                sum_ = acc[0:r, t % 2, :]
                for c in range(TOPK):
                    i = t * TOPK + c
                    dve.wait_ge(got[i % 8], 16 * (i // 8 + 1))
                    if i:
                        dve.wait_ge(added, i)
                    wt = m.weights[0:r, i:i + 1]
                    if c == 0:
                        nc.vector.tensor_scalar(sum_, ring[0:r, i % 8, :], wt, None, ALU.mult).then_inc(added, 1)
                    else:
                        nc.vector.scalar_tensor_tensor(sum_, ring[0:r, i % 8, :], wt, sum_, ALU.mult, ALU.add).then_inc(added, 1)
                dve.wait_ge(added, TOPK * (t + 1))
                nc.vector.tensor_mul(sum_, sum_, (row_p if t < NT else row_s)[0:r, :]).then_inc(gated, 1)
                dve.wait_ge(gated, t + 1)
                nc.vector.tensor_add(m.x2[0:r, t, :], m.x2[0:r, t, :], sum_).then_inc(total, 1)


def program(nc, io, upto=99):
    with ExitStack() as ctx:
        sb = lambda n, s, dt=F32: ctx.enter_context(nc.sbuf_tensor(n, s, dt))
        m = Memory()
        m.wring = sb("weight_ring", [P, NSLOT * SLOT])
        m.arena = sb("arena", [P, ARENA])
        m.ident = sb("identity", [P, P])
        small = sb("small", [P, 1130])
        m.small = Arena(small)
        m.bank = [ctx.enter_context(nc.psum_tensor(f"bank{i}", [P, 512], F32)) for i in range(8)]
        m.mod_dram = nc.dram_tensor("mod_rows", [NB + 1, 6 * D], F32).ap()
        m.tab_dram = nc.dram_tensor("slot_tokens", [(BLOCKS + 1) * BLK, 1], F32).ap()
        m.bias_dram = nc.dram_tensor("bias_parts", [EXPERTS, GUP, 3 * D], BF16).ap()
        m.y_dram = nc.dram_tensor("expert_rows", [BLOCKS * BLK, D], F32).ap()
        m.slots = sb("slots", [P, (NT + 1) * TOPK], I32)
        m.weights = sb("weights", [P, (NT + 1) * TOPK])
        m.gather_idx = sb("gather_idx", [P, BLOCKS + 1], I32)
        m.more_expert = sb("more_expert", [P, MORE + 1], I32)
        m.sx_dram = nc.dram_tensor("sample_rows", [6, NB, AW], F32).ap()
        m.sy_dram = nc.dram_tensor("sample_y", [NB, AW], F32).ap()
        m.levels = sb("level_masks", [P, 2 * LEVELS * P], mybir.dt.uint8)
        m.h2_dram = nc.dram_tensor("h2_rows", [TOK, D], F32).ap()
        a = Arena(m.arena)
        m.ht = a.take(KT, TOK)
        m.ct = m.ht
        m.pp_at = a.at
        m.pp = a.take(RF, 1 + TOK)
        m.v_new = a.take(AW)
        m.rwkv_at = a.at
        m.qt = a.take(4, SEQ)
        m.kt = a.take(4, SEQ)
        m.v_tok = a.take(NT, AW)
        m.scratch_at = a.at
        m.x2_at = m.pp_at
        m.x2 = m.arena[:, m.x2_at:m.x2_at + (NT + 1) * D].rearrange("p (t n) -> p t n", t=NT + 1)
        stages = [("ada", modulation), ("proj", projection), ("attn", attention), ("rwkv", rwkv), ("route", mix_and_route),
                  ("experts", experts), ("combine", combine)]
        m.scattered, m.xg_in = nc.alloc_semaphore("scattered"), nc.alloc_semaphore("xg_in")
        m.got = [nc.alloc_semaphore(f"got{i}") for i in range(8)]
        in_use = []

        def sem(name):
            in_use.append(nc.alloc_semaphore(f"{m.stage}_{name}"))
            return in_use[-1]

        m.sem = sem
        for name, f in stages[:upto]:
            m.small.at = 0
            m.stage = name
            f(nc, io, m)
            nc.clear_and_free_semaphores(in_use)
            nc.all_engine_barrier()
            in_use.clear()
def more_constants():
    def times(dist):
        c = sum(((dist >= 0) & (dist <= w) & (dist % d == 0)).astype(np.float64) for w, d in PATTERNS)
        return np.where(c > 0, 8.0 * np.log(np.maximum(c, 1.0)), -1.0e30).astype(np.float32)

    q, k = np.arange(P)[:, None], np.arange(SEQ)[None, :] - (SEQ - P)
    sample = np.zeros((P, 4, NH), np.float32)
    sample[:, 3, :] = -1.0e30
    sample[0, 3, :] = times(np.array(0))
    head_mask = (np.arange(AW)[None, :] // HD == np.arange(NH)[:, None]).astype(np.float32)
    i, j = np.arange(P)[:, None], np.arange(P)[None, :]
    same = i // CHUNK == j // CHUNK
    tri = np.stack([same & (j > i), same & (j >= i)], 1).astype(np.float32)
    low = [(i // (2 * b) == j // (2 * b)) & (i // b % 2 == 1) & (j // b % 2 == 0) for b in (1, 2, 4, 8, 16, 32)]
    levels = np.concatenate(low + [x.T for x in low], 1).astype(np.float32)
    ones_blk = (i // HD == j // HD).astype(np.float32)
    restart = np.broadcast_to((np.arange(SEQ) % CHUNK != 0).astype(np.float32), (P, SEQ)).copy()
    route = np.concatenate([np.broadcast_to(np.arange(EXPERTS), (P, EXPERTS)), np.broadcast_to(np.arange(MORE), (P, MORE)),
                            np.arange(P)[:, None] + P * np.arange(NT + 1)[None, :]], 1).astype(np.float32)
    rank_tri = (i < j).astype(np.float32)
    return {"route": route, "rank_tri": rank_tri, "tri": tri, "levels": levels, "ones_blk": ones_blk, "restart": restart, "attn_bias": times(q - k), "sample_bias": sample.reshape(P, 4 * NH), "head_mask": head_mask}


INPUTS = ["x_prompt", "x_sample", "cache_k", "cache_v", "state_wkv", "state_shift", "c_prompt", "c_sample",
          "w_ada", "b_ada", "norm1_g", "norm2_g", "w_in", "q_norm_g", "k_norm_g",
          "rwkv_mu", "rwkv_w0", "rwkv_w2", "rwkv_a0", "rwkv_a2", "rwkv_g2",
          "rwkv_k_k", "rwkv_k_a", "rwkv_r_k", "rwkv_ln_w", "rwkv_ln_b", "w_out",
          "router_w", "router_b", "moe_w_gu", "moe_b_gu", "moe_w_down", "moe_b_down"]
OUTPUTS = [("y_prompt", (1, SEQ, D)), ("y_sample", (NB, 1, D)),
           ("k_prompt", (1, 1, SEQ, NH, HD)), ("v_prompt", (1, 1, SEQ, NH, HD)),
           ("wkv_prompt", (1, 1, NH, HD, HD)), ("shift_prompt", (1, 1, RC)),
           ("k_new", (1, NB, 1, NH, HD)), ("v_new", (1, NB, 1, NH, HD)),
           ("wkv_sample", (1, NB, NH, HD, HD)), ("shift_sample", (1, NB, RC))]


def constants():
    pos = np.minimum(np.arange((NT + 1) * P), SEQ).astype(np.float32)
    pos[SEQ:] = PAST
    inv = (1.0 / (np.float32(10000.0) ** (np.arange(0, HD, 2, dtype=np.float32) / HD))).astype(np.float32)
    ang = (pos[:, None] * inv[None, :]).astype(np.float32)
    tiles = lambda t: np.ascontiguousarray(t.reshape(NT + 1, P, -1).transpose(1, 0, 2)).astype(np.float32)
    out = {"ident": np.eye(P, dtype=np.float32), "cos": tiles(np.cos(ang)), "sin": tiles(np.sin(ang))}
    out.update(more_constants())
    return out


def kernel(**inputs):
    from concourse import bacc
    from concourse.bass_utils import run_bass_kernel_spmd

    nc = bacc.Bacc("TRN2", target_bir_lowering=False, num_devices=1)
    arrays = {k: np.ascontiguousarray(inputs[k]) for k in INPUTS}
    arrays.update(constants())
    io = {k: nc.dram_tensor(f"in_{k}", a.shape, mybir.dt.from_np(a.dtype), kind="ExternalInput").ap()
          for k, a in arrays.items()}
    io.update({k: nc.dram_tensor(f"out_{k}", s, F32, kind="ExternalOutput").ap() for k, s in OUTPUTS})
    program(nc, io)
    r = run_bass_kernel_spmd(nc, [{f"in_{k}": a for k, a in arrays.items()}], core_ids=[0])
    return tuple(r.results[0][f"out_{k}"] for k, _ in OUTPUTS)
```

```python
from contextlib import ExitStack

import numpy as np

import concourse.bass as bass
from concourse import mybir

F32 = mybir.dt.float32
BF16 = mybir.dt.bfloat16
I32 = mybir.dt.int32
ALU = mybir.AluOpType
ACT = mybir.ActivationFunctionType
AXX = mybir.AxisListType.X

P = 128
D = 1024
KT = D // P
SEQ = 512
NB = 8
NT = SEQ // P
TOK = SEQ + NB
HD = 64
NH = 8
AW = NH * HD
RC = 3 * AW + 256
RF = RC // P
PAST = 2048
EXPERTS = 32
TOPK = 4
PATTERNS = ((128, 1), (512, 4), (2048, 16))
NORM_EPS = 1e-6
GN_EPS = 64e-5
ARENA = 26800
SLOT = 4096
NSLOT = 6


class Memory:
    pass


class Arena:

    def __init__(self, whole):
        self.whole, self.at = whole, 0

    def take(self, *dims, rows=P):
        n = int(np.prod(dims))
        v = self.whole[0:rows, self.at:self.at + n]
        self.at += n
        assert self.at <= self.whole.shape[1], self.at
        if len(dims) == 2:
            v = v.rearrange("p (a b) -> p a b", b=dims[1])
        if len(dims) == 3:
            v = v.rearrange("p (a b c) -> p a b c", b=dims[1], c=dims[2])
        return v


def rows_of(token_tile):
    return P if token_tile < NT else NB


def cols_of(token_tile):
    return slice(token_tile * P, token_tile * P + rows_of(token_tile))


def slot_view(wring, piece, n=512):
    s = piece % NSLOT
    return wring[:, s * SLOT:s * SLOT + KT * n].rearrange("p (k n) -> p k n", k=KT)


def wide(dram, c0, n=512):
    return dram.rearrange("(k p) n -> p k n", p=P)[:, :, c0:c0 + n]


WIN_AHEAD = 2


def modulation(nc, io, m):
    NC = NB + 1
    NCH = 6 * D // 512
    with ExitStack() as ctx:
        sem = m.sem
        a = Arena(m.arena)
        c_rows = a.take(D, rows=NC)
        c_sig = a.take(D, rows=NC)
        mod = a.take(6 * D, rows=NC)
        bias = a.take(6 * D, rows=NC)
        gains = a.take(2, D, rows=NC)
        ct = a.take(KT, NC)
        levels = a.take(2 * LEVELS * P)
        a.at = m.scratch_at + (NT + 1) * D
        squares = a.take(D)
        ss, rstd = m.row_stats[:, 0:NT + 1], m.row_stats[:, NT + 1:]
        ss_set = sem("ss_set")
        squared = sem("squared")
        mean_done = sem("mean_done")
        ms_done = sem("ms_done")
        c_in = sem("c_in")
        levels_in = sem("levels_in")
        bias_in = sem("bias_in")
        consts_in = sem("consts_in")
        ada_in = [sem(f"ada_in{i}") for i in range(NSLOT)]
        sig_done = sem("sig_done")
        silu_done = sem("silu_done")
        ct_psum = sem("ct_psum")
        ct_done = sem("ct_done")
        chunk_mm = sem("chunk_mm")
        chunk_added = sem("chunk_added")
        mod_scaled = sem("mod_scaled")
        mod_out = sem("mod_out")
        block = ctx.enter_context(nc.Block())

        @block.sync
        def _(sp):
            sp.dma_start(c_rows[0:NB, :], io["c_sample"]).then_inc(c_in, 16)
            sp.dma_start(c_rows[NB:NC, :], io["c_prompt"]).then_inc(c_in, 16)
            for n in range(NCH):
                if n >= NSLOT:
                    sp.wait_ge(chunk_mm, n - NSLOT + 1)
                sp.dma_start(slot_view(m.wring, n), wide(io["w_ada"][0], n * 512)).then_inc(ada_in[n % NSLOT], 16)
            for t in range(NT):
                sp.dma_start(m.h[:, t, :], io["x_prompt"][0, t * P:(t + 1) * P, :]).then_inc(m.x_in[t], 16)
            sp.dma_start(m.h[0:NB, NT, :], io["x_sample"][:, 0, :]).then_inc(m.x_in[NT], 16)
            for j in range(WIN_AHEAD):
                sp.wait_ge(chunk_mm, NCH - NSLOT + j + 1)
                sp.dma_start(slot_view(m.wring, j), wide(io["w_in"][0], j * 512)).then_inc(m.win_in[j], 16)
            sp.wait_ge(mod_scaled, 1)
            sp.dma_start(m.mod_dram, mod).then_inc(mod_out, 16)
            sp.wait_ge(mod_out, 16)

        @block.scalar
        def _(act):
            act.dma_start(m.ident[:, :], io["ident"]).then_inc(consts_in, 16)
            act.dma_start(bias, io["b_ada"].broadcast_to([NC, 6 * D])).then_inc(bias_in, 16)
            act.dma_start(gains[:, 0, :], io["norm1_g"].broadcast_to([NC, D])).then_inc(bias_in, 16)
            act.dma_start(gains[:, 1, :], io["norm2_g"].broadcast_to([NC, D])).then_inc(bias_in, 16)
            act.dma_start(levels, io["levels"]).then_inc(levels_in, 16)
            act.wait_ge(c_in, 32)
            nc.scalar.activation(c_sig, c_rows, ACT.Sigmoid).then_inc(sig_done, 1)
            act.wait_ge(ss_set, 1)
            for t in range(NT + 1):
                r = rows_of(t)
                act.wait_ge(m.x_in[t], 16)
                if t:
                    act.wait_ge(squared, t)
                nc.scalar.activation(squares[0:r, :], m.h[0:r, t, :], ACT.Square, accum_out=ss[0:r, t:t + 1]).then_inc(squared, 1)
            act.wait_ge(ms_done, 1)
            nc.scalar.activation(rstd, rstd, ACT.Sqrt)

        @block.gpsimd
        def _(pool):
            pool.wait_ge(levels_in, 16)
            nc.gpsimd.tensor_copy(m.levels[:, :], levels)

        @block.vector
        def _(dve):
            nc.vector.memset(ss, 1.0).then_inc(ss_set, 1)
            dve.wait_ge(sig_done, 1)
            nc.vector.tensor_mul(c_rows, c_rows, c_sig).then_inc(silu_done, 1)
            dve.wait_ge(ct_psum, 1)
            nc.vector.tensor_copy(ct.rearrange("p k c -> p (k c)"), m.bank[7][:, 0:KT * NC]).then_inc(ct_done, 1)
            dve.wait_ge(bias_in, 48)
            for n in range(NCH):
                dve.wait_ge(chunk_mm, n + 1)
                nc.vector.tensor_add(mod[:, n * 512:(n + 1) * 512], m.bank[n % 2][0:NC, :],
                                     bias[:, n * 512:(n + 1) * 512]).then_inc(chunk_added, 1)
            dve.wait_ge(chunk_added, NCH)
            for i, scale_at in enumerate((1, 4)):
                v = mod[:, scale_at * D:(scale_at + 1) * D]
                last = nc.vector.scalar_tensor_tensor(v, v, 1.0, gains[:, i, :], ALU.add, ALU.mult)
            last.then_inc(mod_scaled, 1)
            dve.wait_ge(squared, NT + 1)
            nc.vector.tensor_scalar(rstd, ss, 1.0 / D, NORM_EPS, ALU.mult, ALU.add).then_inc(mean_done, 1)
            dve.wait_ge(mean_done, 1)
            nc.vector.reciprocal(rstd, rstd).then_inc(ms_done, 1)

        @block.tensor
        def _(pe):
            pe.wait_ge(consts_in, 16)
            pe.wait_ge(silu_done, 1)
            for k in range(KT):
                last = nc.tensor.transpose(m.bank[7][:, k * NC:(k + 1) * NC], c_rows[:, k * P:(k + 1) * P],
                                           m.ident[0:NC, 0:NC])
            last.then_inc(ct_psum, 1)
            pe.wait_ge(ct_done, 1)
            for n in range(NCH):
                pe.wait_ge(ada_in[n % NSLOT], 16 * (n // NSLOT + 1))
                if n >= 2:
                    pe.wait_ge(chunk_added, n - 1)
                w = slot_view(m.wring, n)
                for k in range(KT):
                    last = nc.tensor.matmul(m.bank[n % 2][0:NC, :], ct[:, k, :], w[:, k, :],
                                            start=(k == 0), stop=(k == KT - 1))
                last.then_inc(chunk_mm, 1)


def projection(nc, io, m):
    with ExitStack() as ctx:
        sem = m.sem
        a = Arena(m.arena)
        a.at = m.scratch_at
        a.at += (NT + 1) * D
        h = m.h
        a.at = m.scratch_at
        qk = a.take(2, NT + 1, AW)
        tmp = a.take(2, AW)
        shift_rows = a.take(RC, rows=NB + 1)
        m.qk = qk
        a.at = m.rwkv_at
        row_p = a.take(2, D)
        row_s = a.take(2, D, rows=NB)
        gain = m.small.take(2, HD)
        cos = m.small.take(NT + 1, HD // 2)
        sin = m.small.take(NT + 1, HD // 2)
        rstd = m.row_stats[:, NT + 1:]
        hs = m.small.take(2, NH)
        rn = m.small.take(2, NH)
        win_in = m.win_in
        rows_in = sem("rows_in")
        tables_in = sem("tables_in")
        h_scaled = sem("h_scaled")
        h_done = sem("h_done")
        ht_psum = sem("ht_psum")
        ht_copied = sem("ht_copied")
        proj_mm = sem("proj_mm")
        proj_copied = sem("proj_copied")
        rwkv_mm = sem("rwkv_mm")
        rwkv_copied = sem("rwkv_copied")
        head_ms = sem("head_ms")
        head_rn = sem("head_rn")
        own = sem("vector_own")
        roped = sem("roped")
        qkt_psum = sem("qkt_psum")
        qkt_copied = sem("qkt_copied")
        shift_psum = sem("shift_psum")
        shift_done = sem("shift_done")
        edge_set = sem("edge_set")
        out_kv = sem("out_kv")
        units = [(n, t) for n in range(3) for t in range(NT + 1)]
        block = ctx.enter_context(nc.Block())

        def qk_of(n, t):
            if n == 2:
                return m.v_tok[:, t, :] if t < NT else m.v_new
            return qk[:, n, t, :]

        @block.sync
        def _(sp):
            for i in range(2):
                row = m.mod_dram[NB:NB + 1, i * D:(i + 1) * D]
                sp.dma_start(row_p[:, i, :], row.broadcast_to([P, D])).then_inc(rows_in, 16)
                sp.dma_start(row_s[:, i, :], m.mod_dram[0:NB, i * D:(i + 1) * D]).then_inc(rows_in, 16)
            for j in range(WIN_AHEAD, NSLOT):
                sp.dma_start(slot_view(m.wring, j), wide(io["w_in"][0], j * 512)).then_inc(win_in[j], 16)
            sp.wait_ge(proj_mm, NT + 1)
            sp.dma_start(slot_view(m.wring, NSLOT, 256), wide(io["w_in"][0], NSLOT * 512, 256)).then_inc(win_in[NSLOT], 16)
            for t in range(NT + 1):
                r = rows_of(t)
                sp.wait_ge(proj_copied, 2 * (NT + 1) + t + 1)
                dst = io["v_prompt"][0, 0, t * P:(t + 1) * P] if t < NT else io["v_new"][0, :, 0]
                sp.dma_start(dst.rearrange("t h d -> t (h d)"), qk_of(2, t)[0:r, :]).then_inc(out_kv, 16)
            for t in range(NT + 1):
                r = rows_of(t)
                sp.wait_ge(roped, NT + 1 + t + 1)
                dst = io["k_prompt"][0, 0, t * P:(t + 1) * P] if t < NT else io["k_new"][0, :, 0]
                sp.dma_start(dst.rearrange("t h d -> t (h d)"), qk[0:r, 1, t, :]).then_inc(out_kv, 16)
            sp.wait_ge(shift_done, 4)
            sp.dma_start(io["shift_sample"][0], shift_rows[1:NB + 1, :]).then_inc(out_kv, 16)
            sp.dma_start(io["shift_prompt"][0], shift_rows[0:1, :]).then_inc(out_kv, 16)
            sp.wait_ge(out_kv, 16 * (2 * (NT + 1) + 2))

        @block.scalar
        def _(act):
            act.dma_start(gain[:, 0, :], io["q_norm_g"].broadcast_to([P, HD])).then_inc(tables_in, 16)
            act.dma_start(gain[:, 1, :], io["k_norm_g"].broadcast_to([P, HD])).then_inc(tables_in, 16)
            act.dma_start(cos, io["cos"]).then_inc(tables_in, 16)
            act.dma_start(sin, io["sin"]).then_inc(tables_in, 16)
            for t in range(NT + 1):
                r = rows_of(t)
                act.wait_ge(ht_psum, t + 1)
                for half in range(2):
                    src = m.bank[(2 * t + half) % 4][:, 0:4 * r].rearrange("p (k c) -> p k c", k=4)
                    nc.scalar.copy(m.ht[:, 4 * half:4 * half + 4, cols_of(t)], src).then_inc(ht_copied, 1)
            for u, (n, t) in enumerate(units):
                r = rows_of(t)
                act.wait_ge(proj_mm, u + 1)
                nc.scalar.copy(qk_of(n, t)[0:r, :], m.bank[4 + u % 4][0:r, :]).then_inc(proj_copied, 1)
                if n < 2:
                    act.wait_ge(head_ms, u + 1)
                    nc.scalar.activation(rn[0:r, u % 2, :], rn[0:r, u % 2, :], ACT.Sqrt).then_inc(head_rn, 1)
            for f in range(RF):
                act.wait_ge(rwkv_mm, f + 1)
                nc.scalar.copy(m.pp[:, f, 1:1 + TOK // 2], m.bank[f % 2][:, 0:TOK // 2])
                nc.scalar.copy(m.pp[:, f, 1 + TOK // 2:], m.bank[2 + f % 2][:, 0:TOK // 2]).then_inc(rwkv_copied, 1)
            for u in range(2 * NT):
                n, t = u // NT, u % NT
                act.wait_ge(qkt_psum, u + 1)
                nc.scalar.copy((m.kt if n else m.qt)[:, :, cols_of(t)],
                               m.bank[4 + u % 4][:, :].rearrange("p (k c) -> p k c", k=4)).then_inc(qkt_copied, 1)

        @block.vector
        def _(dve):
            nc.vector.memset(m.pp[:, :, 0:1], 0.0).then_inc(edge_set, 1)
            dve.wait_ge(rows_in, 64)
            for t in range(NT + 1):
                r = rows_of(t)
                rows = row_p if t < NT else row_s
                nc.vector.scalar_tensor_tensor(h[0:r, t, :], h[0:r, t, :], rstd[0:r, t:t + 1], rows[0:r, 1, :],
                                               ALU.mult, ALU.mult).then_inc(h_scaled, 1)
                dve.wait_ge(h_scaled, t + 1)
                nc.vector.tensor_add(h[0:r, t, :], h[0:r, t, :], rows[0:r, 0, :]).then_inc(h_done, 1)
            dve.wait_ge(tables_in, 64)
            done = 0

            def head_sums(u):
                nonlocal done
                n, t = units[u]
                r = rows_of(t)
                x = qk[0:r, n, t, :]
                dve.wait_ge(proj_copied, u + 1)
                if u:
                    dve.wait_ge(own, done)
                    dve.wait_ge(roped, u)
                nc.vector.tensor_mul(tmp[0:r, 0, :], x, x).then_inc(own, 1)
                dve.wait_ge(own, done + 1)
                nc.vector.tensor_reduce(hs[0:r, u % 2, :], tmp[0:r, 0, :].rearrange("p (h d) -> p h d", d=HD),
                                        AXX, ALU.add).then_inc(own, 1)
                dve.wait_ge(own, done + 2)
                nc.vector.tensor_scalar(hs[0:r, u % 2, :], hs[0:r, u % 2, :], 1.0 / HD, NORM_EPS, ALU.mult,
                                        ALU.add).then_inc(own, 1)
                dve.wait_ge(own, done + 3)
                nc.vector.reciprocal(rn[0:r, u % 2, :], hs[0:r, u % 2, :]).then_inc(head_ms, 1)
                done += 3

            def rotate(u):
                nonlocal done
                n, t = units[u]
                r = rows_of(t)
                x = qk[0:r, n, t, :]
                heads = x.rearrange("p (h d) -> p h d", d=HD)
                halves = x.rearrange("p (h s d) -> p h s d", h=NH, s=2)
                c, s = (tmp[0:r, i, :].rearrange("p (h s d) -> p h s d", h=NH, s=2) for i in range(2))
                wide_of = lambda table: table[0:r, t, :].unsqueeze(1).unsqueeze(1).broadcast_to([r, NH, 2, HD // 2])
                dve.wait_ge(head_rn, u + 1)
                nc.vector.tensor_mul(heads, heads, rn[0:r, u % 2, :].unsqueeze(2).broadcast_to([r, NH, HD])).then_inc(own, 1)
                dve.wait_ge(own, done + 1)
                nc.vector.tensor_mul(heads, heads, gain[0:r, n, :].unsqueeze(1).broadcast_to([r, NH, HD])).then_inc(own, 1)
                dve.wait_ge(own, done + 2)
                nc.vector.tensor_mul(c, halves, wide_of(cos)).then_inc(own, 1)
                nc.vector.tensor_mul(s, halves, wide_of(sin)).then_inc(own, 1)
                dve.wait_ge(own, done + 4)
                nc.vector.tensor_sub(halves[:, :, 0, :], c[:, :, 0, :], s[:, :, 1, :]).then_inc(own, 1)
                nc.vector.tensor_add(halves[:, :, 1, :], c[:, :, 1, :], s[:, :, 0, :]).then_inc(roped, 1)
                done += 5

            for u in range(2 * (NT + 1)):
                head_sums(u)
                rotate(u)
            for b in range(4):
                n = min(512, RC - b * 512)
                dve.wait_ge(shift_psum, 1)
                nc.vector.tensor_copy(shift_rows[:, b * 512:b * 512 + n], m.bank[b][0:NB + 1, 0:n]).then_inc(shift_done, 1)

        @block.tensor
        def _(pe):
            for t in range(NT + 1):
                r = rows_of(t)
                pe.wait_ge(h_done, t + 1)
                if t >= 2:
                    pe.wait_ge(ht_copied, 2 * (t - 1))
                for k in range(KT):
                    bank = m.bank[(2 * t + k // 4) % 4]
                    last = nc.tensor.transpose(bank[:, (k % 4) * r:(k % 4 + 1) * r], h[0:r, t, k * P:(k + 1) * P],
                                               m.ident[0:r, 0:r])
                last.then_inc(ht_psum, 1)
            for u, (n, t) in enumerate(units):
                r = rows_of(t)
                pe.wait_ge(ht_copied, 2 * (t + 1))
                pe.wait_ge(win_in[n], 16)
                if u >= 4:
                    pe.wait_ge(proj_copied, u - 3)
                w = slot_view(m.wring, n)
                for k in range(KT):
                    last = nc.tensor.matmul(m.bank[4 + u % 4][0:r, :], m.ht[:, k, cols_of(t)], w[:, k, :],
                                            start=(k == 0), stop=(k == KT - 1))
                last.then_inc(proj_mm, 1)
            for f in range(RF):
                j = 3 + f // 4
                pe.wait_ge(win_in[j], 16)
                if f >= 2:
                    pe.wait_ge(rwkv_copied, f - 1)
                w = slot_view(m.wring, j, 512 if j < 6 else 256)
                for out, cols in ((m.bank[f % 2], slice(0, TOK // 2)), (m.bank[2 + f % 2], slice(TOK // 2, TOK))):
                    for k in range(KT):
                        last = nc.tensor.matmul(out[:, 0:TOK // 2], w[:, k, (f % 4) * P:(f % 4 + 1) * P], m.ht[:, k, cols],
                                                start=(k == 0), stop=(k == KT - 1))
                last.then_inc(rwkv_mm, 1)
            for u in range(2 * NT):
                n, t = u // NT, u % NT
                pe.wait_ge(roped, n * (NT + 1) + t + 1)
                if u >= 4:
                    pe.wait_ge(qkt_copied, u - 3)
                else:
                    pe.wait_ge(proj_copied, 3 * (NT + 1))
                for j in range(4):
                    last = nc.tensor.transpose(m.bank[4 + u % 4][:, j * P:(j + 1) * P],
                                               qk[:, n, t, j * P:(j + 1) * P], m.ident[:, :])
                last.then_inc(qkt_psum, 1)
            pe.wait_ge(rwkv_copied, RF)
            for f in range(RF):
                last = nc.tensor.transpose(m.bank[f // 4][0:NB + 1, (f % 4) * P:(f % 4 + 1) * P],
                                           m.pp[:, f, SEQ:SEQ + NB + 1], m.ident[:, :])
            last.then_inc(shift_psum, 1)


def attention(nc, io, m):
    SCALE = 1.0 / 8.0
    G = 4
    assert HD == 64
    with ExitStack() as ctx:
        sem = m.sem
        a = Arena(m.wring)
        bias = a.take(SEQ)
        prob = a.take(3, SEQ)
        prob_t = a.take(2, SEQ)
        kg = a.take(2, G, AW)
        vg = a.take(2, G, AW)
        prod = a.take(G, AW)
        pick = a.take(NB, P, rows=NB)
        head_mask = a.take(AW, rows=NH)
        own_v = a.take(2, AW, rows=NH)
        sbias = a.take(G * NH)
        sc = a.take(NB, G * NH)
        smax = a.take(NB * NH)
        gmax = a.take(NB * NH)
        rs = a.take(NB, rows=NH)
        ones = a.take(1)
        top = a.take(32)
        ntop = a.take(32)
        psum_of_p = a.take(32)
        rinv = a.take(32)
        zero_rows = a.take(D)
        tables_in = sem("tables_in")
        zero_set = sem("zero_set")
        rows_zero = sem("rows_zero")
        scores_mm = sem("scores_mm")
        top_done = sem("top_done")
        max_ready = sem("max_ready")
        exp_done = sem("exp_done")
        inverse = sem("inverse")
        p_normed = sem("p_normed")
        pt_psum = sem("pt_psum")
        pt_copied = sem("pt_copied")
        pv_mm = sem("pv_mm")
        ct_copied = sem("ct_copied")
        pad_set = sem("pad_set")
        pick_set = sem("pick_set")
        kg_in = [sem(f"kg_in{i}") for i in range(2)]
        vg_in = [sem(f"vg_in{i}") for i in range(2)]
        q_spread = sem("q_spread")
        multiplied = sem("multiplied")
        scored = sem("scored")
        biased = sem("biased")
        sample_max = sem("sample_max")
        global_max = sem("global_max")
        centred = sem("centred")
        sample_exp = sem("sample_exp")
        sample_pv = sem("sample_pv")
        sample_inv = sem("sample_inv")
        own_kept = sem("own_kept")
        sample_ct = sem("sample_ct")
        units = [(h, i) for h in range(NH) for i in range(NT)]
        U = len(units)
        block = ctx.enter_context(nc.Block())

        def base(h):
            return HD * (h % 2)

        @block.sync
        def _(sp):
            sp.dma_start(bias, io["attn_bias"]).then_inc(tables_in, 16)
            sp.dma_start(sbias, io["sample_bias"]).then_inc(tables_in, 16)
            sp.dma_start(head_mask, io["head_mask"]).then_inc(tables_in, 16)
            sp.wait_ge(pad_set, 2)
            sp.wait_ge(zero_set, 1)
            for cache, new, grp, landed, freed in ((io["cache_k"], m.qk[:, 1, NT, :], kg, kg_in, multiplied),
                                                   (io["cache_v"], m.v_new, vg, vg_in, sample_pv)):
                for b in range(NB):
                    if b >= 2:
                        sp.wait_ge(freed, b - 1)
                    past = cache[0, b].rearrange("t h d -> t (h d)")
                    for g, (w, d) in enumerate(PATTERNS):
                        sp.dma_start(grp[:, b % 2, g, :], past[PAST - w:PAST:d, :]).then_inc(landed[b % 2], 16)
                    sp.dma_start(grp[0:1, b % 2, 3, :], new[b:b + 1, :]).then_inc(landed[b % 2], 16)
                    if b < MORE // 2:
                        j = EXPERTS + b + (MORE // 2 if grp is vg else 0)
                        sp.dma_start(m.y_dram[j * BLK:(j + 1) * BLK, :], zero_rows).then_inc(rows_zero, 16)
            sp.wait_ge(rows_zero, 16 * MORE)

        @block.gpsimd
        def _(pool):
            nc.gpsimd.memset(zero_rows, 0.0).then_inc(zero_set, 1)
            nc.gpsimd.memset(kg[:, :, 3, :], 0.0).then_inc(pad_set, 1)
            nc.gpsimd.memset(vg[:, :, 3, :], 0.0).then_inc(pad_set, 1)
            pool.wait_ge(sample_max, 1)
            nc.gpsimd.partition_all_reduce(gmax, smax, P, bass.bass_isa.ReduceOp.max).then_inc(global_max, 1)

        @block.scalar
        def _(act):
            for s in range(U + 2):
                if s < U:
                    h, i = units[s]
                    w = (i + 1) * P
                    act.wait_ge(max_ready, s + 1)
                    nc.scalar.activation(prob[:, s % 3, 0:w], prob[:, s % 3, 0:w], ACT.Exp, bias=ntop[:, s:s + 1],
                                         scale=SCALE, accum_out=psum_of_p[:, s:s + 1]).then_inc(exp_done, 1)
                if s >= 2:
                    u = s - 2
                    w = (units[u][1] + 1) * P
                    act.wait_ge(pt_psum, u + 1)
                    if u >= 2:
                        act.wait_ge(pv_mm, u - 1)
                    nc.scalar.copy(prob_t[:, u % 2, 0:w], m.bank[3 + u % 2][:, 0:w]).then_inc(pt_copied, 1)
            act.wait_ge(centred, 1)
            nc.scalar.activation(sc, sc, ACT.Exp, scale=SCALE).then_inc(sample_exp, 1)

        @block.vector
        def _(dve):
            nc.vector.memset(ones, 1.0).then_inc(pick_set, 1)
            nc.vector.tensor_copy(pick, m.ident[0:NB, 0:NB].unsqueeze(2).broadcast_to([NB, NB, P])).then_inc(pick_set, 1)
            dve.wait_ge(tables_in, 48)

            def sample_products(b):
                dve.wait_ge(kg_in[b % 2], 64 * (b // 2 + 1))
                dve.wait_ge(q_spread, b + 1)
                if b:
                    dve.wait_ge(scored, b)
                nc.vector.tensor_mul(prod, kg[:, b % 2], m.bank[7][:, :].unsqueeze(1).broadcast_to([P, G, AW]))\
                    .then_inc(multiplied, 1)

            def sample_scores(b):
                dve.wait_ge(multiplied, b + 1)
                nc.vector.tensor_reduce(sc[:, b, :], prod.rearrange("p g (h d) -> p (g h) d", d=HD), AXX, ALU.add)\
                    .then_inc(scored, 1)

            def sample_tops():
                dve.wait_ge(scored, NB)
                nc.vector.tensor_add(sc, sc, sbias.unsqueeze(1).broadcast_to([P, NB, G * NH])).then_inc(biased, 1)
                dve.wait_ge(biased, 1)
                nc.vector.tensor_reduce(smax.rearrange("p (b h) -> p b h", b=NB), sc.rearrange("p b (g h) -> p b h g", g=G),
                                        AXX, ALU.max).then_inc(sample_max, 1)

            def sample_centre():
                dve.wait_ge(global_max, 1)
                by_head = sc.rearrange("p b (g h) -> p b g h", g=G)
                nc.vector.tensor_sub(by_head, by_head, gmax.rearrange("p (b h) -> p b h", b=NB).unsqueeze(2)
                                     .broadcast_to([P, NB, G, NH])).then_inc(centred, 1)

            for s in range(U + 3):
                if s % 3 == 2 and s // 3 < NB:
                    sample_products(s // 3)
                if s and s % 3 == 0 and s // 3 <= NB:
                    sample_scores(s // 3 - 1)
                if s == 3 * NB:
                    sample_tops()
                if s == 3 * NB + 4:
                    sample_centre()
                if s < U:
                    w = (units[s][1] + 1) * P
                    dve.wait_ge(scores_mm, s + 1)
                    if s >= 3:
                        dve.wait_ge(pt_psum, s - 2)
                    nc.vector.tensor_tensor_reduce(prob[:, s % 3, 0:w], m.bank[s % 3][:, 0:w], bias[:, SEQ - w:SEQ],
                                                   1.0, -3.0e38, ALU.add, ALU.max, top[:, s:s + 1]).then_inc(top_done, 1)
                    dve.wait_ge(top_done, s + 1)
                    nc.vector.tensor_scalar(ntop[:, s:s + 1], top[:, s:s + 1], -SCALE, None, ALU.mult).then_inc(max_ready, 1)
                if 1 <= s <= U:
                    u = s - 1
                    w = (units[u][1] + 1) * P
                    dve.wait_ge(exp_done, u + 1)
                    nc.vector.reciprocal(rinv[:, u:u + 1], psum_of_p[:, u:u + 1]).then_inc(inverse, 1)
                    dve.wait_ge(inverse, u + 1)
                    nc.vector.tensor_scalar(prob[:, u % 3, 0:w], prob[:, u % 3, 0:w], rinv[:, u:u + 1], None,
                                            ALU.mult).then_inc(p_normed, 1)
                if s >= 3:
                    u = s - 3
                    h, i = units[u]
                    dve.wait_ge(pv_mm, u + 1)
                    nc.vector.tensor_copy(m.ct[base(h):base(h) + HD, h // 2, i * P:(i + 1) * P],
                                          m.bank[5 + u % 2][base(h):base(h) + HD, 0:P]).then_inc(ct_copied, 1)
            for b in range(NB):
                dve.wait_ge(sample_pv, b + 1)
                nc.vector.reciprocal(rs[:, b:b + 1], m.bank[2 + b % 2][0:NH, 0:1]).then_inc(sample_inv, 1)
                dve.wait_ge(sample_inv, b + 1)
                nc.vector.scalar_tensor_tensor(own_v[:, b % 2, :], m.bank[b % 2][0:NH, :], rs[:, b:b + 1], head_mask,
                                               ALU.mult, ALU.mult).then_inc(own_kept, 1)
            dve.wait_ge(sample_ct, NB)
            nc.vector.tensor_copy(m.ct[:, 0:4, SEQ:TOK], m.bank[4][:, 0:4 * NB].rearrange("p (k b) -> p k b", k=4))

        @block.tensor
        def _(pe):
            for s in range(U + 3):
                if s % 3 == 1 and s // 3 < NB:
                    b = s // 3
                    if b == 0:
                        pe.wait_ge(pick_set, 2)
                    else:
                        pe.wait_ge(multiplied, b)
                    nc.tensor.matmul(m.bank[7][:, :], pick[:, b, :], m.qk[0:NB, 0, NT, :], start=True,
                                     stop=True).then_inc(q_spread, 1)
                if s < U:
                    h, i = units[s]
                    if s >= 3:
                        pe.wait_ge(top_done, s - 2)
                    rows = slice(base(h), base(h) + HD)
                    nc.tensor.matmul(m.bank[s % 3][:, 0:(i + 1) * P], m.qt[rows, h // 2, i * P:(i + 1) * P],
                                     m.kt[rows, h // 2, 0:(i + 1) * P], start=True, stop=True).then_inc(scores_mm, 1)
                if 2 <= s < U + 2:
                    u = s - 2
                    pe.wait_ge(p_normed, u + 1)
                    if u >= 2:
                        pe.wait_ge(pt_copied, u - 1)
                    for j in range(units[u][1] + 1):
                        last = nc.tensor.transpose(m.bank[3 + u % 2][:, j * P:(j + 1) * P],
                                                   prob[:, u % 3, j * P:(j + 1) * P], m.ident[:, :])
                    last.then_inc(pt_psum, 1)
                if s >= 3:
                    u = s - 3
                    h, i = units[u]
                    pe.wait_ge(pt_copied, u + 1)
                    if u >= 2:
                        pe.wait_ge(ct_copied, u - 1)
                    for j in range(i + 1):
                        last = nc.tensor.matmul(m.bank[5 + u % 2][base(h):base(h) + HD, 0:P],
                                                m.v_tok[:, j, h * HD:(h + 1) * HD], prob_t[:, u % 2, j * P:(j + 1) * P],
                                                start=(j == 0), stop=(j == i))
                    last.then_inc(pv_mm, 1)
            pe.wait_ge(top_done, U)
            pe.wait_ge(sample_exp, 1)
            pe.wait_ge(pt_copied, U)
            for b in range(NB + 1):
                if b < NB:
                    pe.wait_ge(vg_in[b % 2], 64 * (b // 2 + 1))
                    if b >= 2:
                        pe.wait_ge(own_kept, b - 1)
                    for g in range(G):
                        p_bg = sc[:, b, g * NH:(g + 1) * NH]
                        nc.tensor.matmul(m.bank[b % 2][0:NH, :], p_bg, vg[:, b % 2, g, :], start=(g == 0), stop=(g == G - 1))
                        last = nc.tensor.matmul(m.bank[2 + b % 2][0:NH, 0:1], p_bg, ones, start=(g == 0), stop=(g == G - 1))
                    last.then_inc(sample_pv, 1)
                if b:
                    pe.wait_ge(own_kept, b)
                    for k in range(4):
                        last = nc.tensor.matmul(m.bank[4][:, k * NB + b - 1:k * NB + b],
                                                own_v[:, (b - 1) % 2, k * P:(k + 1) * P], ones[0:NH, :], start=True, stop=True)
                    last.then_inc(sample_ct, 1)


CHUNK = 64
PAIRS = 4
LEVELS = 6
DECAY = float(np.exp(-0.5))
MU, W0, A0, KK_, KA, RK, LNW, LNB = 0, 14, 18, 22, 26, 30, 34, 38
N_PAR = 42


def rwkv(nc, io, m):
    with ExitStack() as ctx:
        sem = m.sem
        w = Arena(m.wring)
        tmp_a, tmp_b, cum = (w.take(PAIRS, TOK) for _ in range(3))
        ar = w.take(PAIRS, NT * 2 * P).rearrange("p h (t x c) -> p h t x c", t=NT, x=2)
        bt, kt = w.take(PAIRS, SEQ), w.take(PAIRS, SEQ)
        b_tok, k_tok, v_tok, a_tok = (w.take(NT, AW) for _ in range(4))
        lora_wa, lora_g = w.take(AW), w.take(AW)
        ones_blk = w.take(P)
        restart = w.take(SEQ)
        tri = w.take(2, P)
        head_pick = w.take(PAIRS, NH)
        w.at = 0
        lm = [w.take(NT, 2 * P).rearrange("p t (x c) -> p t x c", x=2) for _ in range(2)]
        x_inv, x_inv_t, z = ([w.take(NT, P) for _ in range(2)] for _ in range(3))
        mv = [w.take(NT, HD) for _ in range(2)]
        w.at = 3 * PAIRS * TOK + 2 * PAIRS * SEQ + PAIRS * SEQ
        state = w.take(2, PAIRS * P).rearrange("p b (h d) -> p b h d", h=PAIRS)
        sa = w.take(2, PAIRS * 2 * HD).rearrange("p b (h s d) -> p b h s d", h=PAIRS, s=2)
        w.at = 3 * PAIRS * TOK
        ys = w.take(PAIRS, TOK)
        y_sq = w.take(PAIRS, TOK)
        a = Arena(m.arena)
        a.at = m.rwkv_at
        g = a.take(PAIRS, TOK)
        r = a.take(PAIRS, TOK)
        nn_at = a.at
        k = a.take(PAIRS, TOK)
        v = a.take(PAIRS, TOK)
        ga = a.take(PAIRS, TOK)
        sw = a.take(PAIRS, TOK)
        kk_at = a.at
        kk = a.take(PAIRS, TOK)
        par_rows = a.take(P, rows=N_PAR)
        a.at = kk_at
        xl = a.take(2, TOK)
        a.at = nn_at
        nn = a.take(PAIRS * 2 * NT, 2 * P).rearrange("p u (x c) -> p u x c", x=2)
        u_tok = a.take(NT, PAIRS * 2 * HD).rearrange("p t (h s d) -> p t h s d", h=PAIRS, s=2)
        a.at = m.pp_at
        sx = a.take(6, AW, rows=NB)
        a.at = m.pp_at
        wt = a.take(PAIRS, SEQ)
        s_st = a.take(32, HD)
        s_tmp = a.take(32, HD)
        head_rows = a.take(AW, rows=NH)
        inv = a.take(TOK, rows=NH)
        y_rows = m.small.take(AW, rows=NB)
        par = m.small.take(N_PAR)
        ka1 = m.small.take(PAIRS)
        sh = m.small.take(RF, NB)
        sh_rows = tmp_a.rearrange("p h t -> p (h t)")[0:NB, 0:RC]
        pend = m.small.take(PAIRS, SEQ // CHUNK)
        sp_in = m.small.take(5, HD)
        sv_in = m.small.take(32)
        s_sa = m.small.take(32)
        s_y = m.small.take(32)
        names = ("tables_in state_in params_psum params_done mixed_lora lora_act lora_in lora_mm gates_done ones_in "
                 "head_rows_in mixed_rkv kk_sq kk_sum kk_norm kk_inverse kk_spread kk_done keys_done scanned exp_p exp_pm exp_m pm_ready ar_r ar_a b_ready "
                 "em_used bar_ready tok_psum tok_done bonus_in bonus_psum bonus_done sx_psum sx_done sx_out sx_in "
                 "s_ta s_sa_done s_new s_tr s_y_done s_y_out s_y_in s_y_psum "
                 "score_mm score_masked x_init z_mm z_copied xz_mm xt_mm x_new xt_new mv_mm mv_copied wt_mm wt_copied "
                 "u_mm u_copied sa_mm sa_done st_mm st_done y_mm y_copied state_psum state_rows_done wkv_out "
                 "mean_mm centred squared var_mm var_ready root_done inv_spread own").split()
        q = {n: sem("rw_" + n) for n in names}
        cols = (slice(0, SEQ), slice(SEQ, TOK))
        block = ctx.enter_context(nc.Block())

        def half(s):
            return slice(HD * s, HD * s + HD)

        @block.sync
        def _(sp):
            sp.dma_start(sh_rows, io["state_shift"][0]).then_inc(q["state_in"], 16)
            at = 0
            for src, n in ((io["rwkv_mu"], RF), (io["rwkv_w0"], 4), (io["rwkv_a0"], 4), (io["rwkv_k_k"], 4), (io["rwkv_k_a"], 4),
                           (io["rwkv_r_k"], 4), (io["rwkv_ln_w"], 4), (io["rwkv_ln_b"], 4)):
                flat = src[0].rearrange("h d -> (h d)") if len(src.shape) == 3 else src[0]
                sp.dma_start(par_rows[at:at + n, :], flat.rearrange("(n p) -> n p", p=P)).then_inc(q["tables_in"], 16)
                at += n
            sp.dma_start(lora_wa[0:HD, :], io["rwkv_w2"][0]).then_inc(q["lora_in"], 16)
            sp.dma_start(lora_wa[HD:P, :], io["rwkv_a2"][0]).then_inc(q["lora_in"], 16)
            sp.dma_start(lora_g, io["rwkv_g2"][0]).then_inc(q["lora_in"], 16)
            sp.dma_start(ones_blk, io["ones_blk"]).then_inc(q["ones_in"], 16)
            sp.dma_start(restart, io["restart"]).then_inc(q["ones_in"], 16)
            sp.dma_start(tri, io["tri"]).then_inc(q["ones_in"], 16)
            sp.dma_start(head_pick, io["head_pick"].rearrange("p (h n) -> p h n", h=PAIRS)).then_inc(q["ones_in"], 16)
            sp.wait_ge(q["mixed_rkv"], 1)
            sp.dma_start(head_rows, io["head_mask"]).then_inc(q["head_rows_in"], 16)
            sp.wait_ge(q["sx_done"], 6)
            sp.dma_start(m.sx_dram.rearrange("i b c -> b i c"), sx).then_inc(q["sx_out"], 16)
            sp.wait_ge(q["sx_out"], 16)
            for i in range(5):
                for u in range(2):
                    sp.dma_start(sp_in[u:P:2, i, :], m.sx_dram[i].rearrange("b (h d) -> (b h) d", d=HD)).then_inc(q["sx_in"], 16)
            sp.dma_start(sv_in, m.sx_dram[5].rearrange("b (p d) -> (b p) d", d=32)).then_inc(q["sx_in"], 16)
            sp.dma_start(s_st.rearrange("p v k -> p (v k)"),
                         io["state_wkv"][0].rearrange("b h (u v) k -> (b h u) (v k)", u=2)).then_inc(q["sx_in"], 16)
            sp.wait_ge(q["s_new"], 5)
            sp.dma_start(io["wkv_sample"][0].rearrange("b h (u v) k -> (b h u) (v k)", u=2),
                         s_st.rearrange("p v k -> p (v k)")).then_inc(q["wkv_out"], 16)
            sp.wait_ge(q["s_y_done"], 1)
            sp.dma_start(m.sy_dram.rearrange("b (p d) -> (b p) d", d=32), s_y).then_inc(q["s_y_out"], 16)
            sp.wait_ge(q["s_y_out"], 16)
            sp.dma_start(y_rows, m.sy_dram).then_inc(q["s_y_in"], 16)
            sp.wait_ge(q["state_rows_done"], 1)
            for h in range(NH):
                sp.dma_start(io["wkv_prompt"][0, 0, h], tmp_a[half(h % 2), 0, h * HD:(h + 1) * HD])\
                    .then_inc(q["wkv_out"], 16)
            sp.wait_ge(q["wkv_out"], 16 * (1 + NH))

        @block.gpsimd
        def _(pool):
            bc = lambda i: sp_in[:, i, :].unsqueeze(1).broadcast_to([P, 32, HD])
            bv = lambda x: x.unsqueeze(2).broadcast_to([P, 32, HD])
            pool.wait_ge(q["sx_in"], 16 * 12)
            nc.gpsimd.tensor_tensor(s_tmp, s_st, bc(2), ALU.mult).then_inc(q["s_ta"], 1)
            pool.wait_ge(q["s_ta"], 1)
            nc.gpsimd.tensor_tensor(s_st, s_st, bc(4), ALU.mult).then_inc(q["s_new"], 1)
            pool.wait_ge(q["s_sa_done"], 1)
            nc.gpsimd.tensor_tensor(s_tmp, bv(s_sa), bc(3), ALU.mult).then_inc(q["s_new"], 1)
            pool.wait_ge(q["s_new"], 2)
            nc.gpsimd.tensor_tensor(s_st, s_st, s_tmp, ALU.add).then_inc(q["s_new"], 1)
            pool.wait_ge(q["s_new"], 3)
            nc.gpsimd.tensor_tensor(s_tmp, bv(sv_in), bc(1), ALU.mult).then_inc(q["s_new"], 1)
            pool.wait_ge(q["s_new"], 4)
            nc.gpsimd.tensor_tensor(s_st, s_st, s_tmp, ALU.add).then_inc(q["s_new"], 1)
            pool.wait_ge(q["s_new"], 5)
            nc.gpsimd.tensor_tensor(s_tmp, s_st, bc(0), ALU.mult).then_inc(q["s_tr"], 1)

        @block.scalar
        def _(act):
            act.wait_ge(q["mixed_lora"], 1)
            nc.scalar.activation(xl[0:HD, 0, :], xl[0:HD, 0, :], ACT.Tanh).then_inc(q["lora_act"], 1)
            nc.scalar.activation(xl[:, 1, :], xl[:, 1, :], ACT.Sigmoid).then_inc(q["lora_act"], 1)
            act.wait_ge(q["params_done"], 1)
            for y, (dst, func, bias0) in enumerate(((sw, ACT.Sigmoid, W0), (ga, ACT.Sigmoid, A0), (g, ACT.Identity, None))):
                for h in range(PAIRS):
                    i = y * PAIRS + h
                    act.wait_ge(q["lora_mm"], i + 1)
                    for c, src in ((cols[0], m.bank[i % 6][:, :]), (cols[1], m.bank[6 + i % 2][:, 0:NB])):
                        if bias0 is None:
                            last = nc.scalar.copy(dst[:, h, c], src)
                        else:
                            last = nc.scalar.activation(dst[:, h, c], src, func, bias=par[:, bias0 + h:bias0 + h + 1])
                    last.then_inc(q["gates_done"], 1)
            act.wait_ge(q["kk_sum"], 1)
            nc.scalar.activation(inv[:, cols[0]], m.bank[4][0:NH, :], ACT.Sqrt)
            nc.scalar.activation(inv[:, cols[1]], m.bank[5][0:NH, 0:NB], ACT.Sqrt).then_inc(q["kk_norm"], 1)
            act.wait_ge(q["scanned"], PAIRS)
            act.wait_ge(q["kk_inverse"], 1)
            nc.scalar.activation(tmp_b[:, :, 0:SEQ], cum[:, :, 0:SEQ], ACT.Exp, scale=-DECAY).then_inc(q["exp_p"], 1)
            for i in range(6):
                act.wait_ge(q["sx_psum"], i + 1)
                src = m.bank[i][0:NB, :]
                if i == 4:
                    last = nc.scalar.activation(sx[:, i, :], src, ACT.Exp, scale=-DECAY)
                elif i == 2:
                    last = nc.scalar.mul(sx[:, i, :], src, -1.0)
                else:
                    last = nc.scalar.copy(sx[:, i, :], src)
                last.then_inc(q["sx_done"], 1)
            act.wait_ge(q["pm_ready"], 1)
            nc.scalar.activation(tmp_a[:, :, 0:SEQ], tmp_a[:, :, 0:SEQ], ACT.Exp, scale=-DECAY).then_inc(q["exp_pm"], 1)
            act.wait_ge(q["ar_a"], 1)
            nc.scalar.activation(tmp_a[:, :, 0:SEQ], cum[:, :, 0:SEQ], ACT.Exp, scale=DECAY).then_inc(q["exp_m"], 1)
            for i, dst in enumerate((v_tok, a_tok, k_tok, b_tok)):
                for t in range(NT):
                    act.wait_ge(q["tok_psum"], i * NT + t + 1)
                    nc.scalar.copy(dst[:, t, :], m.bank[(i * NT + t) % 6][:, :]).then_inc(q["tok_done"], 1)
            nz = 0
            for h in range(PAIRS):
                for lev in range(LEVELS):
                    for s in range(2):
                        if lev == 0:
                            continue
                        nz += 1
                        act.wait_ge(q["z_mm"], nz)
                        nc.scalar.copy(z[s].rearrange("p t c -> p (t c)"), m.bank[3 * s][:, :]).then_inc(q["z_copied"], 1)
                for s in range(2):
                    i = 2 * h + s
                    act.wait_ge(q["mv_mm"], i + 1)
                    nc.scalar.copy(mv[s].rearrange("p t d -> p (t d)"), m.bank[3 * s][:, 0:NT * HD]).then_inc(q["mv_copied"], 1)
                    act.wait_ge(q["wt_mm"], i + 1)
                    if i == 0:
                        act.wait_ge(q["sx_out"], 16)
                    nc.scalar.copy(wt[half(s), h, :], m.bank[3 * s + 1][half(s), :]).then_inc(q["wt_copied"], 1)
                    act.wait_ge(q["u_mm"], i + 1)
                    nc.scalar.copy(u_tok[:, :, h, s, :], m.bank[3 * s + 2][:, 0:NT * HD].rearrange("p (t d) -> p t d", t=NT))\
                        .then_inc(q["u_copied"], 1)
            for h in range(PAIRS):
                act.wait_ge(q["y_mm"], 8 * PAIRS)
                last = nc.scalar.copy(ys[:, h, 0:SEQ], m.bank[h][:, :])
            act.wait_ge(q["s_y_psum"], 1)
            nc.scalar.copy(ys[:, :, SEQ:TOK], m.bank[6][:, 0:PAIRS * NB].rearrange("p (h b) -> p h b", h=PAIRS)).then_inc(q["y_copied"], 1)
            act.wait_ge(q["var_ready"], 1)
            nc.scalar.activation(inv, inv, ACT.Sqrt).then_inc(q["root_done"], 1)

        @block.vector
        def _(dve):
            n_own = [0]

            def link(ins):
                n_own[0] += 1
                ins.then_inc(q["own"], 1)
                dve.wait_ge(q["own"], n_own[0])

            V = nc.vector
            dve.wait_ge(q["params_psum"], 1)
            link(V.tensor_copy(par, m.bank[0][:, 0:N_PAR]))
            V.tensor_copy(sh.rearrange("p f b -> p (f b)"), m.bank[1][:, 0:RF * NB]).then_inc(q["own"], 1)
            n_own[0] += 1
            V.tensor_scalar(ka1, par[:, KA:KA + PAIRS], -1.0, 1.0, ALU.mult, ALU.add).then_inc(q["params_done"], 1)
            dve.wait_ge(q["own"], n_own[0])
            cur_s = m.pp[:, :, SEQ + 1:]
            link(V.tensor_sub(sh, sh, cur_s))
            link(V.tensor_mul(sh, sh, par[:, MU:MU + RF].unsqueeze(2).broadcast_to([P, RF, NB])))
            for dst, f0, nf, done in ((xl, 12, 2, q["mixed_lora"]), (k, 4, 4, None), (r, 0, 4, None), (v, 8, 4, q["mixed_rkv"])):
                V.tensor_sub(dst[:, :, 0:SEQ], m.pp[:, f0:f0 + nf, 0:SEQ], m.pp[:, f0:f0 + nf, 1:SEQ + 1]).then_inc(q["own"], 1)
                n_own[0] += 1
                V.tensor_add(dst[:, :, SEQ:TOK], sh[:, f0:f0 + nf, :], cur_s[:, f0:f0 + nf, :]).then_inc(q["own"], 1)
                n_own[0] += 1
                dve.wait_ge(q["own"], n_own[0])
                for f in range(nf):
                    last = V.scalar_tensor_tensor(dst[:, f, 0:SEQ], dst[:, f, 0:SEQ], par[:, MU + f0 + f:MU + f0 + f + 1],
                                                  m.pp[:, f0 + f, 1:SEQ + 1], ALU.mult, ALU.add)
                if done is None:
                    link(last)
                else:
                    last.then_inc(done, 1)
            dve.wait_ge(q["mixed_rkv"], 1)
            dve.wait_ge(q["lora_mm"], 3 * PAIRS)
            for h in range(PAIRS):
                last = V.tensor_scalar(kk[:, h, :], k[:, h, :], par[:, KK_ + h:KK_ + h + 1], None, ALU.mult)
            link(last)
            V.tensor_mul(tmp_a, kk, kk).then_inc(q["kk_sq"], 1)
            dve.wait_ge(q["gates_done"], 2 * PAIRS)
            dve.wait_ge(q["ones_in"], 64)
            for h in range(PAIRS):
                V.tensor_tensor_scan(cum[:, h, 0:SEQ], restart, sw[:, h, 0:SEQ], 0.0, ALU.mult, ALU.add).then_inc(q["scanned"], 1)
            dve.wait_ge(q["params_done"], 1)
            for h in range(PAIRS):
                last = V.tensor_scalar(tmp_b[:, h, :], ga[:, h, :], par[:, KA + h:KA + h + 1], ka1[:, h:h + 1], ALU.mult, ALU.add)
            link(last)
            link(V.tensor_mul(k, k, tmp_b))
            dve.wait_ge(q["kk_norm"], 1)
            link(V.tensor_scalar(inv, inv, 1e-12, None, ALU.max))
            V.reciprocal(inv, inv).then_inc(q["kk_inverse"], 1)
            for h in range(PAIRS):
                last = V.scalar_tensor_tensor(tmp_a[:, h, :], r[:, h, :], par[:, RK + h:RK + h + 1], k[:, h, :], ALU.mult, ALU.mult)
            last.then_inc(q["bonus_in"], 1)
            dve.wait_ge(q["exp_p"], 1)
            by_tile = lambda x: x[:, :, 0:SEQ].rearrange("p h (t c) -> p h t c", t=NT)
            for h in range(PAIRS):
                last = V.tensor_mul(ar[:, h, :, 1, :], by_tile(r)[:, h], by_tile(tmp_b)[:, h])
            last.then_inc(q["ar_r"], 1)
            V.tensor_copy(pend, tmp_b[:, :, CHUNK - 1:SEQ:CHUNK])
            for h in range(PAIRS):
                dve.wait_ge(q["kk_spread"], h + 1)
                V.tensor_mul(kk[:, h, cols[0]], kk[:, h, cols[0]], m.bank[h][:, :])
            last = V.tensor_mul(kk[:, :, cols[1]], kk[:, :, cols[1]],
                                m.bank[6][:, 0:PAIRS * NB].rearrange("p (h b) -> p h b", h=PAIRS))
            last.then_inc(q["kk_done"], 1)
            dve.wait_ge(q["kk_done"], 1)
            V.tensor_mul(ga, kk, ga).then_inc(q["keys_done"], 1)
            dve.wait_ge(q["bonus_psum"], PAIRS)
            dve.wait_ge(q["sx_psum"], 6)
            dve.wait_ge(q["ar_r"], 1)
            for h in range(PAIRS):
                V.tensor_mul(r[:, h, cols[0]], m.bank[h][:, :], v[:, h, cols[0]])
                last = V.tensor_mul(r[:, h, cols[1]], m.bank[4 + h // 2][:, NB * (h % 2):NB * (h % 2) + NB], v[:, h, cols[1]])
            last.then_inc(q["bonus_done"], 1)
            dve.wait_ge(q["bonus_done"], 1)
            V.tensor_sub(tmp_a[:, :, 0:SEQ], cum[:, :, 0:SEQ], sw[:, :, 0:SEQ]).then_inc(q["pm_ready"], 1)
            dve.wait_ge(q["exp_pm"], 1)
            for h in range(PAIRS):
                last = V.scalar_tensor_tensor(ar[:, h, :, 0, :], by_tile(kk)[:, h], -1.0, by_tile(tmp_a)[:, h], ALU.mult, ALU.mult)
            last.then_inc(q["ar_a"], 1)
            dve.wait_ge(q["exp_m"], 1)
            dve.wait_ge(q["keys_done"], 1)
            V.tensor_mul(bt, ga[:, :, 0:SEQ], tmp_a[:, :, 0:SEQ])
            V.tensor_mul(kt, k[:, :, 0:SEQ], tmp_a[:, :, 0:SEQ]).then_inc(q["b_ready"], 1)
            dve.wait_ge(q["b_ready"], 1)
            ends = pend.unsqueeze(3).broadcast_to([P, PAIRS, SEQ // CHUNK, CHUNK])
            by_chunk = lambda x: x[:, :, 0:SEQ].rearrange("p h (c t) -> p h c t", t=CHUNK)
            for h in range(PAIRS):
                V.tensor_mul(by_chunk(tmp_b)[:, h], by_chunk(kt)[:, h], ends[:, h])
                last = V.tensor_mul(by_chunk(cum)[:, h], by_chunk(bt)[:, h], ends[:, h])
            last.then_inc(q["bar_ready"], 1)
            dve.wait_ge(q["s_ta"], 1)
            V.tensor_reduce(s_sa, s_tmp, AXX, ALU.add).then_inc(q["s_sa_done"], 1)
            dve.wait_ge(q["tok_done"], 4 * NT)
            nsc = nz = nx = 0
            low = m.levels[:, 0:LEVELS * P].rearrange("p (l c) -> p l c", l=LEVELS)
            up = m.levels[:, LEVELS * P:2 * LEVELS * P].rearrange("p (l c) -> p l c", l=LEVELS)
            four = lambda x: x.unsqueeze(1).broadcast_to([P, NT, P])
            for h in range(PAIRS):
                for s in range(2):
                    if h:
                        dve.wait_ge(q["u_mm"], 2 * h)
                    V.tensor_copy(x_inv[s], four(m.ident[:, :]))
                    V.tensor_copy(x_inv_t[s], four(m.ident[:, :])).then_inc(q["x_init"], 1)
                    for t in range(NT):
                        nsc += 1
                        u = (2 * h + s) * NT + t
                        dve.wait_ge(q["score_mm"], nsc)
                        src = m.bank[6 + nsc % 2][:, :].rearrange("p (x y c) -> p x y c", x=2, y=2)
                        V.tensor_mul(lm[s][:, t], src[:, :, 0, :], tri[:, 0, :].unsqueeze(1).broadcast_to([P, 2, P]))
                        V.tensor_mul(nn[:, u], src[:, :, 1, :], tri[:, 1, :].unsqueeze(1).broadcast_to([P, 2, P]))\
                            .then_inc(q["score_masked"], 1)
                for lev in range(LEVELS):
                    for s in range(2):
                        nx += 1
                        bank_of = lambda i: m.bank[3 * s + i][:, :].rearrange("p (t c) -> p t c", t=NT)
                        if lev == 0:
                            dve.wait_ge(q["x_init"], 2 * h + s + 1)
                            dve.wait_ge(q["score_masked"], 8 * h + 4 * s + 4)
                            dve.wait_ge(q["xz_mm"], nx)
                            V.copy_predicated(x_inv[s], four(low[:, 0, :]), bank_of(0)).then_inc(q["x_new"], 1)
                            V.copy_predicated(x_inv_t[s], four(up[:, 0, :]), lm[s][:, :, 0, :]).then_inc(q["xt_new"], 1)
                        else:
                            dve.wait_ge(q["xz_mm"], nx)
                            V.copy_predicated(x_inv[s], four(low[:, lev, :]), bank_of(1)).then_inc(q["x_new"], 1)
                            V.copy_predicated(x_inv_t[s], four(up[:, lev, :]), bank_of(2)).then_inc(q["xt_new"], 1)
            dve.wait_ge(q["u_copied"], 2 * PAIRS)
            dve.wait_ge(q["s_tr"], 1)
            V.tensor_reduce(s_y, s_tmp, AXX, ALU.add).then_inc(q["s_y_done"], 1)
            dve.wait_ge(q["score_mm"], 8 * PAIRS)
            V.memset(state, 0.0).then_inc(q["st_done"], 1)
            for c in range(SEQ // CHUNK):
                t, rows = c // 2, half(c % 2)
                for h in range(PAIRS):
                    i = c * PAIRS + h
                    dve.wait_ge(q["sa_mm"], i + 1)
                    if c >= 2:
                        dve.wait_ge(q["y_mm"], i + 1 - 2 * PAIRS)
                    V.tensor_add(sa[rows, c % 2, h], m.bank[4 + i % 2][rows, 0:2 * HD].rearrange("p (s d) -> p s d", s=2),
                                 u_tok[rows, t, h]).then_inc(q["sa_done"], 1)
                for h in range(PAIRS):
                    i = c * PAIRS + h
                    dve.wait_ge(q["st_mm"], i + 1)
                    if c >= 1:
                        dve.wait_ge(q["y_mm"], i + 1 - PAIRS)
                    dve.wait_ge(q["st_done"], 1 + i - (PAIRS - 1) if c else 1)
                    for s in range(2):
                        last = V.scalar_tensor_tensor(state[half(s), (c + 1) % 2, h, half(s)], state[half(s), c % 2, h, half(s)],
                                                      pend[half(s), h, c:c + 1], m.bank[6 + i % 2][half(s), half(s)],
                                                      ALU.mult, ALU.add)
                    last.then_inc(q["st_done"], 1)
            dve.wait_ge(q["state_psum"], 1)
            V.tensor_copy(tmp_a[:, 0, 0:AW], m.bank[7][:, :]).then_inc(q["state_rows_done"], 1)
            dve.wait_ge(q["y_copied"], 1)
            samples = lambda bank: bank[:, 0:PAIRS * NB].rearrange("p (h b) -> p h b", h=PAIRS)
            for h in range(PAIRS + 1):
                dve.wait_ge(q["mean_mm"], h + 1 if h < PAIRS else PAIRS)
                part, total = (ys[:, h, cols[0]], m.bank[h][:, :]) if h < PAIRS else (ys[:, :, cols[1]], samples(m.bank[4]))
                link(V.scalar_tensor_tensor(part, total, -1.0 / HD, part, ALU.mult, ALU.add))
                V.tensor_mul(y_sq[:, h, cols[0]] if h < PAIRS else y_sq[:, :, cols[1]], part, part).then_inc(q["squared"], 1)
            dve.wait_ge(q["var_mm"], 1)
            V.tensor_scalar(inv[:, cols[0]], m.bank[5][0:NH, :], 1.0 / HD, GN_EPS, ALU.mult, ALU.add)
            link(V.tensor_scalar(inv[:, cols[1]], m.bank[6][0:NH, 0:NB], 1.0 / HD, GN_EPS, ALU.mult, ALU.add))
            V.reciprocal(inv, inv).then_inc(q["var_ready"], 1)
            dve.wait_ge(q["inv_spread"], 1)
            link(V.tensor_mul(ys[:, :, cols[1]], ys[:, :, cols[1]], samples(m.bank[6])))
            for h in range(PAIRS):
                dve.wait_ge(q["inv_spread"], h + 1)
                link(V.tensor_mul(ys[:, h, cols[0]], ys[:, h, cols[0]], m.bank[h][:, :]))
                link(V.tensor_scalar(ys[:, h, :], ys[:, h, :], par[:, LNW + h:LNW + h + 1], par[:, LNB + h:LNB + h + 1],
                                     ALU.mult, ALU.add))
                link(V.tensor_add(ys[:, h, :], ys[:, h, :], r[:, h, :]))
                V.tensor_mul(m.ct[:, 4 + h, :], ys[:, h, :], g[:, h, :])

        @block.tensor
        def _(pe):
            T = nc.tensor
            pe.wait_ge(q["tables_in"], 16 * 8)
            pe.wait_ge(q["state_in"], 16)
            T.transpose(m.bank[0][:, 0:N_PAR], par_rows, m.ident[0:N_PAR, 0:N_PAR])
            for f in range(RF):
                last = T.transpose(m.bank[1][:, f * NB:(f + 1) * NB], sh_rows[:, f * P:(f + 1) * P], m.ident[0:NB, 0:NB])
            last.then_inc(q["params_psum"], 1)
            pe.wait_ge(q["lora_in"], 48)
            pe.wait_ge(q["lora_act"], 2)
            pe.wait_ge(q["params_done"], 1)
            for y in range(3):
                for h in range(PAIRS):
                    i = y * PAIRS + h
                    if i >= 2:
                        pe.wait_ge(q["gates_done"], max(i - 5, i - 1))
                    rows = (slice(0, HD), slice(HD, P), slice(0, P))[y]
                    wts = (lora_wa if y < 2 else lora_g)[rows, h * P:(h + 1) * P]
                    T.matmul(m.bank[i % 6][:, :], wts, xl[rows, y // 2, cols[0]], start=True, stop=True)
                    T.matmul(m.bank[6 + i % 2][:, 0:NB], wts, xl[rows, y // 2, cols[1]], start=True, stop=True).then_inc(q["lora_mm"], 1)
            pe.wait_ge(q["ones_in"], 64)
            pe.wait_ge(q["kk_sq"], 1)
            pe.wait_ge(q["gates_done"], 3 * PAIRS)

            def head_sums(src, prompt, sample, ready=None):
                for h in range(PAIRS):
                    if ready is not None:
                        pe.wait_ge(ready, h + 1)
                    T.matmul(prompt[0:NH, :], head_pick[:, h, :], src[:, h, cols[0]], start=(h == 0), stop=(h == PAIRS - 1))
                if ready is not None:
                    pe.wait_ge(ready, PAIRS + 1)
                for h in range(PAIRS):
                    last = T.matmul(sample[0:NH, 0:NB], head_pick[:, h, :], src[:, h, cols[1]], start=(h == 0),
                                    stop=(h == PAIRS - 1))
                return last

            def spread(done):
                for h in range(PAIRS):
                    T.matmul(m.bank[6][:, h * NB:(h + 1) * NB], head_rows[:, h * P:(h + 1) * P], inv[:, cols[1]],
                             start=True, stop=True)
                for h in range(PAIRS):
                    T.matmul(m.bank[h][:, :], head_rows[:, h * P:(h + 1) * P], inv[:, cols[0]], start=True,
                             stop=True).then_inc(done, 1)

            head_sums(tmp_a, m.bank[4], m.bank[5]).then_inc(q["kk_sum"], 1)
            pe.wait_ge(q["head_rows_in"], 16)
            pe.wait_ge(q["kk_inverse"], 1)
            spread(q["kk_spread"])
            pe.wait_ge(q["keys_done"], 1)
            for i, src in enumerate((r, k, kk, ga, sw, v)):
                for h in range(PAIRS):
                    last = T.transpose(m.bank[i][0:NB, h * P:(h + 1) * P], src[:, h, cols[1]], m.ident[:, :])
                last.then_inc(q["sx_psum"], 1)
            pe.wait_ge(q["bonus_in"], 1)
            pe.wait_ge(q["sx_done"], 6)
            for h in range(PAIRS):
                T.matmul(m.bank[h][:, :], ones_blk, tmp_a[:, h, cols[0]], start=True, stop=True)
                T.matmul(m.bank[4 + h // 2][:, NB * (h % 2):NB * (h % 2) + NB], ones_blk, tmp_a[:, h, cols[1]],
                         start=True, stop=True).then_inc(q["bonus_psum"], 1)
            pe.wait_ge(q["bonus_done"], 1)
            for i in range(4):
                if i == 1:
                    pe.wait_ge(q["ar_a"], 1)
                if i == 2:
                    pe.wait_ge(q["bar_ready"], 1)
                for t in range(NT):
                    n = i * NT + t
                    if n >= 6:
                        pe.wait_ge(q["tok_done"], n - 5)
                    for h in range(PAIRS):
                        src = (v[:, h, t * P:(t + 1) * P], ar[:, h, t, 0, :], tmp_b[:, h, t * P:(t + 1) * P],
                               cum[:, h, t * P:(t + 1) * P])[i]
                        last = T.transpose(m.bank[n % 6][:, h * P:(h + 1) * P], src, m.ident[:, :])
                    last.then_inc(q["tok_psum"], 1)
            pe.wait_ge(q["tok_done"], 4 * NT)
            nsc = nz = nx = 0
            for h in range(PAIRS):
                if h:
                    pe.wait_ge(q["u_copied"], 2 * h)
                for s in range(2):
                    for t in range(NT):
                        nsc += 1
                        if nsc >= 3:
                            pe.wait_ge(q["score_masked"], nsc - 2)
                        bank = m.bank[6 + nsc % 2]
                        rhs = ar[half(s), h, t].rearrange("p x c -> p (x c)")
                        T.matmul(bank[:, 0:2 * P], bt[half(s), h, t * P:(t + 1) * P], rhs, start=True, stop=True)
                        T.matmul(bank[:, 2 * P:4 * P], kt[half(s), h, t * P:(t + 1) * P], rhs, start=True, stop=True)\
                            .then_inc(q["score_mm"], 1)
                for lev in range(LEVELS):
                    if lev == 0:
                        for s in range(2):
                            nx += 1
                            pe.wait_ge(q["score_masked"], 8 * h + 4 * s + 4)
                            for t in range(NT):
                                last = T.matmul(m.bank[3 * s][:, t * P:(t + 1) * P], lm[s][:, t, 0, :], m.ident[:, :],
                                                start=True, stop=True)
                            last.then_inc(q["xz_mm"], 1)
                        continue
                    for s in range(2):
                        pe.wait_ge(q["x_new"], nx - 1 + s)
                        pe.wait_ge(q["xt_new"], nx - 1 + s)
                        for t in range(NT):
                            last = T.matmul(m.bank[3 * s][:, t * P:(t + 1) * P], lm[s][:, t, 0, :], x_inv[s][:, t, :],
                                            start=True, stop=True)
                        last.then_inc(q["z_mm"], 1)
                    for s in range(2):
                        nz += 1
                        nx += 1
                        pe.wait_ge(q["z_copied"], nz)
                        for t in range(NT):
                            T.matmul(m.bank[3 * s + 1][:, t * P:(t + 1) * P], x_inv_t[s][:, t, :], z[s][:, t, :],
                                     start=True, stop=True)
                            last = T.matmul(m.bank[3 * s + 2][:, t * P:(t + 1) * P], z[s][:, t, :], x_inv_t[s][:, t, :],
                                            start=True, stop=True)
                        last.then_inc(q["xz_mm"], 1)
                for s in range(2):
                    i = 2 * h + s
                    pe.wait_ge(q["xt_new"], LEVELS * 2 * h + 2 * (LEVELS - 1) + s + 1)
                    for t in range(NT):
                        last = T.matmul(m.bank[3 * s][:, t * HD:(t + 1) * HD], lm[s][:, t, 1, :],
                                        v_tok[:, t, h * P + s * HD:h * P + (s + 1) * HD], start=True, stop=True)
                    last.then_inc(q["mv_mm"], 1)
                    for t in range(NT):
                        last = T.matmul(m.bank[3 * s + 1][half(s), t * P:(t + 1) * P],
                                        a_tok[:, t, h * P + s * HD:h * P + (s + 1) * HD], x_inv_t[s][:, t, :],
                                        start=True, stop=True)
                    last.then_inc(q["wt_mm"], 1)
                for s in range(2):
                    i = 2 * h + s
                    pe.wait_ge(q["mv_copied"], i + 1)
                    for t in range(NT):
                        last = T.matmul(m.bank[3 * s + 2][:, t * HD:(t + 1) * HD], x_inv_t[s][:, t, :], mv[s][:, t, :],
                                        start=True, stop=True)
                    last.then_inc(q["u_mm"], 1)
            pe.wait_ge(q["u_copied"], 2 * PAIRS)
            pe.wait_ge(q["score_masked"], 8 * PAIRS)
            for c in range(SEQ // CHUNK):
                t, rows = c // 2, half(c % 2)
                tc = slice(c * CHUNK, (c + 1) * CHUNK)
                for h in range(PAIRS):
                    i = c * PAIRS + h
                    pe.wait_ge(q["st_done"], 1 + max(0, i - PAIRS + 1) if c else 1)
                    if i >= 2:
                        pe.wait_ge(q["sa_done"], i - 1)
                    T.matmul(m.bank[4 + i % 2][rows, 0:P], wt[:, h, tc], state[:, c % 2, h, :], start=True,
                             stop=True).then_inc(q["sa_mm"], 1)
                for h in range(PAIRS):
                    i = c * PAIRS + h
                    pe.wait_ge(q["sa_done"], i + 1)
                    if i >= 2:
                        pe.wait_ge(q["st_done"], i)
                    both = slice(h * P, (h + 1) * P)
                    T.matmul(m.bank[6 + i % 2][:, 0:P], b_tok[rows, t, both], sa[rows, c % 2, h].rearrange("p s d -> p (s d)"),
                             start=True, stop=False)
                    T.matmul(m.bank[6 + i % 2][:, 0:P], k_tok[rows, t, both], v_tok[rows, t, both],
                             start=False, stop=True).then_inc(q["st_mm"], 1)
                    qc = half(c % 2)
                    T.matmul(m.bank[h][:, tc], state[:, c % 2, h, :], ar[:, h, t, 1, qc], start=True, stop=False)
                    for s in range(2):
                        fs = slice(h * P + s * HD, h * P + (s + 1) * HD)
                        u = (2 * h + s) * NT + t
                        out = m.bank[h][half(s), tc]
                        T.matmul(out, sa[rows, c % 2, h, s, :], nn[rows, u, 0, qc], start=False, stop=False)
                        last = T.matmul(out, v_tok[rows, t, fs], nn[rows, u, 1, qc], start=False, stop=True)
                    last.then_inc(q["y_mm"], 1)
            pe.wait_ge(q["st_done"], 1 + 8 * PAIRS)
            for h in range(PAIRS):
                last = T.transpose(m.bank[7][:, h * P:(h + 1) * P], state[:, 0, h, :], m.ident[:, :])
            last.then_inc(q["state_psum"], 1)
            pe.wait_ge(q["s_y_in"], 16)
            for h in range(PAIRS):
                last = T.transpose(m.bank[6][:, h * NB:(h + 1) * NB], y_rows[:, h * P:(h + 1) * P], m.ident[0:NB, 0:NB])
            last.then_inc(q["s_y_psum"], 1)
            pe.wait_ge(q["y_copied"], 1)
            for h in range(PAIRS):
                T.matmul(m.bank[h][:, :], ones_blk, ys[:, h, cols[0]], start=True, stop=True)
                T.matmul(m.bank[4][:, NB * h:NB * h + NB], ones_blk, ys[:, h, cols[1]], start=True,
                         stop=True).then_inc(q["mean_mm"], 1)
            head_sums(y_sq, m.bank[5], m.bank[6], ready=q["squared"]).then_inc(q["var_mm"], 1)
            pe.wait_ge(q["root_done"], 1)
            spread(q["inv_spread"])


BLK = P
MORE = (TOK * TOPK - 1) // BLK
BLOCKS = EXPERTS + MORE
GUP = 3


def mix_and_route(nc, io, m):
    with ExitStack() as ctx:
        sem = lambda n: m.sem("mr_" + n)
        w = Arena(m.wring)
        w.at = 2 * SLOT
        b_raw = w.take(3 * D, rows=EXPERTS)
        b_rest = w.take(3 * D, rows=EXPERTS)
        b_part = [w.take(3 * D // 2, rows=EXPERTS).bitcast(BF16) for _ in range(GUP)]
        a = Arena(m.arena)
        a.at = m.x2_at + (NT + 1) * D
        row_p = a.take(3, D)
        row_s = a.take(3, D, rows=NB)
        xin = a.take(2, D)
        h2 = a.take(2, D)
        h2t = a.take(KT, P)
        rw = a.take(KT, EXPERTS)
        rb = a.take(EXPERTS)
        lg = a.take(EXPERTS)
        route = a.take(EXPERTS + MORE + NT + 1)
        tri = a.take(P)
        ones = a.take(P)
        hot = a.take((NT + 1) * TOPK, EXPERTS)
        chosen = a.take(NT + 1, EXPERTS)
        rank = a.take(NT + 1, EXPERTS)
        slot_of = a.take(NT + 1, EXPERTS)
        prod = a.take((NT + 1) * TOPK, EXPERTS)
        over = a.take(6, EXPERTS)
        ocmp = a.take(MORE, EXPERTS)
        top8 = a.take(8)
        idx8 = a.take(8).bitcast(mybir.dt.uint32)
        idxf = a.take(TOPK)
        slotf = a.take((NT + 1) * TOPK)
        oexpf = a.take(MORE)
        ss = a.take(NT + 1)
        rstd = a.take(NT + 1)
        ntop = a.take(1)
        zeros = a.take(P, rows=BLOCKS + 1)
        tab = a.take(P, rows=BLOCKS + 1)
        names = ("rows_in consts_in wout_in0 wout_in1 bias_in out_mm x2_done squared ms_done root_done h2_done h2_out "
                 "h2t_psum h2t_copied logit_mm logit_read top_done exp_done chosen_done rank_mm rank_read count_mm slots_done "
                 "own zero_set zero_out x2_out scattered tab_in tab_psum idx_done b_hi b_mid b_r1 b_r2 b_lo b_out ones_set").split()
        q = dict({n: sem(n) for n in names if n not in ("scattered", "h2_out")}, scattered=m.scattered,
                 h2_out=[sem(f"h2_out{i}") for i in range(2)])
        x_in = [sem(f"x_in{i}") for i in range(2)]
        e_of, ob_of, tok_of = route[:, 0:EXPERTS], route[:, EXPERTS:EXPERTS + MORE], route[:, EXPERTS + MORE:]
        block = ctx.enter_context(nc.Block())

        @block.sync
        def _(sp):
            def h2_rows_out(t):
                r = rows_of(t)
                sp.wait_ge(q["h2_done"], t + 1)
                sp.dma_start(m.x2_dram[t * P:t * P + r, :], m.x2[0:r, t, :]).then_inc(q["x2_out"], 16)
                sp.dma_start(m.h2_dram[t * P:t * P + r, :], h2[0:r, t % 2, :]).then_inc(q["h2_out"][t % 2], 16)

            for j, landed in enumerate((q["wout_in0"], q["wout_in1"])):
                sp.dma_start(slot_view(m.wring, j), wide(io["w_out"][0], j * 512)).then_inc(landed, 16)
            for i, part in enumerate((2, 3, 4)):
                row = m.mod_dram[NB:NB + 1, part * D:(part + 1) * D]
                sp.dma_start(row_p[:, i, :], row.broadcast_to([P, D])).then_inc(q["rows_in"], 16)
                sp.dma_start(row_s[:, i, :], m.mod_dram[0:NB, part * D:(part + 1) * D]).then_inc(q["rows_in"], 16)
            sp.wait_ge(q["zero_set"], 1)
            sp.dma_start(m.tab_dram.rearrange("(b p) o -> b (p o)", p=P), zeros).then_inc(q["zero_out"], 16)
            sp.dma_start(b_raw[:, 0:2 * D], io["moe_b_gu"][0]).then_inc(q["bias_in"], 16)
            sp.dma_start(b_raw[:, 2 * D:], io["moe_b_down"][0]).then_inc(q["bias_in"], 16)
            for t in range(NT + 1):
                r = rows_of(t)
                if t >= 2:
                    sp.wait_ge(q["x2_done"], 2 * (t - 1))
                src = io["x_prompt"][0, t * P:(t + 1) * P, :] if t < NT else io["x_sample"][:, 0, :]
                sp.dma_start(xin[0:r, t % 2, :], src).then_inc(x_in[t % 2], 16)
                if t >= 2:
                    h2_rows_out(t - 2)
            h2_rows_out(NT - 1)
            h2_rows_out(NT)
            sp.wait_ge(q["b_lo"], 1)
            for i in range(GUP):
                sp.dma_start(m.bias_dram[:, i, :], b_part[i]).then_inc(q["b_out"], 16)
            sp.wait_ge(q["b_out"], 16 * GUP)
            for j in range(NSLOT):
                load_piece(sp, io, m, 0, j)
            sp.wait_ge(q["scattered"], 16 * (NT + 1) * TOPK)
            sp.dma_start(tab, m.tab_dram.rearrange("(b p) o -> b (p o)", p=P)).then_inc(q["tab_in"], 16)
            sp.wait_ge(q["x2_out"], 16 * (NT + 1))
            for i in range(2):
                sp.wait_ge(q["h2_out"][i], 16 * ((NT + 2 - i) // 2))

        @block.gpsimd
        def _(pool):
            nc.gpsimd.memset(zeros, 0.0).then_inc(q["zero_set"], 1)
            nc.gpsimd.memset(ones, 1.0).then_inc(q["ones_set"], 1)
            pool.wait_ge(q["b_hi"], 1)
            nc.gpsimd.tensor_tensor(b_rest, b_raw, b_part[0], ALU.subtract).then_inc(q["b_r1"], 1)
            pool.wait_ge(q["b_mid"], 1)
            nc.gpsimd.tensor_tensor(b_raw, b_rest, b_part[1], ALU.subtract).then_inc(q["b_r2"], 1)
            pool.wait_ge(q["zero_out"], 16)
            pool.wait_ge(q["slots_done"], 1)
            for t in range(NT + 1):
                r = rows_of(t)
                for c in range(TOPK):
                    i = t * TOPK + c
                    nc.gpsimd.indirect_dma_start(out=m.tab_dram, out_offset=bass.IndirectOffsetOnAxis(ap=m.slots[0:r, i:i + 1], axis=0),
                                                 in_=tok_of[0:r, t:t + 1], in_offset=None).then_inc(q["scattered"], 16)

        @block.scalar
        def _(act):
            act.dma_start(rw, io["router_w"][0].rearrange("(k p) e -> p k e", p=P)).then_inc(q["consts_in"], 16)
            act.dma_start(rb, io["router_b"].broadcast_to([P, EXPERTS])).then_inc(q["consts_in"], 16)
            act.dma_start(route, io["route"]).then_inc(q["consts_in"], 16)
            act.dma_start(tri, io["rank_tri"]).then_inc(q["consts_in"], 16)
            act.wait_ge(q["bias_in"], 32)
            nc.scalar.copy(b_part[0], b_raw).then_inc(q["b_hi"], 1)
            for t in range(NT + 1):
                r = rows_of(t)
                act.wait_ge(q["x2_done"], 2 * (t + 1))
                if t >= 2:
                    act.wait_ge(q["h2_out"][t % 2], 16 * (t // 2))
                    act.wait_ge(q["h2t_psum"], t - 1)
                nc.scalar.activation(h2[0:r, t % 2, :], m.x2[0:r, t, :], ACT.Square, accum_out=ss[0:r, t:t + 1]).then_inc(q["squared"], 1)
                act.wait_ge(q["ms_done"], t + 1)
                nc.scalar.activation(rstd[0:r, t:t + 1], rstd[0:r, t:t + 1], ACT.Sqrt).then_inc(q["root_done"], 1)
                act.wait_ge(q["h2t_psum"], t + 1)
                for half in range(2):
                    last = nc.scalar.copy(h2t[:, 4 * half:4 * half + 4, 0:r],
                                          m.bank[4 + half][:, 0:4 * r].rearrange("p (k c) -> p k c", k=4))
                last.then_inc(q["h2t_copied"], 1)
                act.wait_ge(q["top_done"], t + 1)
                nc.scalar.activation(m.weights[0:r, t * TOPK:(t + 1) * TOPK], top8[0:r, 0:TOPK], ACT.Exp,
                                     bias=ntop[0:r, :], accum_out=ss[0:r, t:t + 1]).then_inc(q["exp_done"], 1)
                if t == 0:
                    act.wait_ge(q["b_r1"], 1)
                    nc.scalar.copy(b_part[1], b_rest).then_inc(q["b_mid"], 1)
                if t == 1:
                    act.wait_ge(q["b_r2"], 1)
                    nc.scalar.copy(b_part[2], b_raw).then_inc(q["b_lo"], 1)
            act.wait_ge(q["tab_psum"], 1)
            nc.scalar.copy(m.gather_idx[:, :], m.bank[0][:, 0:BLOCKS + 1]).then_inc(q["idx_done"], 1)

        @block.vector
        def _(dve):
            n_own = [0]

            def link(ins):
                n_own[0] += 1
                ins.then_inc(q["own"], 1)
                dve.wait_ge(q["own"], n_own[0])

            V = nc.vector
            link(V.memset(hot, 0.0))
            link(V.memset(rank, 0.0))
            link(V.memset(m.weights[:, :], 0.0))
            dve.wait_ge(q["rows_in"], 96)
            dve.wait_ge(q["consts_in"], 64)

            def rows_for(t):
                return row_p if t < NT else row_s

            def x2_tile(t):
                r = rows_of(t)
                for n in range(2):
                    c = slice(n * 512, (n + 1) * 512)
                    dve.wait_ge(q["out_mm"], 2 * t + n + 1)
                    link(V.tensor_mul(m.x2[0:r, t, c], m.bank[(2 * t + n) % 4][0:r, :], rows_for(t)[0:r, 0, c]))
                    dve.wait_ge(x_in[t % 2], 16 * (t // 2 + 1))
                    V.tensor_add(m.x2[0:r, t, c], m.x2[0:r, t, c], xin[0:r, t % 2, c]).then_inc(q["x2_done"], 1)

            def norm_tile(t):
                r = rows_of(t)
                rows = rows_for(t)
                dve.wait_ge(q["squared"], t + 1)
                link(V.tensor_scalar(rstd[0:r, t:t + 1], ss[0:r, t:t + 1], 1.0 / D, NORM_EPS, ALU.mult, ALU.add))
                V.reciprocal(rstd[0:r, t:t + 1], rstd[0:r, t:t + 1]).then_inc(q["ms_done"], 1)
                dve.wait_ge(q["root_done"], t + 1)
                link(V.scalar_tensor_tensor(h2[0:r, t % 2, :], m.x2[0:r, t, :], rstd[0:r, t:t + 1], rows[0:r, 2, :],
                                            ALU.mult, ALU.mult))
                V.tensor_add(h2[0:r, t % 2, :], h2[0:r, t % 2, :], rows[0:r, 1, :]).then_inc(q["h2_done"], 1)

            def rank_tile(t):
                r = rows_of(t)
                dve.wait_ge(q["rank_mm"], t + 1)
                V.tensor_copy(rank[0:r, t, :], m.bank[7][0:r, 0:EXPERTS]).then_inc(q["rank_read"], 1)

            x2_tile(0)
            for t in range(NT + 1):
                r = rows_of(t)
                norm_tile(t)
                if t < NT:
                    x2_tile(t + 1)
                dve.wait_ge(q["logit_mm"], t + 1)
                link(V.tensor_add(lg[0:r, :], m.bank[6][0:r, 0:EXPERTS], rb[0:r, :]))
                if t:
                    dve.wait_ge(q["exp_done"], t)
                link(V.max(top8[0:r, :], lg[0:r, :]))
                link(V.max_index(idx8[0:r, :], top8[0:r, :], lg[0:r, :]))
                V.tensor_scalar(ntop[0:r, :], top8[0:r, 0:1], -1.0, None, ALU.mult).then_inc(q["top_done"], 1)
                link(V.tensor_copy(idxf[0:r, :], idx8[0:r, 0:TOPK]))
                mine = hot[0:r, t * TOPK:(t + 1) * TOPK, :]
                link(V.tensor_tensor(mine, e_of[0:r, :].unsqueeze(1).broadcast_to([r, TOPK, EXPERTS]),
                                     idxf[0:r, :].unsqueeze(2).broadcast_to([r, TOPK, EXPERTS]), ALU.is_equal))
                V.tensor_reduce(chosen[0:r, t, :], mine.rearrange("p c e -> p e c"), AXX, ALU.add).then_inc(q["chosen_done"], 1)
                dve.wait_ge(q["exp_done"], t + 1)
                link(V.reciprocal(ss[0:r, t:t + 1], ss[0:r, t:t + 1]))
                wt = m.weights[0:r, t * TOPK:(t + 1) * TOPK]
                link(V.tensor_scalar(wt, wt, ss[0:r, t:t + 1], None, ALU.mult))
                if t:
                    rank_tile(t - 1)
            rank_tile(NT)
            dve.wait_ge(q["rank_read"], NT + 1)
            dve.wait_ge(q["count_mm"], 1)
            link(V.tensor_copy(over[:, 0, :], m.bank[6][:, 0:EXPERTS]))
            link(V.tensor_scalar(over[:, 1, :], over[:, 0, :], float(BLK), None, ALU.is_gt))
            for j in range(2, TOK // BLK + 1):
                link(V.scalar_tensor_tensor(over[:, 1, :], over[:, 0, :], float(BLK * j), over[:, 1, :], ALU.is_gt, ALU.add))
            link(V.tensor_tensor_scan(over[:, 2, :], ones[:, 0:EXPERTS], over[:, 1, :], 0.0, ALU.mult, ALU.add))
            link(V.tensor_sub(over[:, 3, :], over[:, 2, :], over[:, 1, :]))
            link(V.tensor_sub(over[:, 3, :], over[:, 3, :], e_of))
            link(V.tensor_scalar(over[:, 3, :], over[:, 3, :], float(EXPERTS - 1), float(BLK), ALU.add, ALU.mult))
            link(V.tensor_scalar(over[:, 4, :], e_of, float(BLK), None, ALU.mult))
            per_tile = lambda x: x.unsqueeze(1).broadcast_to([P, NT + 1, EXPERTS])
            link(V.scalar_tensor_tensor(slot_of, rank, float(BLK), per_tile(over[:, 3, :]), ALU.is_ge, ALU.mult))
            link(V.tensor_add(slot_of, slot_of, rank))
            link(V.tensor_add(slot_of, slot_of, per_tile(over[:, 4, :])))
            link(V.tensor_mul(prod.rearrange("p (t c) e -> p t c e", c=TOPK), hot.rearrange("p (t c) e -> p t c e", c=TOPK),
                              slot_of.unsqueeze(2).broadcast_to([P, NT + 1, TOPK, EXPERTS])))
            link(V.tensor_reduce(slotf, prod, AXX, ALU.add))
            V.tensor_copy(m.slots[:, :], slotf).then_inc(q["slots_done"], 1)
            link(V.tensor_tensor(ocmp, over[:, 2, :].unsqueeze(1).broadcast_to([P, MORE, EXPERTS]),
                                 ob_of.unsqueeze(2).broadcast_to([P, MORE, EXPERTS]), ALU.is_le))
            link(V.tensor_reduce(oexpf, ocmp, AXX, ALU.add))
            link(V.tensor_scalar(oexpf, oexpf, float(EXPERTS - 1), None, ALU.min))
            link(V.tensor_copy(m.more_expert[:, 0:MORE], oexpf))
            link(V.tensor_copy(m.more_expert[:, MORE:MORE + 1], over[:, 2, EXPERTS - 1:EXPERTS]))

        @block.tensor
        def _(pe):
            T = nc.tensor

            def out_tile(t):
                r = rows_of(t)
                for n in range(2):
                    i = 2 * t + n
                    pe.wait_ge((q["wout_in0"], q["wout_in1"])[n], 16)
                    if i >= 4:
                        pe.wait_ge(q["x2_done"], i - 3)
                    for k in range(KT):
                        last = T.matmul(m.bank[i % 4][0:r, :], m.ct[:, k, cols_of(t)], slot_view(m.wring, n)[:, k, :],
                                        start=(k == 0), stop=(k == KT - 1))
                    last.then_inc(q["out_mm"], 1)

            def logits_tile(t):
                r = rows_of(t)
                pe.wait_ge(q["h2_done"], t + 1)
                if t:
                    pe.wait_ge(q["h2t_copied"], t)
                for k in range(KT):
                    last = T.transpose(m.bank[4 + k // 4][:, (k % 4) * r:(k % 4 + 1) * r], h2[0:r, t % 2, k * P:(k + 1) * P],
                                       m.ident[0:r, 0:r])
                last.then_inc(q["h2t_psum"], 1)
                pe.wait_ge(q["h2t_copied"], t + 1)
                for k in range(KT):
                    last = T.matmul(m.bank[6][0:r, 0:EXPERTS], h2t[:, k, 0:r], rw[:, k, :], start=(k == 0), stop=(k == KT - 1))
                last.then_inc(q["logit_mm"], 1)

            def rank_tile(t):
                r = rows_of(t)
                pe.wait_ge(q["chosen_done"], t + 1)
                if t:
                    pe.wait_ge(q["rank_read"], t)
                for j in range(t):
                    T.matmul(m.bank[7][0:r, 0:EXPERTS], ones[:, 0:r], chosen[:, j, :], start=(j == 0), stop=False)
                T.matmul(m.bank[7][0:r, 0:EXPERTS], tri[0:r, 0:r], chosen[0:r, t, :], start=(t == 0), stop=True)\
                    .then_inc(q["rank_mm"], 1)

            out_tile(0)
            pe.wait_ge(q["consts_in"], 64)
            pe.wait_ge(q["ones_set"], 1)
            for t in range(NT + 1):
                if t < NT:
                    out_tile(t + 1)
                logits_tile(t)
                if t:
                    rank_tile(t - 1)
            rank_tile(NT)
            for j in range(NT + 1):
                r = rows_of(j)
                last = T.matmul(m.bank[6][:, 0:EXPERTS], ones[0:r, :], chosen[0:r, j, :], start=(j == 0), stop=(j == NT))
            last.then_inc(q["count_mm"], 1)
            pe.wait_ge(q["tab_in"], 16)
            pe.wait_ge(q["x2_done"], 2 * (NT + 1))
            T.transpose(m.bank[0][:, 0:BLOCKS + 1], tab, m.ident[0:BLOCKS + 1, 0:BLOCKS + 1]).then_inc(q["tab_psum"], 1)


F32R = mybir.dt.float32r
CH = 2048
CHUNKS = NSLOT * SLOT // CH
SPLIT_RING = 4

POOL_CHUNKS = CHUNKS // 4
VEC_CHUNKS = CHUNKS - POOL_CHUNKS


def nth_vec(i):
    return i + 1 - i // 4


def raw_slots(m):
    return m.wring.rearrange("p (j n) -> p j n", j=NSLOT)


def load_piece(sp, io, m, e, j):
    kh = j % 2
    if j < 4:
        c = j // 2
        src = io["moe_w_gu"][0].rearrange("e (k p) (g n) -> e p k g n", p=P, g=2)
        slot = raw_slots(m)[:, j, :].rearrange("p (k g n) -> p k g n", k=4, g=2)
        for g in range(2):
            part = src[bass.ds(e, 1), :, 4 * kh:4 * kh + 4, g, c * 512:(c + 1) * 512]
            sp.dma_start(slot[:, :, g, :], part.rearrange("e p k n -> (e p) k n")).then_inc(m.piece_in[j], 16)
    else:
        src = io["moe_w_down"][0].rearrange("e (k p) n -> e p k n", p=P)[bass.ds(e, 1), :, 4 * kh:4 * kh + 4, :]
        slot = raw_slots(m)[:, j, :].rearrange("p (k n) -> p k n", k=4)
        sp.dma_start(slot, src.rearrange("e p k n -> (e p) k n")).then_inc(m.piece_in[j], 16)


def experts(nc, io, m):
    LIMIT, ALPHA = 7.0, 1.702
    with ExitStack() as ctx:
        sem = lambda n: m.sem("ex_" + n)
        sb = lambda n, size, dt=F32: Arena(ctx.enter_context(nc.sbuf_tensor("ex_" + n, [P, size], dt)))
        raw = raw_slots(m)
        w_hi, w_lo = (sb(n, SPLIT_RING * CH, F32R).take(SPLIT_RING, CH) for n in ("weights_hi", "weights_lo"))
        x_parts = sb("rows_hi_lo", 4 * D, F32R)
        xt_hi, xt_lo = x_parts.take(KT, P), x_parts.take(KT, P)
        act_hi, act_lo = x_parts.take(KT, P), x_parts.take(KT, P)
        a = sb("plain", 5 * D + D // 2)
        xg = a.take(D)
        gate = a.take(2, 512)
        up = a.take(2, 512)
        sig = a.take(2, 512)
        y = a.take(D)
        down_bias = a.take(D // 2, rows=GUP).bitcast(BF16)
        gu_bias = m.small.take(D, rows=GUP).bitcast(BF16)
        ones3 = m.small.take(P // 2, rows=GUP).bitcast(BF16)
        idx = m.small.take(1).bitcast(I32)
        turn = m.small.take(1)
        names = ("gu_bias_in gu_bias_free down_bias_in down_bias_free ones_set idx_copied xg_in xt_psum xt_hi_done xt_lo_done chunk_used hi_done lo_done pool_lo_done "
                 "gu_free0 gu_free1 gate_done sig_done prod_done up_done act_done actt_psum actt_hi_done actt_lo_done "
                 "y_copied y_out").split()
        q = dict({n: sem(n) for n in names if n != "xg_in"}, xg_in=m.xg_in)
        gu_free = (q["gu_free0"], q["gu_free1"])
        piece_in = m.piece_in
        chunk = lambda i: raw[:, i // 2, (i % 2) * CH:(i % 2 + 1) * CH]
        plain = lambda v: v.bitcast(F32)
        four = lambda v, i: v[:, 4 * i:4 * i + 4, :].rearrange("p k c -> p (k c)")
        block = ctx.enter_context(nc.Block())

        def all_blocks(engine, first, body):
            first(0)
            with engine.Fori(0, EXPERTS - 1) as b:
                body(b, False, True)
            body(EXPERTS - 1, False, False)
            more = engine.value_load(m.more_expert[0:1, MORE:MORE + 1], min_val=0, max_val=MORE)
            with engine.If(more > 0):
                first(EXPERTS)
                with engine.Fori(EXPERTS, BLOCKS - 1) as b:
                    body(b, True, True)
                body(BLOCKS - 1, True, False)

        @block.sync
        def _(sp):
            def load_bias(b, e, down):
                rows = m.bias_dram[bass.ds(e, 1), :, :].rearrange("e i n -> (e i) n")
                free, dst, cols, landed = ((q["gu_bias_free"], gu_bias, slice(0, 2 * D), q["gu_bias_in"]),
                                           (q["down_bias_free"], down_bias, slice(2 * D, 3 * D), q["down_bias_in"]))[down]
                sp.wait_ge(free, b + 1)
                sp.dma_start(dst, rows[:, cols]).then_inc(landed, 16)

            def load(b, further):
                e = b
                if further:
                    e = sp.value_load(m.more_expert[0:1, bass.ds(b - EXPERTS, 1)], min_val=0, max_val=EXPERTS - 1)
                for j in range(NSLOT):
                    if j in (2, 4):
                        load_bias(b, e, j == 4)
                    if j % 2:
                        sp.wait_ge(q["pool_lo_done"], POOL_CHUNKS * b + j // 2 + 1)
                    else:
                        sp.wait_ge(q["lo_done"], VEC_CHUNKS * b + nth_vec(2 * j + 1))
                    load_piece(sp, io, m, e, j)

            def first(b):
                if b == 0:
                    load_bias(0, 0, False)
                    load_bias(0, 0, True)
                else:
                    load(b, True)

            def body(b, further, ahead):
                if ahead:
                    load(b + 1, further)

            all_blocks(sp, first, body)

        @block.gpsimd
        def _(pool):
            nc.gpsimd.memset(ones3, 1.0).then_inc(q["ones_set"], 1)
            nc.gpsimd.memset(turn, 0.0).then_inc(q["ones_set"], 1)
            nc.gpsimd.memset(y, 0.0).then_inc(q["ones_set"], 1)
            pool.wait_ge(q["ones_set"], 3)
            pool.sem_inc(q["pool_lo_done"], POOL_CHUNKS)

            def gather(b):
                pool.wait_ge(q["xt_psum"], 2 * b + 2)
                nc.gpsimd.tensor_copy(idx, m.gather_idx[:, bass.ds(b, 1)]).then_inc(q["idx_copied"], 1)
                pool.wait_ge(q["idx_copied"], b + 1)
                nc.gpsimd.tensor_tensor(turn, turn, turn, ALU.mult)
                nc.gpsimd.indirect_dma_start(out=xg, out_offset=None, in_=m.h2_dram,
                                             in_offset=bass.IndirectOffsetOnAxis(ap=idx, axis=0)).then_inc(q["xg_in"], 16)

            def split_lo(b, i):
                pool.wait_ge(q["lo_done"], VEC_CHUNKS * (b + 1) + nth_vec(i - 1))
                pool.wait_ge(q["hi_done"], CHUNKS * b + i + 1)
                nc.gpsimd.tensor_tensor(w_lo[:, i % SPLIT_RING, :], chunk(i), plain(w_hi[:, i % SPLIT_RING, :]), ALU.subtract)\
                    .then_inc(q["pool_lo_done"], 1)

            def first(b):
                gather(b)
                split_lo(b, 3)

            def body(b, further, ahead):
                if ahead:
                    gather(b + 1)
                split_lo(b, 7)
                split_lo(b, 11)
                if ahead:
                    split_lo(b + 1, 3)

            all_blocks(pool, first, body)

        def piece_landed(engine, b, i):
            j = i // 2
            engine.wait_ge(piece_in[j], (32 if j < 4 else 16) * (b + 1))

        @block.scalar
        def _(act):
            def split_hi(b, *chunks):
                for i in chunks:
                    piece_landed(act, b, i)
                    act.wait_ge(q["chunk_used"], CHUNKS * (b + 1) + i + 1 - SPLIT_RING)
                    nc.scalar.copy(w_hi[:, i % SPLIT_RING, :], chunk(i)).then_inc(q["hi_done"], 1)

            def xt_half(b, i):
                act.wait_ge(q["xt_psum"], 2 * b + i + 3)
                nc.scalar.copy(four(xt_hi, i), m.bank[6 + i][:, :]).then_inc(q["xt_hi_done"], 1)

            def act_half(b, c):
                act.wait_ge(q["actt_psum"], 2 * b + c + 1)
                nc.scalar.copy(four(act_hi, c), m.bank[6 + c][:, :]).then_inc(q["actt_hi_done"], 1)

            def sigmoid(b, c):
                act.wait_ge(q["gate_done"], 2 * b + c + 1)
                nc.scalar.activation(sig[:, c, :], gate[:, c, :], ACT.Sigmoid, scale=ALPHA).then_inc(q["sig_done"], 1)

            def first(b):
                xt_half(b, 0)
                xt_half(b, 1)
                split_hi(b, 0, 1, 2, 3)

            def body(b, further, ahead):
                split_hi(b, 4, 5, 6, 7)
                sigmoid(b, 0)
                split_hi(b, 8, 9)
                act_half(b, 0)
                split_hi(b, 10)
                sigmoid(b, 1)
                split_hi(b, 11)
                act_half(b, 1)
                if ahead:
                    split_hi(b + 1, 0)
                    xt_half(b + 1, 0)
                    split_hi(b + 1, 1)
                    xt_half(b + 1, 1)
                    split_hi(b + 1, 2)
                act.wait_ge(q["y_out"], 16 * (b + 1))
                act.wait_ge(q["chunk_used"], CHUNKS * (b + 2))
                nc.scalar.copy(y[:, 0:512], m.bank[4][:, :])
                nc.scalar.copy(y[:, 512:], m.bank[5][:, :]).then_inc(q["y_copied"], 1)
                act.wait_ge(q["y_copied"], b + 1)
                act.dma_start(m.y_dram[bass.ds(b * BLK, BLK), :], y).then_inc(q["y_out"], 16)
                if ahead:
                    split_hi(b + 1, 3)
                else:
                    act.wait_ge(q["y_out"], 16 * (b + 2))

            act.wait_ge(q["ones_set"], 3)
            act.dma_start(m.y_dram[0:1, :], y[0:1, :]).then_inc(q["y_out"], 16)
            all_blocks(act, first, body)

        @block.vector
        def _(dve):
            V = nc.vector

            def split_lo(b, *chunks):
                for i in chunks:
                    dve.wait_ge(q["hi_done"], CHUNKS * b + i + 1)
                    V.tensor_sub(w_lo[:, i % SPLIT_RING, :], chunk(i), plain(w_hi[:, i % SPLIT_RING, :])).then_inc(q["lo_done"], 1)

            def xt_half(b, i):
                dve.wait_ge(q["xt_hi_done"], 2 * b + i + 1)
                V.tensor_sub(four(xt_lo, i), m.bank[6 + i][:, :], plain(four(xt_hi, i))).then_inc(q["xt_lo_done"], 1)

            def act_half(b, c):
                dve.wait_ge(q["actt_hi_done"], 2 * b + c + 1)
                V.tensor_sub(four(act_lo, c), m.bank[6 + c][:, :], plain(four(act_hi, c))).then_inc(q["actt_lo_done"], 1)

            def clamp(b, c):
                dve.wait_ge(q["chunk_used"], CHUNKS * (b + 1) + 4 * c + 4)
                V.tensor_scalar(gate[:, c, :], m.bank[2 * c][:, :], LIMIT, None, ALU.min).then_inc(q["gate_done"], 1)
                V.tensor_scalar(up[:, c, :], m.bank[2 * c + 1][:, :], LIMIT, -LIMIT, ALU.min, ALU.max).then_inc(gu_free[c], 1)
                dve.wait_ge(gu_free[c], b + 2)
                dve.wait_ge(q["gate_done"], 2 * b + c + 1)
                V.scalar_tensor_tensor(up[:, c, :], up[:, c, :], 1.0, gate[:, c, :], ALU.add, ALU.mult).then_inc(q["prod_done"], 1)

            def activate(b, c):
                dve.wait_ge(q["prod_done"], 2 * b + c + 1)
                dve.wait_ge(q["sig_done"], 2 * b + c + 1)
                V.tensor_mul(up[:, c, :], up[:, c, :], sig[:, c, :]).then_inc(q["act_done"], 1)

            def first(b):
                xt_half(b, 0)
                xt_half(b, 1)
                split_lo(b, 0, 1, 2)

            def body(b, further, ahead):
                split_lo(b, 4, 5, 6)
                clamp(b, 0)
                activate(b, 0)
                split_lo(b, 8, 9)
                act_half(b, 0)
                clamp(b, 1)
                activate(b, 1)
                split_lo(b, 10)
                act_half(b, 1)
                if ahead:
                    split_lo(b + 1, 0)
                    xt_half(b + 1, 0)
                    split_lo(b + 1, 1)
                    xt_half(b + 1, 1)
                    split_lo(b + 1, 2)

            for f in gu_free:
                dve.sem_inc(f, 1)
            dve.sem_inc(q["lo_done"], VEC_CHUNKS)
            all_blocks(dve, first, body)

        @block.tensor
        def _(pe):
            T = nc.tensor

            def xt_half(b, i):
                if i == 0:
                    pe.wait_ge(q["xg_in"], 16 * (b + 1))
                for k in range(4 * i, 4 * i + 4):
                    last = T.transpose(m.bank[6 + i][:, (k % 4) * P:(k % 4 + 1) * P], xg[:, k * P:(k + 1) * P], m.ident[:, :])
                last.then_inc(q["xt_psum"], 1)

            def act_half(b, c):
                pe.wait_ge(q["act_done"], 2 * b + c + 1)
                for k in range(4):
                    last = T.transpose(m.bank[6 + c][:, k * P:(k + 1) * P], up[:, c, k * P:(k + 1) * P], m.ident[:, :])
                last.then_inc(q["actt_psum"], 1)

            def products(b, i, x_hi, x_lo, banks, ends):
                if i % 4 == 3:
                    pe.wait_ge(q["pool_lo_done"], POOL_CHUNKS * (b + 1) + i // 4 + 1)
                else:
                    pe.wait_ge(q["lo_done"], VEC_CHUNKS * (b + 1) + nth_vec(i))
                hi, lo = (v[:, i % SPLIT_RING, :].rearrange("p (k g n) -> p k g n", k=2, g=2) for v in (w_hi, w_lo))
                for k in range(2):
                    kk = 2 * (i % 4) + k
                    for x, w in ((x_hi, lo), (x_hi, hi), (x_lo, hi)):
                        for g in range(2):
                            last = T.matmul(banks[g][:, :], x[:, kk, :], w[:, k, g, :], start=False,
                                            stop=(ends and k == 1 and x is x_lo))
                last.then_inc(q["chunk_used"], 1)

            def first(b):
                xt_half(b, 0)
                xt_half(b, 1)

            def body(b, further, ahead):
                pe.wait_ge(q["gu_bias_in"], 16 * (b + 1))
                pe.wait_ge(q["xt_lo_done"], 2 * b + 2)
                for c in range(2):
                    pe.wait_ge(gu_free[c], b + 1)
                    banks = m.bank[2 * c:2 * c + 2]
                    for g in range(2):
                        last = T.matmul(banks[g][:, :], ones3, gu_bias[:, g * D + c * 512:g * D + (c + 1) * 512],
                                        start=True, stop=False)
                    if c == 1:
                        last.then_inc(q["gu_bias_free"], 1)
                    for i in range(4 * c, 4 * c + 4):
                        products(b, i, xt_hi, xt_lo, banks, i % 4 == 3)
                        if i == 6:
                            act_half(b, 0)
                pe.wait_ge(q["down_bias_in"], 16 * (b + 1))
                for n in range(2):
                    last = T.matmul(m.bank[4 + n][:, :], ones3, down_bias[:, n * 512:(n + 1) * 512],
                                    start=True, stop=False)
                last.then_inc(q["down_bias_free"], 1)
                pe.wait_ge(q["actt_lo_done"], 2 * b + 1)
                for i in range(8, 12):
                    if i == 9:
                        act_half(b, 1)
                    if i == 10:
                        if ahead:
                            xt_half(b + 1, 0)
                        pe.wait_ge(q["actt_lo_done"], 2 * b + 2)
                    products(b, i, act_hi, act_lo, m.bank[4:6], i == 11)
                    if i == 10 and ahead:
                        xt_half(b + 1, 1)

            pe.wait_ge(q["ones_set"], 3)
            for s in (q["gu_bias_free"], q["down_bias_free"]):
                pe.sem_inc(s, 1)
            pe.sem_inc(q["chunk_used"], CHUNKS)
            pe.sem_inc(q["xt_psum"], 2)
            all_blocks(pe, first, body)


def combine(nc, io, m):
    with ExitStack() as ctx:
        sem = lambda n: m.sem("co_" + n)
        a = Arena(ctx.enter_context(nc.sbuf_tensor("co_buffers", [P, (NT + 13) * D], F32)))
        x2 = a.take(NT + 1, D)
        row_p = a.take(D)
        row_s = a.take(D, rows=NB)
        acc = a.take(2, D)
        ring = a.take(8, D)
        row_in, x2_in, scaled, added, gated, total, out = (sem(n) for n in ("row_in", "x2_in", "scaled", "added", "gated",
                                                                            "total", "out"))
        got = m.got
        block = ctx.enter_context(nc.Block())

        @block.sync
        def _(sp):
            row = m.mod_dram[NB:NB + 1, 5 * D:6 * D]
            sp.dma_start(row_p, row.broadcast_to([P, D])).then_inc(row_in, 16)
            sp.dma_start(row_s, m.mod_dram[0:NB, 5 * D:6 * D]).then_inc(row_in, 16)
            sp.wait_ge(added, 1)
            for t in range(NT + 1):
                r = rows_of(t)
                sp.dma_start(x2[0:r, t, :], m.x2_dram[t * P:t * P + r, :]).then_inc(x2_in, 16)
            for t in range(NT + 1):
                r = rows_of(t)
                sp.wait_ge(total, t + 1)
                dst = io["y_prompt"][0, t * P:(t + 1) * P, :] if t < NT else io["y_sample"][:, 0, :]
                sp.dma_start(dst, x2[0:r, t, :]).then_inc(out, 16)
            sp.wait_ge(out, 16 * (NT + 1))

        @block.gpsimd
        def _(pool):
            def add_x2(t):
                r = rows_of(t)
                if t == 0:
                    pool.wait_ge(x2_in, 16 * (NT + 1))
                pool.wait_ge(gated, t + 1)
                nc.gpsimd.tensor_tensor(x2[0:r, t, :], x2[0:r, t, :], acc[0:r, t % 2, :], ALU.add).then_inc(total, 1)

            for i in range((NT + 1) * TOPK):
                r = rows_of(i // TOPK)
                before, c = (i - 8) // TOPK, (i - 8) % TOPK
                if i >= 8 and c == 0:
                    pool.wait_ge(scaled, before + 1)
                elif i >= 8:
                    pool.wait_ge(added, (TOPK - 1) * before + c)
                nc.gpsimd.indirect_dma_start(out=ring[0:r, i % 8, :], out_offset=None, in_=m.y_dram,
                                             in_offset=bass.IndirectOffsetOnAxis(ap=m.slots[0:r, i:i + 1], axis=0))\
                    .then_inc(got[i % 8], 16)
                if i >= 8 and c == TOPK - 1:
                    add_x2(before)
            add_x2(NT - 1)
            add_x2(NT)

        @block.scalar
        def _(act):
            for t in range(NT + 1):
                r = rows_of(t)
                i = t * TOPK
                act.wait_ge(got[i % 8], 16 * (i // 8 + 1))
                if t >= 2:
                    act.wait_ge(total, t - 1)
                nc.scalar.activation(acc[0:r, t % 2, :], ring[0:r, i % 8, :], ACT.Copy, scale=m.weights[0:r, i:i + 1])\
                    .then_inc(scaled, 1)

        @block.vector
        def _(dve):
            for t in range(NT + 1):
                r = rows_of(t)
                sum_ = acc[0:r, t % 2, :]
                dve.wait_ge(scaled, t + 1)
                for c in range(1, TOPK):
                    i = t * TOPK + c
                    dve.wait_ge(got[i % 8], 16 * (i // 8 + 1))
                    if c > 1:
                        dve.wait_ge(added, (TOPK - 1) * t + c - 1)
                    nc.vector.scalar_tensor_tensor(sum_, ring[0:r, i % 8, :], m.weights[0:r, i:i + 1], sum_, ALU.mult, ALU.add)\
                        .then_inc(added, 1)
                dve.wait_ge(added, (TOPK - 1) * (t + 1))
                if t == 0:
                    dve.wait_ge(row_in, 32)
                nc.vector.tensor_mul(sum_, sum_, (row_p if t < NT else row_s)[0:r, :]).then_inc(gated, 1)


def program(nc, io, upto=99):
    with ExitStack() as ctx:
        sb = lambda n, s, dt=F32: ctx.enter_context(nc.sbuf_tensor(n, s, dt))
        m = Memory()
        m.ident = sb("identity", [P, P])
        small = sb("small", [P, 1130])
        m.small = Arena(small)
        m.bank = [ctx.enter_context(nc.psum_tensor(f"bank{i}", [P, 512], F32)) for i in range(8)]
        m.mod_dram = nc.dram_tensor("mod_rows", [NB + 1, 6 * D], F32).ap()
        m.tab_dram = nc.dram_tensor("slot_tokens", [(BLOCKS + 1) * BLK, 1], F32).ap()
        m.bias_dram = nc.dram_tensor("bias_parts", [EXPERTS, GUP, 3 * D], BF16).ap()
        m.y_dram = nc.dram_tensor("expert_rows", [BLOCKS * BLK, D], F32).ap()
        m.row_stats = sb("row_stats", [P, 2 * (NT + 1)])
        m.slots = sb("slots", [P, (NT + 1) * TOPK], I32)
        m.weights = sb("weights", [P, (NT + 1) * TOPK])
        m.gather_idx = sb("gather_idx", [P, BLOCKS + 1], I32)
        m.more_expert = sb("more_expert", [P, MORE + 1], I32)
        m.sx_dram = nc.dram_tensor("sample_rows", [6, NB, AW], F32).ap()
        m.sy_dram = nc.dram_tensor("sample_y", [NB, AW], F32).ap()
        m.levels = sb("level_masks", [P, 2 * LEVELS * P], mybir.dt.uint8)
        m.h2_dram = nc.dram_tensor("h2_rows", [TOK, D], F32).ap()
        m.x2_dram = nc.dram_tensor("x2_rows", [TOK, D], F32).ap()
        m.wring = sb("weight_ring", [P, NSLOT * SLOT])
        before_experts = ctx.enter_context(ExitStack())
        m.arena = before_experts.enter_context(nc.sbuf_tensor("arena", [P, ARENA], F32))
        a = Arena(m.arena)
        m.ht = a.take(KT, TOK)
        m.ct = m.ht
        m.pp_at = a.at
        m.pp = a.take(RF, 1 + TOK)
        m.v_new = a.take(AW)
        m.rwkv_at = a.at
        m.qt = a.take(4, SEQ)
        m.kt = a.take(4, SEQ)
        m.v_tok = a.take(NT, AW)
        m.scratch_at = a.at
        m.h = a.take(NT + 1, D)
        m.x2_at = m.pp_at
        m.x2 = m.arena[:, m.x2_at:m.x2_at + (NT + 1) * D].rearrange("p (t n) -> p t n", t=NT + 1)
        stages = [("ada", modulation), ("proj", projection), ("attn", attention), ("rwkv", rwkv), ("route", mix_and_route),
                  ("experts", experts), ("combine", combine)]
        m.scattered, m.xg_in = nc.alloc_semaphore("scattered"), nc.alloc_semaphore("xg_in")
        m.piece_in = [nc.alloc_semaphore(f"piece_in{j}") for j in range(NSLOT)]
        m.x_in = [nc.alloc_semaphore(f"x_in{t}") for t in range(NT + 1)]
        m.win_in = [nc.alloc_semaphore(f"win_in{j}") for j in range(NSLOT + 1)]
        m.got = [nc.alloc_semaphore(f"got{i}") for i in range(8)]
        in_use = []

        def sem(name):
            in_use.append(nc.alloc_semaphore(f"{m.stage}_{name}"))
            return in_use[-1]

        m.sem = sem
        for name, f in stages[:upto]:
            m.small.at = 0
            m.stage = name
            if name == "experts":
                before_experts.close()
            f(nc, io, m)
            nc.clear_and_free_semaphores(in_use)
            nc.all_engine_barrier()
            in_use.clear()
def more_constants():
    def times(dist):
        c = sum(((dist >= 0) & (dist <= w) & (dist % d == 0)).astype(np.float64) for w, d in PATTERNS)
        return np.where(c > 0, 8.0 * np.log(np.maximum(c, 1.0)), -1.0e30).astype(np.float32)

    q, k = np.arange(P)[:, None], np.arange(SEQ)[None, :] - (SEQ - P)
    sample = np.zeros((P, 4, NH), np.float32)
    sample[:, 3, :] = -1.0e30
    sample[0, 3, :] = times(np.array(0))
    head_mask = (np.arange(AW)[None, :] // HD == np.arange(NH)[:, None]).astype(np.float32)
    i, j = np.arange(P)[:, None], np.arange(P)[None, :]
    same = i // CHUNK == j // CHUNK
    tri = np.stack([same & (j > i), same & (j >= i)], 1).astype(np.float32)
    low = [(i // (2 * b) == j // (2 * b)) & (i // b % 2 == 1) & (j // b % 2 == 0) for b in (1, 2, 4, 8, 16, 32)]
    levels = np.concatenate(low + [x.T for x in low], 1).astype(np.float32)
    ones_blk = (i // HD == j // HD).astype(np.float32)
    restart = np.broadcast_to((np.arange(SEQ) % CHUNK != 0).astype(np.float32), (P, SEQ)).copy()
    route = np.concatenate([np.broadcast_to(np.arange(EXPERTS), (P, EXPERTS)), np.broadcast_to(np.arange(MORE), (P, MORE)),
                            np.arange(P)[:, None] + P * np.arange(NT + 1)[None, :]], 1).astype(np.float32)
    rank_tri = (i < j).astype(np.float32)
    head_pick = (2 * np.arange(PAIRS)[None, :, None] + i[:, :, None] // HD == np.arange(NH)[None, None, :])
    return {"head_pick": head_pick.astype(np.float32).reshape(P, PAIRS * NH), "route": route, "rank_tri": rank_tri, "tri": tri, "levels": levels, "ones_blk": ones_blk, "restart": restart, "attn_bias": times(q - k), "sample_bias": sample.reshape(P, 4 * NH), "head_mask": head_mask}


INPUTS = ["x_prompt", "x_sample", "cache_k", "cache_v", "state_wkv", "state_shift", "c_prompt", "c_sample",
          "w_ada", "b_ada", "norm1_g", "norm2_g", "w_in", "q_norm_g", "k_norm_g",
          "rwkv_mu", "rwkv_w0", "rwkv_w2", "rwkv_a0", "rwkv_a2", "rwkv_g2",
          "rwkv_k_k", "rwkv_k_a", "rwkv_r_k", "rwkv_ln_w", "rwkv_ln_b", "w_out",
          "router_w", "router_b", "moe_w_gu", "moe_b_gu", "moe_w_down", "moe_b_down"]
OUTPUTS = [("y_prompt", (1, SEQ, D)), ("y_sample", (NB, 1, D)),
           ("k_prompt", (1, 1, SEQ, NH, HD)), ("v_prompt", (1, 1, SEQ, NH, HD)),
           ("wkv_prompt", (1, 1, NH, HD, HD)), ("shift_prompt", (1, 1, RC)),
           ("k_new", (1, NB, 1, NH, HD)), ("v_new", (1, NB, 1, NH, HD)),
           ("wkv_sample", (1, NB, NH, HD, HD)), ("shift_sample", (1, NB, RC))]


def constants():
    pos = np.minimum(np.arange((NT + 1) * P), SEQ).astype(np.float32)
    pos[SEQ:] = PAST
    inv = (1.0 / (np.float32(10000.0) ** (np.arange(0, HD, 2, dtype=np.float32) / HD))).astype(np.float32)
    ang = (pos[:, None] * inv[None, :]).astype(np.float32)
    tiles = lambda t: np.ascontiguousarray(t.reshape(NT + 1, P, -1).transpose(1, 0, 2)).astype(np.float32)
    out = {"ident": np.eye(P, dtype=np.float32), "cos": tiles(np.cos(ang)), "sin": tiles(np.sin(ang))}
    out.update(more_constants())
    return out


def kernel(**inputs):
    from concourse import bacc
    from concourse.bass_utils import run_bass_kernel_spmd

    nc = bacc.Bacc("TRN2", target_bir_lowering=False, num_devices=1)
    arrays = {k: np.ascontiguousarray(inputs[k]) for k in INPUTS}
    arrays.update(constants())
    io = {k: nc.dram_tensor(f"in_{k}", a.shape, mybir.dt.from_np(a.dtype), kind="ExternalInput").ap()
          for k, a in arrays.items()}
    io.update({k: nc.dram_tensor(f"out_{k}", s, F32, kind="ExternalOutput").ap() for k, s in OUTPUTS})
    program(nc, io)
    r = run_bass_kernel_spmd(nc, [{f"in_{k}": a for k, a in arrays.items()}], core_ids=[0])
    return tuple(r.results[0][f"out_{k}"] for k, _ in OUTPUTS)
```
